# Optimizing a Trainium2 kernel written in Bass

```python
import math
import jax, jax.numpy as jnp
from jax import lax
import numpy as np

D_MODEL = 1024
BATCH = 1
SEQ = 256
DEPTH = 2

GLA_HEADS = 4
GLA_DK = 64
GLA_DV = 128
GLA_RANK = 16
GLA_TAU = 16.0
GLA_CHUNK = 64
DIFF_HEADS = 4
DIFF_DH = 64
DIFF_DV = 2 * DIFF_DH
Q_BLOCK = 128
A_QK = GLA_HEADS * GLA_DK
A_V = GLA_HEADS * GLA_DV
B_QK = DIFF_HEADS * 2 * DIFF_DH
B_V = DIFF_HEADS * DIFF_DV
EVEN_IN = 2 * A_QK + 2 * A_V + GLA_RANK + 2 * B_QK + B_V
EVEN_MIX = A_V + B_V
DIL_PATTERNS = ((128, 1), (512, 4), (2048, 16))
DIL_GROUPS = 3
DIL_HEADS = 4
DIL_DH = 128
ODD_IN = DIL_GROUPS * 3 * DIL_HEADS * DIL_DH
ODD_MIX = DIL_HEADS * DIL_DH
D_FF = 2816
CONV_W = 3
EPS = 1e-6
N_EVEN = (DEPTH + 1) // 2
N_ODD = DEPTH // 2


def rmsnorm(x, g):
    xf = x.astype(jnp.float32)
    y = xf * lax.rsqrt(jnp.mean(xf * xf, axis=-1, keepdims=True) + EPS)
    return (y * g.astype(jnp.float32)).astype(x.dtype)

def gla(q, k, v, log_a):
    B, S, H, dk = q.shape
    dv = v.shape[-1]
    C = GLA_CHUNK
    N = S // C
    f32 = jnp.float32

    def chunk(t):
        return t.astype(f32).reshape(B, N, C, H, t.shape[-1]).transpose(0, 3, 1, 2, 4)

    qc, kc, vc, lc = chunk(q * (dk ** -0.5)), chunk(k), chunk(v), chunk(log_a)
    b = jnp.cumsum(lc, axis=3)
    b_last = b[:, :, :, -1:, :]
    q_d = qc * jnp.exp(b)
    k_d = kc * jnp.exp(-b)
    causal = jnp.tril(jnp.ones((C, C), dtype=bool))
    att = jnp.where(causal, jnp.einsum('bhnik,bhnjk->bhnij', q_d, k_d), 0.0)
    o_intra = jnp.einsum('bhnij,bhnjv->bhniv', att, vc)
    kv = jnp.einsum('bhnjk,bhnjv->bhnkv', kc * jnp.exp(b_last - b), vc)
    decay = jnp.exp(b_last[:, :, :, 0, :])

    def step(state, inp):
        kv_n, dec_n = inp
        return dec_n[..., None] * state + kv_n, state

    s0 = jnp.zeros((B, H, dk, dv), f32)
    _, states = lax.scan(step, s0, (jnp.moveaxis(kv, 2, 0), jnp.moveaxis(decay, 2, 0)))
    states = jnp.moveaxis(states, 0, 2)
    o = o_intra + jnp.einsum('bhnik,bhnkv->bhniv', q_d, states)
    return o.transpose(0, 2, 3, 1, 4).reshape(B, S, H, dv).astype(v.dtype)

def diff_attention(q, k, v, lam):
    B, S, H, _, dh = q.shape
    dv = v.shape[-1]
    nb = S // Q_BLOCK
    qb = (q * (dh ** -0.5)).reshape(B, nb, Q_BLOCK, H, 2, dh).transpose(1, 0, 3, 4, 2, 5)
    kt = k.transpose(0, 2, 3, 1, 4)
    vt = v.transpose(0, 2, 1, 3)
    kpos = jnp.arange(S)

    def block(args):
        qblk, n = args
        s = jnp.einsum('bhcqd,bhckd->bhcqk', qblk, kt).astype(jnp.float32)
        qpos = n * Q_BLOCK + jnp.arange(Q_BLOCK)
        s = jnp.where(kpos[None, :] <= qpos[:, None], s, -jnp.inf)
        p = jax.nn.softmax(s, axis=-1)
        w = p[:, :, 0] - lam * p[:, :, 1]
        return jnp.einsum('bhqk,bhkv->bhqv', w.astype(vt.dtype), vt)

    o = lax.map(block, (qb, jnp.arange(nb)))
    return o.transpose(1, 0, 3, 2, 4).reshape(B, S, H, dv)

def dilated_branch(q, k, v, dilation, wc):
    B, S, H, dh = q.shape
    L = S // dilation
    nb = -(-L // wc)
    Lp = nb * wc

    def to_class(t):
        t = t.reshape(B, L, dilation, H, dh).transpose(0, 2, 3, 1, 4)
        t = jnp.pad(t, ((0, 0), (0, 0), (0, 0), (0, Lp - L), (0, 0)))
        return t.reshape(B, dilation, H, nb, wc, dh)

    def band(t):
        prev = jnp.pad(t, ((0, 0),) * 3 + ((1, 0), (0, 0), (0, 0)))[:, :, :, :-1]
        return jnp.concatenate([prev, t], axis=-2)

    qc = to_class(q)
    kb = band(to_class(k))
    vb = band(to_class(v))
    s = jnp.einsum('brhnqd,brhnkd->brhnqk', qc, kb).astype(jnp.float32) * (dh ** -0.5)
    i = jnp.arange(wc)[:, None]
    j = jnp.arange(2 * wc)[None, :]
    dist = i + wc - j
    blk = jnp.arange(nb)[:, None, None]
    valid = (dist >= 0) & (dist <= wc) & ((blk > 0) | (j >= wc))
    s = jnp.where(valid, s, -jnp.inf)
    lse = jax.nn.logsumexp(s, axis=-1)
    p = jnp.exp(s - lse[..., None])
    o = jnp.einsum('brhnqk,brhnkd->brhnqd', p.astype(vb.dtype), vb)
    o = o.reshape(B, dilation, H, Lp, dh)[:, :, :, :L].transpose(0, 3, 1, 2, 4).reshape(B, S, H, dh)
    lse = lse.reshape(B, dilation, H, Lp)[..., :L].transpose(0, 3, 1, 2).reshape(B, S, H)
    return o, lse

def even_mixer(h, w_in, w_a2, b_a, gla_gain, dq_gain, dk_gain, lq1, lk1, lq2, lk2, diff_gain, w_out, lambda_init):
    B, S, _ = h.shape
    z = h @ w_in
    sizes = [A_QK, A_QK, A_V, A_V, GLA_RANK, B_QK, B_QK]
    aq, ak, av, ag, ar, bq, bk, bv = jnp.split(z, [int(c) for c in np.cumsum(sizes)], axis=-1)
    log_a = jax.nn.log_sigmoid((ar @ w_a2 + b_a).astype(jnp.float32)) / GLA_TAU
    oa = gla(aq.reshape(B, S, GLA_HEADS, GLA_DK), ak.reshape(B, S, GLA_HEADS, GLA_DK),
             av.reshape(B, S, GLA_HEADS, GLA_DV), log_a.reshape(B, S, GLA_HEADS, GLA_DK))
    oa = rmsnorm(oa, gla_gain) * jax.nn.silu(ag.reshape(B, S, GLA_HEADS, GLA_DV))
    bq = rmsnorm(bq.reshape(B, S, DIFF_HEADS, 2, DIFF_DH), dq_gain)
    bk = rmsnorm(bk.reshape(B, S, DIFF_HEADS, 2, DIFF_DH), dk_gain)
    f32 = jnp.float32
    lam = (jnp.exp(jnp.sum(lq1.astype(f32) * lk1.astype(f32)))
           - jnp.exp(jnp.sum(lq2.astype(f32) * lk2.astype(f32))) + lambda_init)
    ob = diff_attention(bq, bk, bv.reshape(B, S, DIFF_HEADS, DIFF_DV), lam)
    ob = rmsnorm(ob, diff_gain) * (1.0 - lambda_init)
    o = jnp.concatenate([oa.reshape(B, S, A_V), ob.reshape(B, S, B_V)], axis=-1)
    return o @ w_out

def odd_mixer(h, w_in, q_gain, k_gain, w_out):
    B, S, _ = h.shape
    z = (h @ w_in).reshape(B, S, DIL_GROUPS, 3, DIL_HEADS, DIL_DH)
    q = rmsnorm(z[:, :, :, 0], q_gain)
    k = rmsnorm(z[:, :, :, 1], k_gain)
    v = z[:, :, :, 2]
    outs, lses = [], []
    for g, (window, dilation) in enumerate(DIL_PATTERNS):
        o_g, lse_g = dilated_branch(q[:, :, g], k[:, :, g], v[:, :, g], dilation, window // dilation)
        outs.append(o_g)
        lses.append(lse_g)
    wts = jax.nn.softmax(jnp.stack(lses, axis=0), axis=0)
    o = jnp.sum(wts[..., None].astype(v.dtype) * jnp.stack(outs, axis=0), axis=0)
    return o.reshape(B, S, ODD_MIX) @ w_out

def conv_ffn(h, w_up, conv_w, conv_b, w_down):
    u = h @ w_up
    u = lax.conv_general_dilated(u, conv_w, window_strides=(1,), padding=[(CONV_W - 1, 0)],
                                 dimension_numbers=('NWC', 'WIO', 'NWC'),
                                 feature_group_count=2 * D_FF) + conv_b
    gate, val = jnp.split(u, 2, axis=-1)
    return (jax.nn.silu(gate) * val) @ w_down

def first_inputs(seed: int = 0) -> dict:
    key = jax.random.key(seed)
    ks = iter(jax.random.split(key, 32))
    nrm = lambda shape, scale: jax.random.normal(next(ks), shape, jnp.float32) * scale
    gain = lambda shape: 1.0 + nrm(shape, 0.02)
    return {
        "x": nrm((BATCH, SEQ, D_MODEL), 1.0),
        "norm_mix": gain((DEPTH, D_MODEL)),
        "norm_ffn": gain((DEPTH, D_MODEL)),
        "ev_w_in": nrm((N_EVEN, D_MODEL, EVEN_IN), D_MODEL ** -0.5),
        "ev_w_a2": nrm((N_EVEN, GLA_RANK, A_QK), GLA_RANK ** -0.5),
        "ev_b_a": nrm((N_EVEN, A_QK), 0.1),
        "ev_gla_gain": gain((N_EVEN, GLA_DV)),
        "ev_dq_gain": gain((N_EVEN, DIFF_DH)),
        "ev_dk_gain": gain((N_EVEN, DIFF_DH)),
        "ev_lq1": nrm((N_EVEN, DIFF_DH), 0.1),
        "ev_lk1": nrm((N_EVEN, DIFF_DH), 0.1),
        "ev_lq2": nrm((N_EVEN, DIFF_DH), 0.1),
        "ev_lk2": nrm((N_EVEN, DIFF_DH), 0.1),
        "ev_diff_gain": gain((N_EVEN, DIFF_DV)),
        "ev_w_out": nrm((N_EVEN, EVEN_MIX, D_MODEL), EVEN_MIX ** -0.5),
        "od_w_in": nrm((N_ODD, D_MODEL, ODD_IN), D_MODEL ** -0.5),
        "od_q_gain": gain((N_ODD, DIL_DH)),
        "od_k_gain": gain((N_ODD, DIL_DH)),
        "od_w_out": nrm((N_ODD, ODD_MIX, D_MODEL), ODD_MIX ** -0.5),
        "ffn_w_up": nrm((DEPTH, D_MODEL, 2 * D_FF), D_MODEL ** -0.5),
        "ffn_conv_w": nrm((DEPTH, CONV_W, 1, 2 * D_FF), CONV_W ** -0.5),
        "ffn_conv_b": nrm((DEPTH, 2 * D_FF), 0.01),
        "ffn_w_down": nrm((DEPTH, D_FF, D_MODEL), D_FF ** -0.5),
    }

def first_block(x, norm_mix, norm_ffn, ev_w_in, ev_w_a2, ev_b_a, ev_gla_gain, ev_dq_gain, ev_dk_gain,
              ev_lq1, ev_lk1, ev_lq2, ev_lk2, ev_diff_gain, ev_w_out, od_w_in, od_q_gain, od_k_gain,
              od_w_out, ffn_w_up, ffn_conv_w, ffn_conv_b, ffn_w_down):
    for i in range(DEPTH):
        h = rmsnorm(x, norm_mix[i])
        if i % 2 == 0:
            e = i // 2
            lambda_init = 0.8 - 0.6 * math.exp(-0.3 * i)
            x = x + even_mixer(h, ev_w_in[e], ev_w_a2[e], ev_b_a[e], ev_gla_gain[e], ev_dq_gain[e],
                               ev_dk_gain[e], ev_lq1[e], ev_lk1[e], ev_lq2[e], ev_lk2[e],
                               ev_diff_gain[e], ev_w_out[e], lambda_init)
        else:
            o = i // 2
            x = x + odd_mixer(h, od_w_in[o], od_q_gain[o], od_k_gain[o], od_w_out[o])
        x = x + conv_ffn(rmsnorm(x, norm_ffn[i]), ffn_w_up[i], ffn_conv_w[i], ffn_conv_b[i], ffn_w_down[i])
    return x


POOL_WINDOWS = (2, 4, 8, 16)
N_POOL_GROUPS = len(POOL_WINDOWS)
POOL_GROUP_DIM = D_MODEL // 8
POOL_DIM = N_POOL_GROUPS * POOL_GROUP_DIM

N_HEADS = D_MODEL // 128
QK_NOPE = 64
QK_ROPE = 32
V_DIM = 64
Q_LORA = 384
KV_LORA = 256
ROPE_THETA = 10000.0
ATTN_DIM = N_HEADS * V_DIM

D_FF_2 = 4 * D_MODEL

N_MOD = 6

IN_SPLITS = (POOL_DIM, Q_LORA, KV_LORA, QK_ROPE, D_MODEL, D_MODEL)
D_IN = sum(IN_SPLITS)


def rms_norm(x, g):
    xf = x.astype(jnp.float32)
    y = xf * lax.rsqrt(jnp.mean(xf * xf, axis=-1, keepdims=True) + EPS)
    return y.astype(x.dtype) * g

def apply_rope(x, cos, sin):
    half = x.shape[-1] // 2
    x1, x2 = x[..., :half], x[..., half:]
    return jnp.concatenate([x1 * cos - x2 * sin, x2 * cos + x1 * sin], axis=-1)

def pool_mixer(u, w_pool, pool_scale):
    B, S, _ = u.shape
    t = jnp.arange(S)
    outs = []
    for g, w in enumerate(POOL_WINDOWS):
        ug = u[..., g * POOL_GROUP_DIM:(g + 1) * POOL_GROUP_DIM].astype(jnp.float32)
        cs = jnp.cumsum(ug, axis=1)
        lag = jnp.pad(cs, ((0, 0), (w, 0), (0, 0)))[:, :S]
        cnt = jnp.minimum(t + 1, w).astype(jnp.float32)[None, :, None]
        outs.append(((cs - lag) / cnt - ug).astype(u.dtype))
    p = jnp.stack(outs, axis=2)
    y = jnp.einsum('bsgc,gcd->bsgd', p, w_pool).reshape(B, S, POOL_DIM)
    return y * pool_scale

def mla(c_q_raw, c_kv_raw, k_rope_raw, q_norm_g, w_uq, kv_norm_g, w_uk, w_uv, cos, sin):
    B, S, _ = c_q_raw.shape
    c_q = rms_norm(c_q_raw, q_norm_g)
    q = jnp.einsum('bsr,rhd->bshd', c_q, w_uq)
    q_nope = q[..., :QK_NOPE]
    q_rope = apply_rope(q[..., QK_NOPE:], cos[:, :, None, :], sin[:, :, None, :])
    c_kv = rms_norm(c_kv_raw, kv_norm_g)
    k_nope = jnp.einsum('bsr,rhd->bhsd', c_kv, w_uk)
    v = jnp.einsum('bsr,rhd->bhsd', c_kv, w_uv)
    k_rope = apply_rope(k_rope_raw, cos, sin)

    nb = S // Q_BLOCK
    def to_blocks(a):
        d = a.shape[-1]
        return a.reshape(B, nb, Q_BLOCK, N_HEADS, d).transpose(1, 0, 3, 2, 4)
    qn_b = to_blocks(q_nope)
    qr_b = to_blocks(q_rope)
    starts = jnp.arange(nb, dtype=jnp.int32) * Q_BLOCK
    key_pos = jnp.arange(S, dtype=jnp.int32)
    scale = 1.0 / math.sqrt(QK_NOPE + QK_ROPE)
    neg = jnp.finfo(jnp.float32).min

    def attend(args):
        qn, qr, start = args
        s = (jnp.einsum('bhqd,bhkd->bhqk', qn, k_nope)
             + jnp.einsum('bhqd,bkd->bhqk', qr, k_rope)).astype(jnp.float32) * scale
        q_pos = start + jnp.arange(Q_BLOCK, dtype=jnp.int32)
        mask = q_pos[:, None] >= key_pos[None, :]
        p = jax.nn.softmax(jnp.where(mask, s, neg), axis=-1)
        return jnp.einsum('bhqk,bhkd->bhqd', p.astype(v.dtype), v)

    o = lax.map(attend, (qn_b, qr_b, starts))
    return o.transpose(1, 0, 3, 2, 4).reshape(B, S, ATTN_DIM)

def second_inputs(seed: int = 0) -> dict:
    key = jax.random.key(seed)
    ks = jax.random.split(key, 24)
    f32 = jnp.float32

    def dense(k, shape, fan_in, mult=1.0):
        return jax.random.normal(k, shape, f32) * (mult * fan_in ** -0.5)

    def gain(k, shape):
        return 1.0 + 0.02 * jax.random.normal(k, shape, f32)

    x = jax.random.normal(ks[0], (BATCH, SEQ, D_MODEL), f32)
    c = jax.random.normal(ks[1], (BATCH, D_MODEL), f32)
    offsets = jax.random.randint(ks[2], (BATCH, 1), 0, 1024, dtype=jnp.int32)
    positions = offsets + jnp.arange(SEQ, dtype=jnp.int32)[None, :]
    return {
        "x": x,
        "c": c,
        "positions": positions,
        "ln1_g": gain(ks[3], (DEPTH, D_MODEL)),
        "ln2_g": gain(ks[4], (DEPTH, D_MODEL)),
        "w_ada": dense(ks[5], (DEPTH, D_MODEL, N_MOD * D_MODEL), D_MODEL, 0.5),
        "b_ada": 0.01 * jax.random.normal(ks[6], (DEPTH, N_MOD * D_MODEL), f32),
        "w_in": dense(ks[7], (DEPTH, D_MODEL, D_IN), D_MODEL),
        "q_norm_g": gain(ks[8], (DEPTH, Q_LORA)),
        "w_uq": dense(ks[9], (DEPTH, Q_LORA, N_HEADS, QK_NOPE + QK_ROPE), Q_LORA),
        "kv_norm_g": gain(ks[10], (DEPTH, KV_LORA)),
        "w_uk": dense(ks[11], (DEPTH, KV_LORA, N_HEADS, QK_NOPE), KV_LORA),
        "w_uv": dense(ks[12], (DEPTH, KV_LORA, N_HEADS, V_DIM), KV_LORA),
        "w_pool": dense(ks[13], (DEPTH, N_POOL_GROUPS, POOL_GROUP_DIM, POOL_GROUP_DIM), POOL_GROUP_DIM),
        "pool_scale": gain(ks[14], (DEPTH, POOL_DIM)),
        "p_pool": dense(ks[15], (DEPTH, POOL_DIM, D_MODEL), POOL_DIM),
        "p_attn": dense(ks[16], (DEPTH, ATTN_DIM, D_MODEL), ATTN_DIM),
        "w_out": dense(ks[17], (DEPTH, D_MODEL, D_MODEL), D_MODEL),
        "w_ff1": dense(ks[18], (DEPTH, D_MODEL, D_FF_2), D_MODEL),
        "w_ff2": dense(ks[19], (DEPTH, D_FF_2, D_MODEL), D_FF_2),
        "final_g": gain(ks[20], (D_MODEL,)),
    }

def second_block(x, c, positions, ln1_g, ln2_g, w_ada, b_ada, w_in, q_norm_g, w_uq,
              kv_norm_g, w_uk, w_uv, w_pool, pool_scale, p_pool, p_attn, w_out,
              w_ff1, w_ff2, final_g):
    inv_freq = ROPE_THETA ** (-jnp.arange(0, QK_ROPE, 2, dtype=jnp.float32) / QK_ROPE)
    ang = positions.astype(jnp.float32)[..., None] * inv_freq
    cos = jnp.cos(ang).astype(x.dtype)
    sin = jnp.sin(ang).astype(x.dtype)
    c_act = jax.nn.silu(c)
    cuts = np.cumsum(IN_SPLITS)[:-1].tolist()

    for l in range(DEPTH):
        mod = c_act @ w_ada[l] + b_ada[l]
        sh1, sc1, g1, sh2, sc2, g2 = [m[:, None, :] for m in jnp.split(mod, N_MOD, axis=-1)]

        h = rms_norm(x, ln1_g[l]) * (1.0 + sc1) + sh1
        z = h @ w_in[l]
        u_pool, c_q_raw, c_kv_raw, k_rope_raw, gz_a, gz_b = jnp.split(z, cuts, axis=-1)
        y_a = pool_mixer(u_pool, w_pool[l], pool_scale[l]) @ p_pool[l]
        y_b = mla(c_q_raw, c_kv_raw, k_rope_raw, q_norm_g[l], w_uq[l], kv_norm_g[l],
                  w_uk[l], w_uv[l], cos, sin) @ p_attn[l]
        merged = jax.nn.sigmoid(gz_a) * y_a + jax.nn.sigmoid(gz_b) * y_b
        x = x + g1 * (merged @ w_out[l])

        h2 = rms_norm(x, ln2_g[l]) * (1.0 + sc2) + sh2
        x = x + g2 * (jnp.square(jax.nn.relu(h2 @ w_ff1[l])) @ w_ff2[l])

    return rms_norm(x, final_g)


def setup_inputs(seed=0):
    out = dict(first_inputs(seed))
    for name, value in second_inputs(seed + 1).items():
        if name != "x":
            out[name + "_2"] = value
    return out


def reference(
    x, norm_mix, norm_ffn, ev_w_in, ev_w_a2, ev_b_a, ev_gla_gain, ev_dq_gain, ev_dk_gain,
    ev_lq1, ev_lk1, ev_lq2, ev_lk2, ev_diff_gain, ev_w_out, od_w_in, od_q_gain, od_k_gain,
    od_w_out, ffn_w_up, ffn_conv_w, ffn_conv_b, ffn_w_down, c_2, positions_2, ln1_g_2, ln2_g_2,
    w_ada_2, b_ada_2, w_in_2, q_norm_g_2, w_uq_2, kv_norm_g_2, w_uk_2, w_uv_2, w_pool_2,
    pool_scale_2, p_pool_2, p_attn_2, w_out_2, w_ff1_2, w_ff2_2, final_g_2,
):
    x = first_block(
        x, norm_mix, norm_ffn, ev_w_in, ev_w_a2, ev_b_a, ev_gla_gain, ev_dq_gain, ev_dk_gain,
        ev_lq1, ev_lk1, ev_lq2, ev_lk2, ev_diff_gain, ev_w_out, od_w_in, od_q_gain, od_k_gain,
        od_w_out, ffn_w_up, ffn_conv_w, ffn_conv_b, ffn_w_down,
    )
    return second_block(
        x, c_2, positions_2, ln1_g_2, ln2_g_2, w_ada_2, b_ada_2, w_in_2, q_norm_g_2, w_uq_2,
        kv_norm_g_2, w_uk_2, w_uv_2, w_pool_2, pool_scale_2, p_pool_2, p_attn_2, w_out_2,
        w_ff1_2, w_ff2_2, final_g_2,
    )


_drawn_inputs = setup_inputs


def setup_inputs(seed=0):
    import zlib

    import numpy as np

    out = dict(_drawn_inputs(seed))
    spreads = {}
    factors = {'norm_ffn': 3.012,
     'ev_b_a': 3.027,
     'ev_gla_gain': 6.297,
     'ev_dq_gain': 4.661,
     'ev_dk_gain': 5.014,
     'ev_lq1': 6.112,
     'ev_lk1': 8.0,
     'ev_diff_gain': 4.82,
     'od_q_gain': 8.0,
     'od_k_gain': 8.0,
     'ffn_conv_b': 6.172,
     'ln1_g_2': 8.0,
     'ln2_g_2': 6.445,
     'b_ada_2': 3.816,
     'q_norm_g_2': 8.0,
     'w_uq_2': 2.796,
     'kv_norm_g_2': 8.0,
     'w_uk_2': 3.297,
     'pool_scale_2': 8.0,
     'final_g_2': 7.891,
     'ev_lq2': 5.002,
     'ev_lk2': 8.0}
    for name, (base, spread) in spreads.items():
        noise = np.random.default_rng([zlib.crc32(name.encode()), seed]).standard_normal(out[name].shape)
        drawn = base * np.exp(spread * noise) if base else spread * noise
        out[name] = __import__('jax').numpy.asarray(drawn.astype(out[name].dtype))
    for name, factor in factors.items():
        out[name] = (out[name] * factor).astype(out[name].dtype)
    return out
```

```python
from contextlib import ExitStack

import numpy as np
import concourse.bass as bass
from concourse import mybir

P = 128
TOK = 256
D = 1024
KB = D // P
FF1, FF2 = 2816, 4096
EPS = 1e-6
F32 = mybir.dt.float32
F32R = mybir.dt.float32r
I32 = mybir.dt.int32
U32 = mybir.dt.uint32
ALU = mybir.AluOpType
ACT = mybir.ActivationFunctionType
AX = mybir.AxisListType
RAW, SPLIT, LIN = 3, 3, 3
CHUNK = 2048
NEG = -1e30
EXP_LN = "natural_log_exp_and_others"
TWO_PI_PARTS = (6.28125, 0.0019302368164062500, 0.0000050703630862)


def linear_chunks():
    c = []

    def add(name, src, rows, cols, first=True, last=True, tm=False, diag=False, op="O", banks=None):
        ncols = len(cols)
        nb = max(1, ncols // 256) if not diag else 2
        c.append(dict(name=name, src=src, rows=list(rows), cols=cols, first=first, last=last, tm=tm,
                      diag=diag, op=op, banks=banks or nb, width=ncols * (1 if diag else len(rows))))

    def cols(a, n):
        return list(range(a, a + n))

    k8 = range(8)
    o = {"aq": 0, "ak": 256, "av": 512, "ag": 1024, "ar": 1536, "bq": 1552, "bk": 2064, "bv": 2576}
    w = ("ev_w_in", 0)
    for name, base, tm in (("av0", o["av"], 1), ("av1", o["av"] + 256, 1), ("bq0", o["bq"], 0),
                           ("bk0", o["bk"], 0), ("aq", o["aq"], 0), ("ak", o["ak"], 0), ("bv0", o["bv"], 1),
                           ("bq1", o["bq"] + 256, 0), ("bk1", o["bk"] + 256, 0), ("bv1", o["bv"] + 256, 1),
                           ("ag0", o["ag"], 0), ("ag1", o["ag"] + 256, 0)):
        add(name, w, k8, cols(base, 256), tm=bool(tm))

    def out_proj(tag, src):
        for p in range(4):
            add(f"{tag}{p}", src, k8, cols(256 * p, 256))

    def conv_ffn(l):
        for j in range(11):
            add(f"up{l}g{j}", ("ffn_w_up", l), k8, cols(256 * j, 256))
            add(f"up{l}v{j}", ("ffn_w_up", l), k8, cols(FF1 + 256 * j, 256))
        for p in range(4):
            for i, r in enumerate((range(0, 8), range(8, 16), range(16, 22))):
                add(f"down{l}_{p}_{i}", ("ffn_w_down", l), r, cols(256 * p, 256), i == 0, i == 2, op="A")

    out_proj("evo", ("ev_w_out", 0))
    conv_ffn(0)
    for hp in range(2):
        for g in range(3):
            for s in range(3):
                add(f"od{hp}{g}{s}", ("od_w_in", 0), k8, cols(g * 1536 + s * 512 + hp * 256, 256), tm=s == 2)
    for p in range(4):
        add(f"odo{p}", ("od_w_out", 0), range(4), cols(256 * p, 256))
    conv_ffn(1)
    nope = [h * 96 + i for h in range(8) for i in range(64)]
    rope = [h * 96 + 64 + i for h in range(8) for i in range(32)]
    for l in range(2):
        w = ("w_in_2", l)
        add(f"cq{l}a", w, k8, cols(512, 256))
        add(f"cq{l}b", w, k8, cols(768, 128))
        add(f"ckv{l}", w, k8, cols(896, 256))
        add(f"u{l}0", w, k8, cols(0, 256))
        add(f"u{l}1", w, k8, cols(256, 256))
        add(f"uqn{l}", ("w_uq_2", l), range(3), nope, op="Q")
        add(f"uqr{l}", ("w_uq_2", l), range(3), rope, op="Q")
        add(f"uk{l}", ("w_uk_2", l), range(2), cols(0, 512), op="C")
        add(f"uv{l}", ("w_uv_2", l), range(2), cols(0, 512), tm=True, op="C")
        for p in range(4):
            add(f"gz{l}a{p}", w, k8, cols(1184 + 256 * p, 256))
        add(f"wp{l}", ("w_pool_2", l), range(4), cols(0, 512), diag=True, op="Q")
        for p in range(4):
            add(f"gz{l}b{p}", w, k8, cols(2208 + 256 * p, 256))
        for i in range(2):
            add(f"pp{l}_{i}", ("p_pool_2", l), range(4), cols(512 * i, 512), op="Q")
        for i in range(2):
            add(f"pa{l}_{i}", ("p_attn_2", l), range(4), cols(512 * i, 512), op="C")
        out_proj(f"wo{l}_", ("w_out_2", l))
        for p in range(16):
            add(f"fa{l}_{p}", ("w_ff1_2", l), k8, cols(256 * p, 256))
        for p in range(4):
            for i in range(4):
                add(f"fb{l}_{p}_{i}", ("w_ff2_2", l), range(8 * i, 8 * i + 8), cols(256 * p, 256),
                    i == 0, i == 3, op="A")
    at, bank = 0, 0
    for n, x in enumerate(c):
        x["n"], x["at"] = n, at
        at += x["width"]
        if x["first"]:
            x["bank"] = bank
            bank += x["banks"]
        else:
            x["bank"] = c[n - 1]["bank"]
    return c, at


def columns():
    where = {}
    sizes = {"consts": 0, "params": 0}

    def put(kind, name, n):
        where[name] = (kind, sizes[kind], n)
        sizes[kind] += n

    for name, n in (("ident", 128), ("ones", 128), ("ones64", 128), ("causal", 256), ("dil0", 384),
                    ("dil1", 768), ("gla_mask", 128), ("rot", 128), ("inv_freq", 1), ("cnt", 64), ("eps", 1)):
        put("consts", name, n)
    for name, n in (("norm_mix", 16), ("norm_ffn", 16), ("b_a", 2), ("gla_gain", 1), ("dq_gain", 1),
                    ("dk_gain", 1), ("diff_gain", 1), ("od_q_gain", 1), ("od_k_gain", 1), ("conv", 2 * 44 * 4),
                    ("lam", 256), ("ln1", 16), ("ln2", 16), ("b_ada", 96), ("q_norm", 6), ("kv_norm", 4),
                    ("pool_scale", 8), ("final_g", 8), ("c", 8), ("w_a2", 256), ("w_ar", 128), ("w_kr", 512)):
        put("params", name, n)
    return where, sizes


def build(nc, xT, stream, ada, consts_d, params_d, positions, out):
    CH, _ = linear_chunks()
    BY = {x["name"]: x for x in CH}
    NCH = len(CH)
    where, sizes = columns()
    ctx = ExitStack()
    with ctx:
        def sb(name, shape, dt=F32, stack=ctx):
            return stack.enter_context(nc.sbuf_tensor(name, shape, dt))

        def sem(name):
            return ctx.enter_context(nc.semaphore(name))

        consts = sb("consts", [P, sizes["consts"]])
        params = sb("params", [P, sizes["params"]])

        def col(name, a=0, n=None):
            kind, at, size = where[name]
            t = consts if kind == "consts" else params
            return t[:, at + a:at + a + (size - a if n is None else n)]

        raw = [sb(f"raw{i}", [P, CHUNK]) for i in range(RAW)]
        high = [sb(f"high{i}", [P, CHUNK], F32R) for i in range(SPLIT)]
        low = [sb(f"low{i}", [P, CHUNK], F32R) for i in range(SPLIT)]
        x = sb("x", [P, KB, TOK])
        h = sb("h", [P, KB, TOK])
        OH = sb("op_high", [P, KB, TOK], F32R)
        OL = sb("op_low", [P, KB, TOK], F32R)
        rn = sb("rn", [P, TOK])
        sq = [sb(f"sq{i}", [P, 2, TOK]) for i in range(2)]
        rb = [sb(f"rb{i}", [P, 2, TOK]) for i in range(2)]
        cosT = sb("cosT", [P, TOK])
        sinT = sb("sinT", [P, TOK])
        mod = sb("mod", [P, 2, 48])
        gmod = sb("gmod", [P, 2, 2, KB])
        cact = sb("cact", [P, KB])
        small = sb("small", [P, 64])
        neglam = small[:, 0:1]
        gain8 = small[:, 1:2]

        first = ExitStack()
        f = lambda n, s, d=F32: sb(n, s, d, first)
        posi = f("posi", [P, TOK], I32)
        ang = f("ang", [P, TOK])
        turn = f("turn", [P, TOK])
        ar = f("ar", [16, TOK])
        la = f("la", [P, 2, TOK])
        bc = f("bc", [P, 2, TOK])
        eb = f("eb", [P, 2, TOK])
        enb = f("enb", [P, 2, TOK])
        ebl = f("ebl", [P, 2, TOK])
        dec = f("dec", [64, 4, 4])
        qd = f("qd", [64, 4, TOK])
        kd = f("kd", [64, 4, TOK])
        keT = f("keT", [64, 3, 256])
        va = f("va", [P, 2, 512])
        va1 = f("va1", [64, 512])
        att = f("att", [P, 4, 2, 128])
        st = [f(f"st{i}", [64, 4, 128]) for i in range(3)]
        sg = f("sg", [P, 4, TOK])
        Qd = f("Qd", [64, 2, 4, TOK])
        Kd = f("Kd", [64, 2, 4, TOK])
        vb = f("vb", [P, 2, 512])
        Sb = [f(f"Sb{i}", [P, 2, TOK]) for i in range(2)]
        W = [f(f"W{i}", [P, TOK]) for i in range(2)]
        WT = [f(f"WT{i}", [P, TOK]) for i in range(2)]
        stat = f("stat", [P, 2, 12])
        lamt = f("lamt", [P, 136])
        first.close()

        ffn = ExitStack()
        f = lambda n, s, d=F32: sb(n, s, d, ffn)
        AH = f("act_high", [P, 22, TOK], F32R)
        AL = f("act_low", [P, 22, TOK], F32R)
        cg = [f(f"gate{i}", [P, 2, TOK]) for i in range(2)]
        cv = [f(f"val{i}", [P, 2, TOK]) for i in range(2)]
        adaw = [f(f"adaw{i}", [P, 2, D]) for i in range(2)]
        adas = [f(f"adas{i}", [P, D]) for i in range(2)]
        ffn.close()

        odd = ExitStack()
        f = lambda n, s, d=F32: sb(n, s, d, odd)
        dq = [[f(f"dq{b}{g}", [P, 2, TOK]) for g in range(3)] for b in range(2)]
        dk = [[f(f"dk{b}{g}", [P, 2, TOK]) for g in range(3)] for b in range(2)]
        dv = [[f(f"dv{b}{g}", [P, 2, TOK]) for g in range(3)] for b in range(2)]
        DS = [f(f"DS{i}", [P, 3 * TOK]) for i in range(2)]
        DT = [f(f"DT{i}", [P, 6, P]) for i in range(2)]
        dstat = f("dstat", [P, 2, 4])
        odd.close()

        mla = ExitStack()
        f = lambda n, s, d=F32: sb(n, s, d, mla)
        MQ = f("MQ", [96, 8, TOK])
        MK = f("MK", [96, 8, TOK])
        mv = f("mv", [P, 2, 512])
        qr = f("qr", [P, 2, TOK])
        qs = f("qs", [P, 2, TOK])
        kr = f("kr", [32, TOK])
        krs = f("krs", [32, TOK])
        SQH = f("smallq_high", [P, 4, TOK], F32R)
        SQL = f("smallq_low", [P, 4, TOK], F32R)
        SCH = f("smallc_high", [P, 4, TOK], F32R)
        SCL = f("smallc_low", [P, 4, TOK], F32R)
        PAD = 16
        up = f("up", [P, 4, PAD + TOK])
        p1 = f("p1", [P, 4, PAD + TOK])
        p2 = f("p2", [P, 4, PAD + TOK])
        za = f("za", [P, KB, TOK])
        zb = f("zb", [P, KB, TOK])
        MS = [f(f"MS{i}", [P, TOK]) for i in range(2)]
        MT = [f(f"MT{i}", [P, TOK]) for i in range(2)]
        mstat = f("mstat", [P, 2, 4])
        mla.close()

        ffn2 = ExitStack()
        f = lambda n, s, d=F32: sb(n, s, d, ffn2)
        BH = f("act2_high", [P, 32, TOK], F32R)
        BL = f("act2_low", [P, 32, TOK], F32R)
        rl = [f(f"relu{i}", [P, 2, TOK]) for i in range(2)]
        ffn2.close()

        ps = [ctx.enter_context(nc.psum_tensor(f"bank{i}", [P, 2, TOK], F32)) for i in range(8)]
        NB, SB0, SB1, TB, OB = 3, 4, 5, 6, 7

        raw_in = [sem(f"raw_in{i}") for i in range(RAW)]
        names = """consts_in params_in x_in pos_in high_ready low_ready products_done
            trig_angle trig_done lam_sums lam_exp lam_done dve_chain act_chain pool_chain
            x_updated squares_ready sumsq_ready rstd_ready normed operand_high operand_low
            unit_squares unit_sums unit_rstd unit_normed
            ar_done ar_copied la_done la_biased la_log la_diff gate_exps va_ready gla_q gla_k ket_done
            ket_copied att_done att_zero att_masked kv_done state_ready gla_o_done vb_ready silu_ag
            diff_scores diff_max diff_exp diff_w diff_turned diff_copied diff_pv mix_ready
            conv_init conv_done silu_done act_mul act_high act_low c_silu ada_in0 ada_in1 ada_acc ada_sum ada_mod gmod_ready
            dil_scores dil_max dil_exp dil_w dil_turned dil_copied dil_pv dv_ready dil_out
            pool_zero kr_done kr_copied krot_done krope_done kfull q_nope k_nope qr_copied qrot_done q_rope mv_ready
            wide_squares wide_sums wide_rstd wide_normed cq_high cq_low ckv_high ckv_low
            u_ready pooled pooled_high pooled_low y_ready y_high y_low gates_raw gates gated_a
            mla_scores mla_max mla_exp mla_w mla_turned mla_copied mla_pv att_high att_low merged
            relu_done sq_done act2_high act2_low stored""".split()
        S = {n: sem(n) for n in names}

        block = ctx.enter_context(nc.Block())

        FILLS = {}
        total = 0
        for name, pairs in (("n0", 4), ("mix0", 4), ("n1", 4), ("n2", 4), ("mix1", 2), ("n3", 4), ("n4", 4),
                            ("merged0", 4), ("n5", 4), ("n6", 4), ("merged1", 4), ("n7", 4)):
            FILLS[name] = total
            total += pairs

        order = []
        units = {"bq0": 0, "bk0": 1, "bq1": 2, "bk1": 3}
        DIFF_U, GLA_U, DIFF_QK = (4, 7), (5, 6), (1, 3)

        def c(name):
            order.append(("chunk", name))

        def st_(name, i=0):
            order.append((name, i))

        st_("trig"), st_("lam"), st_("norm", 0), st_("ar"), c("av0"), st_("la"), c("av1"), st_("la_exps")
        c("bq0"), c("bk0"), st_("unit", 0), c("aq"), st_("unit", 1), c("ak"), c("bv0"), st_("ket")
        st_("diff_s", 0), st_("diff_s", 1), c("bq1"), st_("gla_att"), st_("diff_t", 0), st_("diff_t", 1), st_("gla_kv")
        st_("diff_s", 2), st_("diff_s", 3), c("bk1"), st_("unit", 2), st_("diff_t", 2), st_("diff_t", 3)
        c("bv1"), st_("unit", 3), st_("diff_n", 0), st_("diff_r", 0)
        st_("gla_o", 0), st_("diff_s", 4), c("ag0"), st_("gla_r", 0), st_("diff_s", 5), st_("gla_o", 1), c("ag1")
        st_("gla_r", 1), st_("diff_t", 4), st_("diff_t", 5), st_("diff_s", 6), st_("diff_s", 7), st_("diff_t", 6)
        st_("diff_t", 7), st_("ag_silu"), st_("diff_n", 1), st_("diff_r", 1)
        for p in range(4):
            c(f"evo{p}")

        def conv_stages(l):
            st_("norm", 2 * l + 1), st_("ffn_in", l)
            for j in range(11):
                c(f"up{l}g{j}")
                if j:
                    st_("act", (l, j - 1))
                c(f"up{l}v{j}"), st_("silu", (l, j))
                if j in (2, 4, 6, 8, 10):
                    st_("ada", (l, j // 2 - 1))
            st_("act", (l, 10))
            for p in range(4):
                for i in range(3):
                    c(f"down{l}_{p}_{i}")
                if p == 1:
                    st_("ada", (l, 5))

        conv_stages(0)
        st_("norm", 2)
        for hp in range(2):
            for g in range(3):
                for q in range(3):
                    c(f"od{hp}{g}{q}")
                    u = 8 + 6 * hp + 2 * g + q
                    if q >= 1:
                        st_("unit", u - 1)
                    if hp == 1:
                        k = 3 * g + q
                        if k < 4:
                            st_("dil_s", k)
                        if 1 <= k < 5:
                            st_("dil_t", k - 1)
        for u in range(4, 8):
            st_("dil_s", u)
            if u > 4:
                st_("dil_t", u - 1)
            else:
                st_("mix1", 0)
        st_("dil_t", 7)
        st_("mix1", 1)
        for p in range(4):
            c(f"odo{p}")
        conv_stages(1)
        for l in range(2):
            st_("norm", 4 + 2 * l), st_("kr", l), c(f"cq{l}a"), c(f"cq{l}b"), st_("krot", l), c(f"ckv{l}"), st_("wide", (l, 0))
            c(f"u{l}0"), st_("wide", (l, 1)), c(f"u{l}1"), c(f"uqn{l}"), c(f"uqr{l}"), c(f"uk{l}"), st_("qrot", l), c(f"uv{l}")
            st_("pool", l)
            u = 0
            for p in range(4):
                st_("mla_s", (l, u)), st_("mla_s", (l, u + 1)), c(f"gz{l}a{p}")
                st_("mla_t", (l, u)), st_("mla_t", (l, u + 1))
                u += 2
            st_("pool_split", l), c(f"wp{l}"), st_("y", l)
            for p in range(4):
                st_("mla_s", (l, u)), st_("mla_s", (l, u + 1)), c(f"gz{l}b{p}")
                st_("mla_t", (l, u)), st_("mla_t", (l, u + 1))
                u += 2
            st_("gates", l), c(f"pp{l}_0"), c(f"pp{l}_1"), c(f"pa{l}_0"), c(f"pa{l}_1")
            for p in range(4):
                c(f"wo{l}_{p}")
            st_("norm", 5 + 2 * l)
            for p in range(16):
                c(f"fa{l}_{p}")
                if p:
                    st_("act2", (l, p - 1))
            st_("act2", (l, 15))
            for p in range(4):
                for i in range(4):
                    c(f"fb{l}_{p}_{i}")
        st_("norm", 8)
        for n, name in enumerate(v for k, v in order if k == "chunk"):
            assert CH[n]["name"] == name, (n, name, CH[n]["name"])

        def bank_of(ch, i=0):
            return (ch["bank"] + i) % LIN

        def freed_by(ch, i):
            name = ch["name"]
            if name in ("av0", "av1"):
                return S["va_ready"], int(name[2]) + 1
            if name in units:
                return S["unit_normed"], units[name] + 1
            if name == "aq":
                return S["gla_q"], 1
            if name == "ak":
                return S["gla_k"], 1
            if name in ("bv0", "bv1"):
                return S["vb_ready"], int(name[2]) + 1
            if name in ("ag0", "ag1"):
                return S["silu_ag"], int(name[2]) + 1
            if name.startswith("evo"):
                return S["x_updated"], int(name[3]) + 1
            if name.startswith("up"):
                l, j = int(name[2]), int(name[4:])
                return S["conv_done"], 22 * l + 2 * j + (name[3] == "v") + 1
            if name.startswith("down"):
                l, p, _ = (int(v) for v in name[4:].split("_"))
                return S["x_updated"], 4 * (2 * l + 1) + p + 1
            if name.startswith("odo"):
                return S["x_updated"], 8 + int(name[3]) + 1
            if name.startswith("od"):
                hp, g, q = (int(v) for v in name[2:])
                if q == 2:
                    return S["dv_ready"], 3 * hp + g + 1
                return S["unit_normed"], 8 + 6 * hp + 2 * g + q + 1
            l = int([v for v in name if v.isdigit()][0])
            if name.startswith("cq"):
                return S["wide_normed"], 2 * l + 1
            if name.startswith("ckv"):
                return S["wide_normed"], 2 * l + 2
            if name[0] == "u" and name[1].isdigit():
                return S["u_ready"], 2 * l + int(name[2]) + 1
            if name.startswith("uqn"):
                return S["q_nope"], 2 * l + i + 1
            if name.startswith("uqr"):
                return S["qr_copied"], l + 1
            if name.startswith("uk"):
                return S["k_nope"], 2 * l + i + 1
            if name.startswith("uv"):
                return S["mv_ready"], 2 * l + i + 1
            if name.startswith("gz"):
                return S["gates_raw"], 8 * l + 4 * (name[3] == "b") + int(name[4]) + 1
            if name.startswith("wp"):
                return S["y_ready"], 2 * l + i + 1
            if name.startswith("pp"):
                return S["gated_a"], 4 * l + 2 * int(name[-1]) + i + 1
            if name.startswith("pa"):
                return S["merged"], 4 * l + 2 * int(name[-1]) + i + 1
            if name.startswith("wo"):
                return S["x_updated"], 16 + 8 * l + int(name[-1]) + 1
            if name.startswith("fa"):
                return S["relu_done"], 16 * l + int(name.split("_")[1]) + 1
            if name.startswith("fb"):
                return S["x_updated"], 20 + 8 * l + int(name.split("_")[1]) + 1
            raise ValueError(name)

        @block.sync
        def _(sp):
            sp.dma_start(x[:], xT).then_inc(S["x_in"], 16)
            sp.dma_start(consts[:], consts_d).then_inc(S["consts_in"], 16)
            sp.dma_start(params[:], params_d).then_inc(S["params_in"], 16)
            sp.dma_start(posi[:], positions.to_broadcast([P, TOK])).then_inc(S["pos_in"], 16)
            for ch in CH:
                n, w = ch["n"], ch["width"]
                if n >= RAW:
                    sp.wait_ge(S["low_ready"], n - RAW + 1)
                sp.dma_start(raw[n % RAW][:, 0:w], stream[ch["at"] * P:(ch["at"] + w) * P]
                             .rearrange("(p w) -> p w", p=P)).then_inc(raw_in[n % RAW], 16)
            sp.wait_ge(S["normed"], 36)
            sp.dma_start(out, h[:]).then_inc(S["stored"], 16)
            sp.wait_ge(S["stored"], 16)

        @block.tensor
        def _(pe):
            free_after, taken = {}, set()

            def claim(b):
                assert b in free_after or b not in taken, b
                taken.add(b)
                if b in free_after:
                    pe.wait_ge(*free_after.pop(b))

            def operand_wait(name):
                if name in ("av0",):
                    return S["operand_low"], lambda k: FILLS["n0"] + k // 2 + 1
                if name == "evo0":
                    return S["operand_low"], lambda k: FILLS["mix0"] + k // 2 + 1
                if name in ("up0g0", "up1g0"):
                    return S["operand_low"], lambda k: FILLS["n1" if name[2] == "0" else "n3"] + k // 2 + 1
                if name == "od000":
                    return S["operand_low"], lambda k: FILLS["n2"] + k // 2 + 1
                if name == "odo0":
                    return S["operand_low"], lambda k: FILLS["mix1"] + k // 2 + 1
                if name.startswith("down") and name.split("_")[1] == "0":
                    l = int(name[4])
                    return S["act_low"], lambda k: 11 * l + k // 2 + 1
                if name.startswith("cq") and name.endswith("a"):
                    l = int(name[2])
                    return S["operand_low"], lambda k: FILLS[f"n{4 + 2 * l}"] + k // 2 + 1
                if name.startswith("uqn"):
                    return S["cq_low"], lambda k: int(name[3]) + 1
                if name.startswith("uk"):
                    return S["ckv_low"], lambda k: int(name[2]) + 1
                if name.startswith("wp"):
                    return S["pooled_low"], lambda k: 2 * int(name[2]) + 2
                if name.startswith("pp") and name.endswith("0"):
                    return S["y_low"], lambda k: 2 * int(name[2]) + k // 2 + 1
                if name.startswith("pa") and name.endswith("_0"):
                    return S["att_low"], lambda k: 2 * int(name[2]) + k // 2 + 1
                if name.startswith("wo") and name.endswith("_0"):
                    return S["operand_low"], lambda k: FILLS[f"merged{name[2]}"] + k // 2 + 1
                if name.startswith("fa") and name.endswith("_0"):
                    return S["operand_low"], lambda k: FILLS[f"n{5 + 2 * int(name[2])}"] + k // 2 + 1
                if name.startswith("fb") and name.split("_")[1] == "0":
                    return S["act2_low"], lambda k: 16 * int(name[2]) + k // 2 + 1
                return None

            def chunk(name):
                ch = BY[name]
                n, rows, width = ch["n"], ch["rows"], ch["width"]
                wh, wl = high[n % SPLIT], low[n % SPLIT]
                act = "A" if ch["op"] == "A" and name[0] == "d" else "B" if ch["op"] == "A" else ch["op"]
                oh, ol = {"O": (OH, OL), "A": (AH, AL), "B": (BH, BL), "Q": (SQH, SQL), "C": (SCH, SCL)}[act]
                waits, seen = operand_wait(name), 0
                ncols = len(ch["cols"])
                pe.wait_ge(S["low_ready"], n + 1)
                if ch["first"]:
                    for i in range(ch["banks"]):
                        claim(bank_of(ch, i))

                def need(k):
                    nonlocal seen
                    if waits is not None and waits[1](k) > seen:
                        seen = waits[1](k)
                        pe.wait_ge(waits[0], seen)

                if ch["tm"]:
                    for t in range(2):
                        for i, k in enumerate(rows):
                            need(k)
                            o = (ps[bank_of(ch)][:, t, :] if ncols == 256 else
                                 ps[bank_of(ch, t)][:].rearrange("p a b -> p (a b)"))
                            w = slice(i * ncols, (i + 1) * ncols)
                            tk = slice(t * P, (t + 1) * P)
                            pe.matmul(o, ol[:, k, tk], wh[:, w], start=i == 0, stop=False)
                            pe.matmul(o, oh[:, k, tk], wl[:, w], start=False, stop=False)
                            mm = pe.matmul(o, oh[:, k, tk], wh[:, w], start=False, stop=i == len(rows) - 1)
                else:
                    for b in range(ncols // P):
                        o = ps[bank_of(ch, b // 2)][:, b % 2, :]
                        mine = [b] if ch["diag"] else rows
                        for i, k in enumerate(mine):
                            need(k)
                            w = slice(b * P, (b + 1) * P) if ch["diag"] else slice(i * ncols + b * P,
                                                                                   i * ncols + (b + 1) * P)
                            one = ch["first"] and i == 0 and (b % 2 == 0 or (ch["last"]))
                            end = ch["last"] and i == len(mine) - 1
                            pe.matmul(o, wl[:, w], oh[:, k, :], start=one, stop=False, skip_group_check=True)
                            pe.matmul(o, wh[:, w], ol[:, k, :], start=False, stop=False, skip_group_check=True)
                            mm = pe.matmul(o, wh[:, w], oh[:, k, :], start=False, stop=end, skip_group_check=True)
                mm.then_inc(S["products_done"], 1)
                if ch["last"]:
                    for i in range(ch["banks"]):
                        free_after[bank_of(ch, i)] = freed_by(ch, i)

            def norm(i):
                claim(NB)
                for k in range(KB):
                    pe.wait_ge(S["squares_ready"], 4 * i + k // 2 + 1)
                    mm = pe.matmul(ps[NB][:, 0, :], col("ones"), h[:, k, :], start=k == 0, stop=k == KB - 1)
                mm.then_inc(S["sumsq_ready"], 1)
                free_after[NB] = (S["rstd_ready"], i + 1)

            def unit(u):
                pe.wait_ge(S["unit_squares"], u + 1)
                claim(NB)
                pe.matmul(ps[NB][:].rearrange("p a b -> p (a b)"), col("ones64" if u < 4 else "ones"),
                          sq[u % 2][:].rearrange("p a b -> p (a b)"), start=True, stop=True).then_inc(S["unit_sums"], 1)
                free_after[NB] = (S["unit_rstd"], u + 1)

            def ar_(_):
                claim(OB)
                for k in range(KB):
                    if k % 2 == 0:
                        pe.wait_ge(S["normed"], k // 2 + 1)
                    mm = pe.matmul(ps[OB][0:16, 0, :], col("w_ar", 16 * k, 16), h[:, k, :], start=k == 0,
                                   stop=k == KB - 1)
                mm.then_inc(S["ar_done"], 1)
                free_after[OB] = (S["ar_copied"], 1)

            def la_(_):
                pe.wait_ge(S["ar_copied"], 1)
                claim(TB)
                for b in range(2):
                    mm = pe.matmul(ps[TB][:, b, :], col("w_a2", b * P, P)[0:16], ar[:], start=True, stop=True)
                mm.then_inc(S["la_done"], 1)
                free_after[TB] = (S["la_biased"], 1)

            def ket(_):
                pe.wait_ge(S["gla_k"], 1)
                claim(TB)
                for t in range(2):
                    for b in range(2):
                        mm = pe.transpose(ps[TB][:, t, b * P:(b + 1) * P], la[:, b, t * P:(t + 1) * P], col("ident"))
                mm.then_inc(S["ket_done"], 1)
                free_after[TB] = (S["ket_copied"], 1)

            def gla_att(_):
                for hh in range(4):
                    if hh % 2 == 0:
                        claim((SB0, SB1)[hh // 2])
                    for t in range(2):
                        tk = slice(t * P, (t + 1) * P)
                        mm = pe.matmul(ps[(SB0, SB1)[hh // 2]][:, hh % 2, tk], kd[:, hh, tk], qd[:, hh, tk],
                                       start=True, stop=True)
                    if hh % 2:
                        mm.then_inc(S["att_done"], 1)
                        free_after[(SB0, SB1)[hh // 2]] = (S["att_masked"], hh // 2 + 1)

            def gla_kv(_):
                pe.wait_ge(S["ket_copied"], 1)
                pe.wait_ge(S["va_ready"], 2)
                for cc in range(3):
                    claim(TB)
                    v = (va[0:64, 0, :], va1[:], va[0:64, 1, :])[cc]
                    for hh in range(4):
                        o = ps[TB][0:64].rearrange("p a b -> p (a b)")
                        mm = pe.matmul(o[:, hh * P:(hh + 1) * P], keT[:, cc, hh * 64:(hh + 1) * 64],
                                       v[:, hh * P:(hh + 1) * P], start=True, stop=True)
                    mm.then_inc(S["kv_done"], 1)
                    free_after[TB] = (S["state_ready"], cc + 1)

            def gla_o(hp):
                if hp == 0:
                    pe.wait_ge(S["att_masked"], 2)
                    pe.wait_ge(S["state_ready"], 3)
                claim(OB)
                for hh in (2 * hp, 2 * hp + 1):
                    for t in range(2):
                        pe.matmul(ps[OB][:, hh % 2, t * P:(t + 1) * P], va[:, t, hh * P:(hh + 1) * P], att[:, hh, t, :],
                                  start=True, stop=False, skip_group_check=True)
                        for cc in (2 * t, 2 * t + 1):
                            if cc:
                                ck = slice(cc * 64, (cc + 1) * 64)
                                mm = pe.matmul(ps[OB][:, hh % 2, ck], st[cc - 1][:, hh, :], qd[:, hh, ck], start=False,
                                               stop=cc % 2 == 1, skip_group_check=True)
                mm.then_inc(S["gla_o_done"], 1)
                free_after[OB] = (S["unit_normed"], GLA_U[hp] + 1)

            def diff_s(u):
                hh, qt = u // 2, u % 2
                if u % 4 == 0:
                    pe.wait_ge(S["unit_normed"], DIFF_QK[u // 4] + 1)
                claim((SB0, SB1)[u % 2])
                nk = P * (qt + 1)
                for cc in range(2):
                    mm = pe.matmul(ps[(SB0, SB1)[u % 2]][:, cc, 0:nk], Qd[:, cc, hh, qt * P:(qt + 1) * P],
                                   Kd[:, cc, hh, 0:nk], start=True, stop=True)
                mm.then_inc(S["diff_scores"], 1)
                free_after[(SB0, SB1)[u % 2]] = (S["diff_max"], u + 1)

            def diff_t(u):
                hh, qt = u // 2, u % 2
                pe.wait_ge(S["diff_w"], u + 1)
                claim(TB)
                for kt in range(qt + 1):
                    mm = pe.transpose(ps[TB][:, 0, kt * P:(kt + 1) * P], W[u % 2][:, kt * P:(kt + 1) * P], col("ident"))
                mm.then_inc(S["diff_turned"], 1)
                free_after[TB] = (S["diff_copied"], u + 1)
                pe.wait_ge(S["diff_copied"], u + 1)
                if u % 4 == 0:
                    pe.wait_ge(S["vb_ready"], u // 4 + 1)
                    claim(OB)
                for kt in range(qt + 1):
                    mm = pe.matmul(ps[OB][:, hh % 2, qt * P:(qt + 1) * P], vb[:, kt, hh * P:(hh + 1) * P],
                                   WT[u % 2][:, kt * P:(kt + 1) * P], start=kt == 0, stop=kt == qt)
                mm.then_inc(S["diff_pv"], 1)
                if u % 4 == 3:
                    free_after[OB] = (S["unit_normed"], DIFF_U[u // 4] + 1)

            def dil_s(u):
                hh, qt = u // 2, u % 2
                hp = hh // 2
                if u % 4 == 0:
                    pe.wait_ge(S["unit_normed"], 8 + 6 * hp + 6)
                nk = P * (qt + 1)
                for b in (SB0, SB1):
                    claim(b)
                for g in range(3):
                    o = ps[(SB0, SB1)[g // 2]][:, g % 2, 0:nk]
                    mm = pe.matmul(o, dq[hp][g][:, hh % 2, qt * P:(qt + 1) * P], dk[hp][g][:, hh % 2, 0:nk],
                                   start=True, stop=True)
                mm.then_inc(S["dil_scores"], 1)
                free_after[SB0] = free_after[SB1] = (S["dil_max"], u + 1)

            def dil_t(u):
                hh, qt = u // 2, u % 2
                hp, nk = hh // 2, P * (qt + 1)
                pe.wait_ge(S["dil_w"], u + 1)
                n = 3 * (qt + 1)
                for part in range(0, n, 3):
                    claim(TB)
                    for i in range(part, part + 3):
                        o = ps[TB][:].rearrange("p a b -> p (a b)")[:, (i - part) * P:(i - part + 1) * P]
                        mm = pe.transpose(o, DS[u % 2][:, i * P:(i + 1) * P], col("ident"))
                    mm.then_inc(S["dil_turned"], 1)
                    turned = 3 * hh + qt + part // 3 + 1
                    free_after[TB] = (S["dil_copied"], turned)
                pe.wait_ge(S["dil_copied"], turned)
                if u % 4 == 0:
                    pe.wait_ge(S["dv_ready"], 3 * hp + 3)
                    claim(OB)
                for g in range(3):
                    for kt in range(qt + 1):
                        mm = pe.matmul(ps[OB][:, hh % 2, qt * P:(qt + 1) * P], dv[hp][g][:, kt, (hh % 2) * P:(hh % 2 + 1) * P],
                                       DT[u % 2][:, g * (qt + 1) + kt, :], start=g == 0 and kt == 0,
                                       stop=g == 2 and kt == qt)
                mm.then_inc(S["dil_pv"], 1)
                if u % 4 == 3:
                    free_after[OB] = (S["dil_out"], hp + 1)

            def ada_(a):
                l, seg = a
                pe.wait_ge(S["ada_acc"], 6 * l + seg + 1)
                claim(NB)
                for b in range(8):
                    mm = pe.matmul(ps[NB][:, 0, b:b + 1], adas[seg % 2][:, b * P:(b + 1) * P], col("ones", 0, 1),
                                   start=True, stop=True)
                mm.then_inc(S["ada_sum"], 1)
                free_after[NB] = (S["ada_mod"], 6 * l + seg + 1)

            def kr_(l):
                claim(OB)
                for k in range(KB):
                    if k % 2 == 0:
                        pe.wait_ge(S["normed"], 4 * (4 + 2 * l) + k // 2 + 1)
                    mm = pe.matmul(ps[OB][0:32, 0, :], col("w_kr", (8 * l + k) * 32, 32), h[:, k, :], start=k == 0,
                                   stop=k == KB - 1)
                mm.then_inc(S["kr_done"], 1)
                free_after[OB] = (S["kr_copied"], l + 1)

            def krot(l):
                pe.wait_ge(S["kr_copied"], l + 1)
                claim(TB)
                pe.matmul(ps[TB][0:32, 0, :], col("rot", 0, 32)[0:32], kr[:], start=True, stop=True)\
                    .then_inc(S["krot_done"], 1)
                free_after[TB] = (S["krope_done"], l + 1)

            def wide(a):
                l, which = a
                i = 2 * l + which
                pe.wait_ge(S["wide_squares"], i + 1)
                claim(NB)
                blocks = range(3) if which == 0 else range(3, 5)
                for k in blocks:
                    mm = pe.matmul(ps[NB][:, 0, :], col("ones"), h[:, k, :], start=k == blocks[0], stop=k == blocks[-1])
                mm.then_inc(S["wide_sums"], 1)
                free_after[NB] = (S["wide_rstd"], i + 1)

            def qrot(l):
                pe.wait_ge(S["qr_copied"], l + 1)
                claim(TB)
                pe.matmul(ps[TB][:].rearrange("p a b -> p (a b)"), col("rot"), qr[:].rearrange("p a b -> p (a b)"),
                          start=True, stop=True).then_inc(S["qrot_done"], 1)
                free_after[TB] = (S["q_rope"], 2 * l + 1)

            def mla_s(a):
                l, u = a
                hh, qt = u // 2, u % 2
                U = 16 * l + u
                if u == 0:
                    pe.wait_ge(S["q_rope"], 2 * l + 2)
                    pe.wait_ge(S["q_nope"], 2 * l + 2)
                    pe.wait_ge(S["k_nope"], 2 * l + 2)
                    pe.wait_ge(S["kfull"], l + 1)
                claim((SB0, SB1)[u % 2])
                nk = P * (qt + 1)
                pe.matmul(ps[(SB0, SB1)[u % 2]][:, 0, 0:nk], MQ[:, hh, qt * P:(qt + 1) * P], MK[:, hh, 0:nk],
                          start=True, stop=True).then_inc(S["mla_scores"], 1)
                free_after[(SB0, SB1)[u % 2]] = (S["mla_max"], U + 1)

            def mla_t(a):
                l, u = a
                hh, qt = u // 2, u % 2
                U = 16 * l + u
                pe.wait_ge(S["mla_w"], U + 1)
                claim(TB)
                for kt in range(qt + 1):
                    mm = pe.transpose(ps[TB][:, 0, kt * P:(kt + 1) * P], MS[u % 2][:, kt * P:(kt + 1) * P], col("ident"))
                mm.then_inc(S["mla_turned"], 1)
                free_after[TB] = (S["mla_copied"], U + 1)
                pe.wait_ge(S["mla_copied"], U + 1)
                if u == 0:
                    pe.wait_ge(S["mv_ready"], 2 * l + 2)
                if u % 8 == 0:
                    claim(OB)
                r = slice(64 * (hh % 2), 64 * (hh % 2) + 64)
                for kt in range(qt + 1):
                    mm = pe.matmul(ps[OB][r, (hh // 2) % 2, qt * P:(qt + 1) * P], mv[:, kt, hh * 64:(hh + 1) * 64],
                                   MT[u % 2][:, kt * P:(kt + 1) * P], start=kt == 0, stop=kt == qt)
                mm.then_inc(S["mla_pv"], 1)
                if u % 8 == 7:
                    free_after[OB] = (S["att_low"], 2 * l + u // 8 + 1)

            pe.wait_ge(S["consts_in"], 16)
            pe.wait_ge(S["params_in"], 16)
            stages = dict(chunk=chunk, norm=norm, unit=unit, ar=ar_, la=la_, ket=ket, gla_att=gla_att, gla_kv=gla_kv,
                          gla_o=gla_o, diff_s=diff_s, diff_t=diff_t, dil_s=dil_s, dil_t=dil_t, ada=ada_, kr=kr_,
                          krot=krot, wide=wide, qrot=qrot, mla_s=mla_s, mla_t=mla_t, gla_r=lambda hp: unit(GLA_U[hp]),
                          diff_r=lambda hp: unit(DIFF_U[hp]))
            for stage, i in order:
                if stage in stages:
                    stages[stage](i)

        @block.scalar
        def _(act):
            chain, split_to = [0], [0]

            def link(ins):
                chain[0] += 1
                ins.then_inc(S["act_chain"], 1)
                act.wait_ge(S["act_chain"], chain[0])

            def high_upto(n):
                while split_to[0] <= min(n, NCH - 1):
                    m = split_to[0]
                    act.wait_ge(raw_in[m % RAW], 16 * (m // RAW + 1))
                    if m >= SPLIT:
                        act.wait_ge(S["products_done"], m - SPLIT + 1)
                        act.wait_ge(S["low_ready"], m - SPLIT + 1)
                    w = CH[m]["width"]
                    act.activation(high[m % SPLIT][:, 0:w], raw[m % RAW][:, 0:w], ACT.Copy)\
                        .then_inc(S["high_ready"], 1)
                    split_to[0] += 1

            def squares_of(u, bank):
                if u >= 2:
                    act.wait_ge(S["unit_sums"], u - 1)
                act.activation(sq[u % 2][:], ps[bank][:], ACT.Square).then_inc(S["unit_squares"], 1)

            def unit(u):
                act.wait_ge(S["unit_sums"], u + 1)
                if u >= 2:
                    act.wait_ge(S["unit_normed"], u - 1)
                link(act.activation(rb[u % 2][:], ps[NB][:], ACT.Ln, scale=1.0 / (64 if u < 4 else 128),
                                    bias=col("eps")))
                act.activation(rb[u % 2][:], rb[u % 2][:], ACT.Exp, scale=-0.5).then_inc(S["unit_rstd"], 1)

            def chunk(name):
                ch = BY[name]
                n = ch["n"]
                act.wait_ge(S["products_done"], n + 1)
                b = bank_of(ch)
                if name in ("av0", "av1"):
                    j = int(name[2]) * 256
                    act.activation(va[:, :, j:j + 256], ps[b][:], ACT.Copy)
                    act.activation(va1[:, j:j + 256], ps[b][64:128, 0, :], ACT.Copy).then_inc(S["va_ready"], 1)
                elif name in units:
                    squares_of(units[name], b)
                elif name in ("bv0", "bv1"):
                    j = int(name[2]) * 256
                    act.activation(vb[:, :, j:j + 256], ps[b][:], ACT.Copy).then_inc(S["vb_ready"], 1)
                elif name in ("ag0", "ag1"):
                    j = int(name[2]) * 2
                    act.activation(sg[:, j:j + 2, :], ps[b][:], ACT.Copy).then_inc(S["silu_ag"], 1)
                elif name.startswith("up"):
                    l, j, v = int(name[2]), int(name[4:]), int(name[3] == "v")
                    if j >= 2:
                        act.wait_ge(S["act_low"], 11 * l + j - 1)
                    dst = (cg, cv)[v][j % 2]
                    for i in range(2):
                        t = (44 * l + 22 * v + 2 * j + i) * 4
                        ins = act.activation(dst[:, i, :], ps[b][:, i, :], ACT.Identity, scale=col("conv", t + 2, 1),
                                             bias=col("conv", t + 3, 1))
                    ins.then_inc(S["conv_init"], 1)
                elif name.startswith("od") and name[2] != "o":
                    hp, g, q = (int(v) for v in name[2:])
                    if q == 2:
                        act.activation(dv[hp][g][:], ps[b][:], ACT.Copy).then_inc(S["dv_ready"], 1)
                    else:
                        squares_of(8 + 6 * hp + 2 * g + q, b)
                elif name.startswith("cq"):
                    if name[3] == "a":
                        act.activation(h[:, 0:2, :], ps[b][:], ACT.Square)
                    else:
                        act.activation(h[:, 2, :], ps[b][:, 0, :], ACT.Square).then_inc(S["wide_squares"], 1)
                elif name.startswith("ckv"):
                    act.activation(h[:, 3:5, :], ps[b][:], ACT.Square).then_inc(S["wide_squares"], 1)
                elif name[0] == "u" and name[1].isdigit():
                    j = int(name[2])
                    act.activation(up[:, 2 * j:2 * j + 2, PAD:], ps[b][:], ACT.Copy).then_inc(S["u_ready"], 1)
                elif name.startswith("uqn"):
                    for i in range(2):
                        for half in range(2):
                            ins = act.activation(MQ[0:64, 4 * i + half:4 * i + 4:2, :],
                                                 ps[bank_of(ch, i)][64 * half:64 * half + 64], ACT.Copy)
                        ins.then_inc(S["q_nope"], 1)
                elif name.startswith("uqr"):
                    act.activation(qr[:], ps[b][:], ACT.Copy).then_inc(S["qr_copied"], 1)
                elif name.startswith("uv"):
                    for t in range(2):
                        act.activation(mv[:, t, :], ps[bank_of(ch, t)][:].rearrange("p a b -> p (a b)"), ACT.Copy)\
                            .then_inc(S["mv_ready"], 1)
                elif name.startswith("gz"):
                    p = int(name[4])
                    act.activation((za, zb)[name[3] == "b"][:, 2 * p:2 * p + 2, :], ps[b][:], ACT.Copy)\
                        .then_inc(S["gates_raw"], 1)
                elif name.startswith("wp"):
                    l = int(name[2])
                    for g in range(4):
                        ins = act.activation(p1[:, g, PAD:], ps[bank_of(ch, g // 2)][:, g % 2, :], ACT.Copy,
                                             scale=col("pool_scale", 4 * l + g, 1))
                        if g % 2:
                            ins.then_inc(S["y_ready"], 1)
                elif name.startswith("fa"):
                    l, p = int(name[2]), int(name.split("_")[1])
                    if p >= 2:
                        act.wait_ge(S["act2_low"], 16 * l + p - 1)
                    act.activation(rl[p % 2][:], ps[b][:], ACT.Relu).then_inc(S["relu_done"], 1)
                elif name.startswith("pa"):
                    l, i2 = int(name[2]), int(name[-1])
                    high_upto(n + SPLIT)
                    for p in (2 * i2, 2 * i2 + 1):
                        act.wait_ge(S["merged"], 4 * l + p + 1)
                        act.activation(OH[:, 2 * p:2 * p + 2, :], h[:, 2 * p:2 * p + 2, :], ACT.Copy)\
                            .then_inc(S["operand_high"], 1)
                high_upto(n + SPLIT)

            def norm(i):
                if i == 0:
                    act.wait_ge(S["x_in"], 16)
                for p in range(4):
                    if i:
                        act.wait_ge(S["x_updated"], 4 * (i - 1) + p + 1)
                    act.activation(h[:, 2 * p:2 * p + 2, :], x[:, 2 * p:2 * p + 2, :], ACT.Square)\
                        .then_inc(S["squares_ready"], 1)
                if i in (2, 4, 6, 8):
                    act.preload_act_table_set(EXP_LN)
                act.wait_ge(S["sumsq_ready"], i + 1)
                link(act.activation(rn[:], ps[NB][:, 0, :], ACT.Ln, scale=1.0 / D, bias=col("eps")))
                act.activation(rn[:], rn[:], ACT.Exp, scale=-0.5).then_inc(S["rstd_ready"], 1)
                if i < 8:
                    for p in range(4):
                        act.wait_ge(S["normed"], 4 * i + p + 1)
                        act.activation(OH[:, 2 * p:2 * p + 2, :], h[:, 2 * p:2 * p + 2, :], ACT.Copy)\
                            .then_inc(S["operand_high"], 1)

            def trig(_):
                act.wait_ge(S["trig_angle"], 1)
                act.activation(sinT[:], ang[:], ACT.Sin)
                act.activation(cosT[:], turn[:], ACT.Sin).then_inc(S["trig_done"], 1)
                act.preload_act_table_set(EXP_LN)

            def lam(_):
                act.wait_ge(S["lam_sums"], 1)
                act.activation(small[:, 4:6], small[:, 2:4], ACT.Exp).then_inc(S["lam_exp"], 1)

            def ar_(_):
                act.wait_ge(S["ar_done"], 1)
                act.activation(ar[:], ps[OB][0:16, 0, :], ACT.Copy).then_inc(S["ar_copied"], 1)

            def la_(_):
                act.wait_ge(S["la_done"], 1)
                for b in range(2):
                    ins = act.activation(la[:, b, :], ps[TB][:, b, :], ACT.Identity, bias=col("b_a", b, 1))
                ins.then_inc(S["la_biased"], 1)
                act.wait_ge(S["la_biased"], 1)
                link(act.activation(ebl[:], la[:], ACT.Abs))
                link(act.activation(ebl[:], ebl[:], ACT.Exp, scale=-1.0))
                act.activation(ebl[:], ebl[:], ACT.Ln, bias=col("ones", 0, 1)).then_inc(S["la_log"], 1)

            def la_exps(_):
                act.wait_ge(S["la_diff"], 1)
                act.activation(eb[:], bc[:], ACT.Exp, scale=1 / 16).then_inc(S["gate_exps"], 1)
                act.activation(enb[:], bc[:], ACT.Exp, scale=-1 / 16).then_inc(S["gate_exps"], 1)
                act.activation(ebl[:], ebl[:], ACT.Exp, scale=1 / 16).then_inc(S["gate_exps"], 1)

            def ket(_):
                act.wait_ge(S["ket_done"], 1)
                for cc in range(3):
                    r = slice(64 * (cc % 2), 64 * (cc % 2) + 64)
                    ins = act.activation(keT[:, cc, :], ps[TB][r, cc // 2, :], ACT.Copy)
                ins.then_inc(S["ket_copied"], 1)

            def ag_silu(_):
                act.wait_ge(S["silu_ag"], 2)
                act.activation(sg[:], sg[:], ACT.Silu).then_inc(S["silu_ag"], 1)
                act.preload_act_table_set(EXP_LN)
                mix_high((0, 1))

            def mix_high(pairs):
                for p in pairs:
                    if p < 2:
                        act.wait_ge(S["mix_ready"], p + 1)
                    else:
                        act.wait_ge(S["unit_normed"], DIFF_U[p - 2] + 1)
                    act.activation(OH[:, 2 * p:2 * p + 2, :], h[:, 2 * p:2 * p + 2, :], ACT.Copy)\
                        .then_inc(S["operand_high"], 1)

            def softmax_exp(scores, sums, src, neg_max, total, scale, inc):
                act.wait_ge(*scores)
                act.activation(src, src, ACT.Exp, bias=neg_max, scale=scale, accum_out=total).then_inc(inc, 1)

            def diff_s(u):
                act.wait_ge(S["diff_max"], u + 1)
                nk = P * (u % 2 + 1)
                for cc in range(2):
                    ins = act.activation(Sb[u % 2][:, cc, 0:nk], Sb[u % 2][:, cc, 0:nk], ACT.Exp, scale=0.125,
                                         bias=stat[:, u % 2, 2 + cc:3 + cc], accum_out=stat[:, u % 2, 4 + cc:5 + cc])
                ins.then_inc(S["diff_exp"], 1)

            def diff_t(u):
                nk = P * (u % 2 + 1)
                act.wait_ge(S["diff_turned"], u + 1)
                if u >= 2:
                    act.wait_ge(S["diff_pv"], u - 1)
                act.activation(WT[u % 2][:, 0:nk], ps[TB][:, 0, 0:nk], ACT.Copy).then_inc(S["diff_copied"], 1)

            def dil_s(u):
                act.wait_ge(S["dil_max"], u + 1)
                nk = P * (u % 2 + 1)
                act.activation(DS[u % 2][:, 0:3 * nk], DS[u % 2][:, 0:3 * nk], ACT.Exp, scale=128 ** -0.5,
                               bias=dstat[:, u % 2, 1:2], accum_out=dstat[:, u % 2, 2:3]).then_inc(S["dil_exp"], 1)

            def dil_t(u):
                hh, qt = u // 2, u % 2
                for part in range(qt + 1):
                    turned = 3 * hh + qt + part + 1
                    act.wait_ge(S["dil_turned"], turned)
                    if u >= 2 and part == 0:
                        act.wait_ge(S["dil_pv"], u - 1)
                    act.activation(DT[u % 2][:, 3 * part:3 * part + 3, :], ps[TB][:].rearrange("p a b -> p (a b)")[:, 0:384]
                                   .rearrange("p (a b) -> p a b", a=3), ACT.Copy).then_inc(S["dil_copied"], 1)
                if u % 4 == 3:
                    hp = u // 4
                    act.wait_ge(S["dil_pv"], u + 1)
                    act.activation(h[:, 2 * hp:2 * hp + 2, :], ps[OB][:], ACT.Copy).then_inc(S["dil_out"], 1)

            def mix1(hp):
                act.wait_ge(S["dil_out"], hp + 1)
                act.wait_ge(S["products_done"], BY["od122"]["n"] + 1)
                act.activation(OH[:, 2 * hp:2 * hp + 2, :], h[:, 2 * hp:2 * hp + 2, :], ACT.Copy)\
                    .then_inc(S["operand_high"], 1)

            def ffn_in(l):
                if l == 0:
                    act.activation(cact[:], col("c"), ACT.Silu).then_inc(S["c_silu"], 1)

            def silu(a):
                l, j = a
                act.wait_ge(S["conv_done"], 22 * l + 2 * j + 1)
                act.activation(cg[j % 2][:], cg[j % 2][:], ACT.Silu).then_inc(S["silu_done"], 1)

            def act_(a):
                l, j = a
                act.wait_ge(S["act_mul"], 11 * l + j + 1)
                act.activation(AH[:, 2 * j:2 * j + 2, :], cg[j % 2][:], ACT.Copy).then_inc(S["act_high"], 1)

            def act2(a):
                l, p = a
                act.wait_ge(S["sq_done"], 16 * l + p + 1)
                act.activation(BH[:, 2 * p:2 * p + 2, :], rl[p % 2][:], ACT.Copy).then_inc(S["act2_high"], 1)

            def kr_(l):
                act.wait_ge(S["kr_done"], l + 1)
                act.activation(kr[:], ps[OB][0:32, 0, :], ACT.Copy).then_inc(S["kr_copied"], 1)

            def wide(a):
                l, which = a
                i = 2 * l + which
                act.wait_ge(S["wide_sums"], i + 1)
                if i:
                    act.wait_ge(S["wide_normed"], i)
                link(act.activation(rn[:], ps[NB][:, 0, :], ACT.Ln, scale=1.0 / (384, 256)[which], bias=col("eps")))
                act.activation(rn[:], rn[:], ACT.Exp, scale=-0.5).then_inc(S["wide_rstd"], 1)
                act.wait_ge(S["wide_normed"], i + 1)
                if which == 0:
                    act.activation(SQH[:, 0:3, :], h[:, 0:3, :], ACT.Copy).then_inc(S["cq_high"], 1)
                else:
                    act.activation(SCH[:, 0:2, :], h[:, 3:5, :], ACT.Copy).then_inc(S["ckv_high"], 1)

            def pool_split(l):
                act.wait_ge(S["pooled"], 2 * l + 1)
                act.activation(SQH[:, 0::2, :], p1[:, 0::2, PAD:], ACT.Copy).then_inc(S["pooled_high"], 1)
                act.wait_ge(S["pooled"], 2 * l + 2)
                act.activation(SQH[:, 1::2, :], p2[:, 1::2, PAD:], ACT.Copy).then_inc(S["pooled_high"], 1)

            def y_(l):
                for i in range(2):
                    act.wait_ge(S["y_ready"], 2 * l + i + 1)
                    act.activation(SQH[:, 2 * i:2 * i + 2, :], p1[:, 2 * i:2 * i + 2, PAD:], ACT.Copy)\
                        .then_inc(S["y_high"], 1)

            def gates(l):
                act.wait_ge(S["gates_raw"], 8 * l + 8)
                act.activation(za[:], za[:], ACT.Sigmoid).then_inc(S["gates"], 1)
                act.activation(zb[:], zb[:], ACT.Sigmoid).then_inc(S["gates"], 1)

            def mla_s(a):
                l, u = a
                U, nk = 16 * l + u, P * (u % 2 + 1)
                act.wait_ge(S["mla_max"], U + 1)
                act.activation(MS[u % 2][:, 0:nk], MS[u % 2][:, 0:nk], ACT.Exp, scale=96 ** -0.5,
                               bias=mstat[:, u % 2, 1:2], accum_out=mstat[:, u % 2, 2:3]).then_inc(S["mla_exp"], 1)

            def mla_t(a):
                l, u = a
                U, nk = 16 * l + u, P * (u % 2 + 1)
                act.wait_ge(S["mla_turned"], U + 1)
                if U >= 2:
                    act.wait_ge(S["mla_pv"], U - 1)
                act.activation(MT[u % 2][:, 0:nk], ps[TB][:, 0, 0:nk], ACT.Copy).then_inc(S["mla_copied"], 1)
                if u % 8 == 7:
                    i = u // 8
                    act.wait_ge(S["mla_pv"], U + 1)
                    act.activation(SCH[:, 2 * i:2 * i + 2, :], ps[OB][:], ACT.Copy).then_inc(S["att_high"], 1)

            act.wait_ge(S["consts_in"], 16)
            act.wait_ge(S["params_in"], 16)
            high_upto(SPLIT - 1)

            def gla_o(hp):
                act.wait_ge(S["gla_o_done"], hp + 1)
                squares_of(GLA_U[hp], OB)

            def diff_n(i):
                act.wait_ge(S["diff_pv"], 4 * i + 4)
                squares_of(DIFF_U[i], OB)

            def diff_r(i):
                unit(DIFF_U[i])
                if i == 1:
                    mix_high((2, 3))

            stages = dict(chunk=chunk, norm=norm, unit=unit, trig=trig, lam=lam, ar=ar_, la=la_, la_exps=la_exps, ket=ket,
                          ag_silu=ag_silu, diff_s=diff_s, diff_t=diff_t, dil_s=dil_s, dil_t=dil_t, mix1=mix1, ffn_in=ffn_in,
                          silu=silu, act=act_, act2=act2, kr=kr_, wide=wide, pool_split=pool_split, y=y_, gates=gates,
                          mla_s=mla_s, mla_t=mla_t, gla_o=gla_o, gla_r=lambda hp: unit(GLA_U[hp]), diff_n=diff_n,
                          diff_r=diff_r)
            for stage, i in order:
                if stage in stages:
                    stages[stage](i)

        @block.vector
        def _(dve):
            chain, split_to = [0], [0]

            def link(ins):
                chain[0] += 1
                ins.then_inc(S["dve_chain"], 1)
                dve.wait_ge(S["dve_chain"], chain[0])

            def low_upto(n):
                while split_to[0] <= min(n, NCH - 1):
                    m = split_to[0]
                    if m >= SPLIT:
                        dve.wait_ge(S["products_done"], m - SPLIT + 1)
                    dve.wait_ge(S["high_ready"], m + 1)
                    w = CH[m]["width"]
                    dve.tensor_tensor(low[m % SPLIT][:, 0:w], raw[m % RAW][:, 0:w], high[m % SPLIT][:, 0:w],
                                      ALU.subtract).then_inc(S["low_ready"], 1)
                    split_to[0] += 1

            def operand_low(f, p):
                dve.wait_ge(S["operand_high"], FILLS[f] + p + 1)
                dve.tensor_tensor(OL[:, 2 * p:2 * p + 2, :], h[:, 2 * p:2 * p + 2, :], OH[:, 2 * p:2 * p + 2, :],
                                  ALU.subtract).then_inc(S["operand_low"], 1)

            def add_to_x(b, p, gain=None):
                xp = x[:, 2 * p:2 * p + 2, :]
                if gain is None:
                    dve.tensor_tensor(xp, ps[b][:], xp, ALU.add).then_inc(S["x_updated"], 1)
                else:
                    for i in range(2):
                        ins = dve.scalar_tensor_tensor(out=x[:, 2 * p + i, :], in0=ps[b][:, i, :],
                                                       scalar=gain[:, 2 * p + i:2 * p + i + 1], in1=x[:, 2 * p + i, :],
                                                       op0=ALU.mult, op1=ALU.add)
                    ins.then_inc(S["x_updated"], 1)

            def chunk(name):
                ch = BY[name]
                n, b = ch["n"], bank_of(ch)
                if ch["last"]:
                    dve.wait_ge(S["products_done"], n + 1)
                if name == "aq":
                    dve.wait_ge(S["gate_exps"], 3)
                    for half in range(2):
                        r = slice(64 * half, 64 * half + 64)
                        ins = dve.scalar_tensor_tensor(out=qd[:, half::2, :], in0=ps[b][r], scalar=0.125, in1=eb[r],
                                                       op0=ALU.mult, op1=ALU.mult)
                    ins.then_inc(S["gla_q"], 1)
                elif name == "ak":
                    for half in range(2):
                        r = slice(64 * half, 64 * half + 64)
                        dve.tensor_tensor(kd[:, half::2, :], ps[b][r], enb[r], ALU.mult)
                    dve.tensor_tensor(la[:], ps[b][:], ebl[:], ALU.mult).then_inc(S["gla_k"], 1)
                elif name.startswith("evo"):
                    add_to_x(b, int(name[3]))
                elif name.startswith("odo"):
                    add_to_x(b, int(name[3]))
                elif name.startswith("down") and ch["last"]:
                    add_to_x(b, int(name.split("_")[1]))
                elif name.startswith("up"):
                    l, j, v = int(name[2]), int(name[4:]), int(name[3] == "v")
                    dst = (cg, cv)[v][j % 2]
                    dve.wait_ge(S["conv_init"], 22 * l + 2 * j + v + 1)
                    for tap in (1, 0):
                        d = 2 - tap
                        for i in range(2):
                            t = (44 * l + 22 * v + 2 * j + i) * 4
                            ins = dve.scalar_tensor_tensor(out=dst[:, i, d:], in0=ps[b][:, i, 0:TOK - d],
                                                           scalar=col("conv", t + tap, 1), in1=dst[:, i, d:],
                                                           op0=ALU.mult, op1=ALU.add)
                        if tap:
                            link(ins)
                    ins.then_inc(S["conv_done"], 1)
                elif name.startswith("uk"):
                    for i in range(2):
                        for half in range(2):
                            ins = dve.tensor_copy(MK[0:64, 4 * i + half:4 * i + 4:2, :],
                                                  ps[bank_of(ch, i)][64 * half:64 * half + 64])
                        ins.then_inc(S["k_nope"], 1)
                elif name.startswith("pp"):
                    l, i2 = int(name[2]), int(name[-1])
                    dve.wait_ge(S["gates"], 2 * l + 1)
                    for i in range(2):
                        p = 2 * i2 + i
                        dve.tensor_tensor(h[:, 2 * p:2 * p + 2, :], ps[bank_of(ch, i)][:], za[:, 2 * p:2 * p + 2, :],
                                          ALU.mult).then_inc(S["gated_a"], 1)
                elif name.startswith("pa"):
                    l, i2 = int(name[2]), int(name[-1])
                    dve.wait_ge(S["gates"], 2 * l + 2)
                    dve.wait_ge(S["gated_a"], 4 * l + 4)
                    for i in range(2):
                        p = 2 * i2 + i
                        hp_ = h[:, 2 * p:2 * p + 2, :]
                        zp = zb[:, 2 * p:2 * p + 2, :]
                        link(dve.tensor_tensor(zp, ps[bank_of(ch, i)][:], zp, ALU.mult))
                        dve.tensor_tensor(hp_, hp_, zp, ALU.add).then_inc(S["merged"], 1)
                    low_upto(n + SPLIT)
                    for i in range(2):
                        operand_low(f"merged{l}", 2 * i2 + i)
                elif name.startswith("wo"):
                    l = int(name[2])
                    add_to_x(b, int(name[-1]), mod[:, l, 16:24])
                elif name.startswith("fb") and ch["last"]:
                    l = int(name[2])
                    add_to_x(b, int(name.split("_")[1]), mod[:, l, 40:48])
                low_upto(n + SPLIT)

            def norm(i):
                if i < 4:
                    g = col("norm_mix" if i % 2 == 0 else "norm_ffn", 8 * (i // 2), 8)
                    shift = None
                elif i < 8:
                    l, which = (i - 4) // 2, i % 2
                    g = gmod[:, l, which, :]
                    shift = mod[:, l, 24 * which:24 * which + 8]
                else:
                    g, shift = col("final_g"), None
                fill = {0: "n0", 1: "n1", 2: "n2", 3: "n3", 4: "n4", 5: "n5", 6: "n6", 7: "n7"}.get(i)
                dve.wait_ge(S["rstd_ready"], i + 1)
                for p in range(4):
                    for k in (2 * p, 2 * p + 1):
                        ins = dve.scalar_tensor_tensor(out=h[:, k, :], in0=x[:, k, :], scalar=g[:, k:k + 1], in1=rn[:],
                                                       op0=ALU.mult, op1=ALU.mult)
                    if shift is not None:
                        link(ins)
                        for k in (2 * p, 2 * p + 1):
                            ins = dve.tensor_scalar(h[:, k, :], h[:, k, :], shift[:, k:k + 1], None, ALU.add)
                    ins.then_inc(S["normed"], 1)
                    if p and fill:
                        operand_low(fill, p - 1)
                if fill:
                    operand_low(fill, 3)

            def trig(_):
                magic = 12582912.0
                dve.wait_ge(S["pos_in"], 16)
                dve.wait_ge(S["consts_in"], 16)
                link(dve.tensor_copy(ang[:], posi[:]))
                link(dve.tensor_scalar(ang[:], ang[:], col("inv_freq"), None, ALU.mult))
                link(dve.tensor_scalar(turn[:], ang[:], 1.0 / (2 * np.pi), None, ALU.mult))
                link(dve.tensor_scalar(turn[:], turn[:], magic, None, ALU.add))
                link(dve.tensor_scalar(turn[:], turn[:], -magic, None, ALU.add))
                for part in TWO_PI_PARTS:
                    link(dve.scalar_tensor_tensor(out=ang[:], in0=turn[:], scalar=-part, in1=ang[:], op0=ALU.mult,
                                                  op1=ALU.add))
                lim = 3.1415925
                link(dve.tensor_scalar(turn[:], ang[:], float(np.pi / 2), None, ALU.add))
                link(dve.tensor_scalar(rn[:], turn[:], float(np.pi), -2 * float(np.pi), ALU.is_gt, ALU.mult))
                link(dve.tensor_tensor(turn[:], turn[:], rn[:], ALU.add))
                link(dve.tensor_scalar(turn[:], turn[:], lim, -lim, ALU.min, ALU.max))
                dve.tensor_scalar(ang[:], ang[:], lim, -lim, ALU.min, ALU.max).then_inc(S["trig_angle"], 1)

            def lam(_):
                dve.wait_ge(S["params_in"], 16)
                v = col("lam").rearrange("p (a b) -> p a b", a=4)
                lt = lamt[:, 0:128].rearrange("p (a b) -> p a b", a=2)
                link(dve.tensor_tensor(lt, v[:, 0::2, :], v[:, 1::2, :], ALU.mult))
                dve.reduce_sum(small[:, 2:4], lt, AX.X).then_inc(S["lam_sums"], 1)
                dve.wait_ge(S["lam_exp"], 1)
                link(dve.tensor_tensor(small[:, 6:7], small[:, 5:6], small[:, 4:5], ALU.subtract))
                link(dve.tensor_scalar(gain8, col("diff_gain"), 1.0 - LAMBDA_INIT, None, ALU.mult))
                link(dve.tensor_scalar(neglam, small[:, 6:7], -LAMBDA_INIT, None, ALU.add))

            def la_(_):
                dve.wait_ge(S["la_log"], 1)
                link(dve.scalar_tensor_tensor(out=la[:], in0=la[:], scalar=0.0, in1=ebl[:], op0=ALU.min,
                                              op1=ALU.subtract))
                for b in range(2):
                    for cc in range(4):
                        ck = slice(64 * cc, 64 * cc + 64)
                        ins = dve.tensor_tensor_scan(out=bc[:, b, ck], data0=col("ones", 0, 64), data1=la[:, b, ck],
                                                     initial=0.0, op0=ALU.mult, op1=ALU.add)
                link(ins)
                b4 = bc[:].rearrange("p b (c t) -> p (b c) t", c=4)
                dve.tensor_tensor(ebl[:].rearrange("p b (c t) -> p (b c) t", c=4), b4[:, :, 63:64].to_broadcast([P, 8, 64]),
                                  b4, ALU.subtract).then_inc(S["la_diff"], 1)

            def la_exps(_):
                dve.wait_ge(S["gate_exps"], 3)
                for half in range(2):
                    e4 = eb[64 * half:64 * half + 64].rearrange("p b (c t) -> p b c t", c=4)
                    ins = dve.tensor_copy(dec[:, half::2, :], e4[:, :, :, 63])
                link(ins)

            def unit(u):
                dve.wait_ge(S["unit_rstd"], u + 1)
                if u < 4:
                    hp, k = u // 2, u % 2
                    for half in range(2):
                        r = slice(64 * half, 64 * half + 64)
                        ins = dve.scalar_tensor_tensor(out=(Qd, Kd)[k][:, half, 2 * hp:2 * hp + 2, :],
                                                       in0=ps[bank_of(BY[("bq0", "bk0", "bq1", "bk1")[u]])][r],
                                                       scalar=col(("dq_gain", "dk_gain")[k])[r], in1=rb[u % 2][r],
                                                       op0=ALU.mult, op1=ALU.mult)
                    ins.then_inc(S["unit_normed"], 1)
                elif u < 8:
                    p = {5: 0, 6: 1, 4: 2, 7: 3}[u]
                    dve.scalar_tensor_tensor(out=h[:, 2 * p:2 * p + 2, :], in0=ps[OB][:],
                                             scalar=col("gla_gain") if p < 2 else gain8, in1=rb[u % 2][:],
                                             op0=ALU.mult, op1=ALU.mult).then_inc(S["unit_normed"], 1)
                else:
                    hp, g, k = (u - 8) // 6, (u - 8) % 6 // 2, u % 2
                    dve.scalar_tensor_tensor(out=(dq, dk)[k][hp][g][:], in0=ps[bank_of(BY[f"od{hp}{g}{k}"])][:],
                                             scalar=col(("od_q_gain", "od_k_gain")[k]), in1=rb[u % 2][:],
                                             op0=ALU.mult, op1=ALU.mult).then_inc(S["unit_normed"], 1)

            def gla_att(_):
                dve.wait_ge(S["att_zero"], 1)
                for i in range(2):
                    dve.wait_ge(S["att_done"], i + 1)
                    mask = col("gla_mask").bitcast(U32).rearrange("p (a b) -> p a b", a=1).to_broadcast([P, 4, P])
                    dve.copy_predicated(out=att[:, 2 * i:2 * i + 2].rearrange("p a t b -> p (a t) b"), mask=mask,
                                        data=ps[(SB0, SB1)[i]][:].rearrange("p a (t b) -> p (a t) b", t=2))\
                        .then_inc(S["att_masked"], 1)

            def gla_kv(_):
                for cc in range(3):
                    dve.wait_ge(S["kv_done"], cc + 1)
                    kv = ps[TB][0:64].rearrange("p a (t b) -> p (a t) b", t=2)
                    if cc == 0:
                        dve.tensor_copy(st[0][:], kv).then_inc(S["state_ready"], 1)
                    else:
                        dve.wait_ge(S["state_ready"], cc)
                        link(dve.tensor_tensor(st[cc][:], st[cc - 1][:], dec[:, :, cc:cc + 1].to_broadcast([64, 4, P]),
                                               ALU.mult))
                        dve.tensor_tensor(st[cc][:], kv, st[cc][:], ALU.add).then_inc(S["state_ready"], 1)

            def ag_silu(_):
                dve.wait_ge(S["unit_normed"], GLA_U[1] + 1)
                dve.wait_ge(S["silu_ag"], 3)
                for p in range(2):
                    hp_ = h[:, 2 * p:2 * p + 2, :]
                    dve.tensor_tensor(hp_, hp_, sg[:, 2 * p:2 * p + 2, :], ALU.mult).then_inc(S["mix_ready"], 1)
                for p in range(2):
                    operand_low("mix0", p)

            def diff_r(i):
                unit(DIFF_U[i])
                if i == 1:
                    for p in (2, 3):
                        operand_low("mix0", p)

            def diff_s(u):
                qt = u % 2
                nk = P * (qt + 1)
                S_ = Sb[u % 2][:, :, 0:nk]
                m = col("causal")[:, TOK - nk:TOK].rearrange("p (a b) -> p a b", a=1).to_broadcast([P, 2, nk])
                dve.wait_ge(S["diff_scores"], u + 1)
                link(dve.tensor_tensor(S_, ps[(SB0, SB1)[u % 2]][:, :, 0:nk], m, ALU.add))
                link(dve.reduce_max(stat[:, u % 2, 0:2], S_, AX.X))
                dve.tensor_scalar(stat[:, u % 2, 2:4], stat[:, u % 2, 0:2], -0.125, None, ALU.mult)\
                    .then_inc(S["diff_max"], 1)

            def diff_w(u):
                nk = P * (u % 2 + 1)
                s_ = stat[:, u % 2]
                dve.wait_ge(S["diff_exp"], u + 1)
                link(dve.reciprocal(s_[:, 6:8], s_[:, 4:6]))
                link(dve.tensor_scalar(s_[:, 8:9], s_[:, 7:8], neglam, None, ALU.mult))
                if u >= 2:
                    dve.wait_ge(S["diff_turned"], u - 1)
                link(dve.tensor_scalar(W[u % 2][:, 0:nk], Sb[u % 2][:, 0, 0:nk], s_[:, 6:7], None, ALU.mult))
                dve.scalar_tensor_tensor(out=W[u % 2][:, 0:nk], in0=Sb[u % 2][:, 1, 0:nk], scalar=s_[:, 8:9],
                                         in1=W[u % 2][:, 0:nk], op0=ALU.mult, op1=ALU.add).then_inc(S["diff_w"], 1)

            def dil_s(u):
                qt = u % 2
                nk = P * (qt + 1)
                m = col(f"dil{qt}").rearrange("p (g k) -> p g k", g=3)
                S_ = DS[u % 2][:, 0:3 * nk].rearrange("p (g k) -> p g k", g=3)
                dve.wait_ge(S["dil_scores"], u + 1)
                if u >= 2:
                    dve.wait_ge(S["dil_turned"], 3 * (u // 2) - 2 if qt == 0 else 3 * (u // 2))
                dve.tensor_tensor(S_[:, 0:2, :], ps[SB0][:, :, 0:nk], m[:, 0:2, :], ALU.add)
                link(dve.tensor_tensor(S_[:, 2, :], ps[SB1][:, 0, 0:nk], m[:, 2, :], ALU.add))
                link(dve.reduce_max(dstat[:, u % 2, 0:1], DS[u % 2][:, 0:3 * nk], AX.X))
                dve.tensor_scalar(dstat[:, u % 2, 1:2], dstat[:, u % 2, 0:1], -(128 ** -0.5), None, ALU.mult)\
                    .then_inc(S["dil_max"], 1)

            def dil_w(u):
                nk = P * (u % 2 + 1)
                dve.wait_ge(S["dil_exp"], u + 1)
                link(dve.reciprocal(dstat[:, u % 2, 3:4], dstat[:, u % 2, 2:3]))
                dve.tensor_scalar(DS[u % 2][:, 0:3 * nk], DS[u % 2][:, 0:3 * nk], dstat[:, u % 2, 3:4], None, ALU.mult)\
                    .then_inc(S["dil_w"], 1)

            def dil_t(u):
                dil_w(u)

            def mix1(hp):
                operand_low("mix1", hp)

            def ada_(a):
                l, seg = a
                dve.wait_ge(S["ada_sum"], 6 * l + seg + 1)
                dve.tensor_tensor(mod[:, l, 8 * seg:8 * seg + 8], ps[NB][:, 0, 0:8], col("b_ada", 48 * l + 8 * seg, 8),
                                  ALU.add).then_inc(S["ada_mod"], 1)
                if seg == 5:
                    dve.wait_ge(S["ada_mod"], 6 * l + 6)
                    for which in range(2):
                        link(dve.scalar_tensor_tensor(out=gmod[:, l, which, :],
                                                      in0=mod[:, l, 24 * which + 8:24 * which + 16], scalar=1.0,
                                                      in1=col(("ln1", "ln2")[which], 8 * l, 8), op0=ALU.add,
                                                      op1=ALU.mult))

            def krot(l):
                dve.wait_ge(S["krot_done"], l + 1)
                dve.wait_ge(S["trig_done"], 1)
                link(dve.tensor_tensor(krs[:], ps[TB][0:32, 0, :], sinT[0:32], ALU.mult))
                link(dve.tensor_tensor(kr[:], kr[:], cosT[0:32], ALU.mult))
                dve.tensor_tensor(kr[:], kr[:], krs[:], ALU.add).then_inc(S["krope_done"], 1)

            def wide(a):
                l, which = a
                i = 2 * l + which
                dve.wait_ge(S["wide_rstd"], i + 1)
                if which == 0:
                    for k in range(3):
                        o = ps[bank_of(BY[f"cq{l}a"])][:, k, :] if k < 2 else ps[bank_of(BY[f"cq{l}b"])][:, 0, :]
                        ins = dve.scalar_tensor_tensor(out=h[:, k, :], in0=o, scalar=col("q_norm", 3 * l + k, 1),
                                                       in1=rn[:], op0=ALU.mult, op1=ALU.mult)
                    ins.then_inc(S["wide_normed"], 1)
                    dve.wait_ge(S["cq_high"], l + 1)
                    dve.tensor_tensor(SQL[:, 0:3, :], h[:, 0:3, :], SQH[:, 0:3, :], ALU.subtract)\
                        .then_inc(S["cq_low"], 1)
                else:
                    for k in range(2):
                        ins = dve.scalar_tensor_tensor(out=h[:, 3 + k, :], in0=ps[bank_of(BY[f"ckv{l}"])][:, k, :],
                                                       scalar=col("kv_norm", 2 * l + k, 1), in1=rn[:],
                                                       op0=ALU.mult, op1=ALU.mult)
                    ins.then_inc(S["wide_normed"], 1)
                    dve.wait_ge(S["ckv_high"], l + 1)
                    dve.tensor_tensor(SCL[:, 0:2, :], h[:, 3:5, :], SCH[:, 0:2, :], ALU.subtract)\
                        .then_inc(S["ckv_low"], 1)

            def qrot(l):
                dve.wait_ge(S["qrot_done"], l + 1)
                bc2 = lambda t: t[:].rearrange("p (a b) -> p a b", a=1).to_broadcast([P, 2, TOK])
                dve.tensor_tensor(qs[:], ps[TB][:], bc2(sinT), ALU.mult).then_inc(S["q_rope"], 1)
                link(dve.tensor_tensor(qr[:], qr[:], bc2(cosT), ALU.mult))
                dve.wait_ge(S["q_rope"], 2 * l + 1)
                for i in range(4):
                    r = slice(32 * i, 32 * i + 32)
                    ins = dve.tensor_tensor(MQ[64:96, i::4, :], qr[r], qs[r], ALU.add)
                ins.then_inc(S["q_rope"], 1)

            def pool_split(l):
                dve.wait_ge(S["pooled_high"], 2 * l + 1)
                dve.tensor_tensor(SQL[:, 0::2, :], p1[:, 0::2, PAD:], SQH[:, 0::2, :], ALU.subtract)\
                    .then_inc(S["pooled_low"], 1)
                dve.wait_ge(S["pooled_high"], 2 * l + 2)
                dve.tensor_tensor(SQL[:, 1::2, :], p2[:, 1::2, PAD:], SQH[:, 1::2, :], ALU.subtract)\
                    .then_inc(S["pooled_low"], 1)

            def y_(l):
                for i in range(2):
                    dve.wait_ge(S["y_high"], 2 * l + i + 1)
                    dve.tensor_tensor(SQL[:, 2 * i:2 * i + 2, :], p1[:, 2 * i:2 * i + 2, PAD:],
                                      SQH[:, 2 * i:2 * i + 2, :], ALU.subtract).then_inc(S["y_low"], 1)

            def mla_s(a):
                l, u = a
                U, nk = 16 * l + u, P * (u % 2 + 1)
                S_ = MS[u % 2][:, 0:nk]
                dve.wait_ge(S["mla_scores"], U + 1)
                if U >= 2:
                    dve.wait_ge(S["mla_turned"], U - 1)
                link(dve.tensor_tensor(S_, ps[(SB0, SB1)[u % 2]][:, 0, 0:nk], col("causal")[:, TOK - nk:TOK], ALU.add))
                link(dve.reduce_max(mstat[:, u % 2, 0:1], S_, AX.X))
                dve.tensor_scalar(mstat[:, u % 2, 1:2], mstat[:, u % 2, 0:1], -(96 ** -0.5), None, ALU.mult)\
                    .then_inc(S["mla_max"], 1)

            def mla_t(a):
                l, u = a
                U, nk = 16 * l + u, P * (u % 2 + 1)
                S_ = MS[u % 2][:, 0:nk]
                dve.wait_ge(S["mla_exp"], U + 1)
                link(dve.reciprocal(mstat[:, u % 2, 3:4], mstat[:, u % 2, 2:3]))
                dve.tensor_scalar(S_, S_, mstat[:, u % 2, 3:4], None, ALU.mult).then_inc(S["mla_w"], 1)
                if u % 8 == 7:
                    i = u // 8
                    dve.wait_ge(S["att_high"], 2 * l + i + 1)
                    dve.tensor_tensor(SCL[:, 2 * i:2 * i + 2, :], ps[OB][:], SCH[:, 2 * i:2 * i + 2, :], ALU.subtract)\
                        .then_inc(S["att_low"], 1)

            def act2(a):
                l, p = a
                dve.wait_ge(S["relu_done"], 16 * l + p + 1)
                dve.tensor_tensor(rl[p % 2][:], rl[p % 2][:], rl[p % 2][:], ALU.mult).then_inc(S["sq_done"], 1)
                dve.wait_ge(S["act2_high"], 16 * l + p + 1)
                dve.tensor_tensor(BL[:, 2 * p:2 * p + 2, :], rl[p % 2][:], BH[:, 2 * p:2 * p + 2, :], ALU.subtract)\
                    .then_inc(S["act2_low"], 1)

            low_upto(SPLIT - 1)
            stages = dict(chunk=chunk, norm=norm, unit=unit, trig=trig, lam=lam, la=la_, la_exps=la_exps, gla_att=gla_att,
                          gla_kv=gla_kv, ag_silu=ag_silu, diff_s=diff_s, diff_t=diff_w, diff_r=diff_r, dil_s=dil_s,
                          dil_t=dil_t, mix1=mix1, ada=ada_, krot=krot, wide=wide, qrot=qrot, pool_split=pool_split, y=y_,
                          mla_s=mla_s, mla_t=mla_t, act2=act2, gla_r=lambda hp: unit(GLA_U[hp]))
            for stage, i in order:
                if stage in stages:
                    stages[stage](i)

        @block.gpsimd
        def _(pool):
            chain = [0]

            def link(ins):
                chain[0] += 1
                ins.then_inc(S["pool_chain"], 1)
                pool.wait_ge(S["pool_chain"], chain[0])

            ada_in = (S["ada_in0"], S["ada_in1"])
            ada_at = [0]

            def ada_load(a):
                pool.dma_start(adaw[a % 2][:].rearrange("p a b -> p (a b)"),
                               ada[a * P * 2048:(a + 1) * P * 2048].rearrange("(p w) -> p w", p=P))\
                    .then_inc(ada_in[a % 2], 16)

            def ada_piece(l):
                a = ada_at[0]
                seg, part = a // 4 - 6 * l, a % 4
                if a >= 24 * (l + 1):
                    return
                pool.wait_ge(ada_in[a % 2], 16 * (a // 2 + 1))
                acc = adas[seg % 2]
                if part == 0 and seg + 6 * l >= 2:
                    pool.wait_ge(S["ada_sum"], seg + 6 * l - 1)
                for i in range(2):
                    k = 2 * part + i
                    w, scale = adaw[a % 2][:, i, :], cact[:, k:k + 1]
                    if k == 0:
                        link(pool.tensor_scalar(acc[:], w, scale, None, ALU.mult))
                        continue
                    link(pool.tensor_scalar(w, w, scale, None, ALU.mult))
                    if k < 7:
                        link(pool.tensor_tensor(acc[:], w, acc[:], ALU.add))
                    else:
                        pool.tensor_tensor(acc[:], w, acc[:], ALU.add).then_inc(S["ada_acc"], 1)
                        pool.wait_ge(S["ada_acc"], 6 * l + seg + 1)
                if a + 2 < 24 * (l + 1):
                    ada_load(a + 2)
                ada_at[0] += 1

            def ffn_in(l):
                pool.wait_ge(S["products_done"], BY[("evo3", "odo3")[l]]["n"] + 1)
                pool.wait_ge(S["c_silu"], 1)
                ada_load(24 * l)
                ada_load(24 * l + 1)

            def silu(a):
                l, j = a
                pool.wait_ge(S["silu_done"], 11 * l + j + 1)
                pool.wait_ge(S["conv_done"], 22 * l + 2 * j + 2)
                pool.tensor_tensor(cg[j % 2][:], cg[j % 2][:], cv[j % 2][:], ALU.mult).then_inc(S["act_mul"], 1)
                ada_piece(l)

            def act_(a):
                l, j = a
                pool.wait_ge(S["act_high"], 11 * l + j + 1)
                pool.tensor_tensor(AL[:, 2 * j:2 * j + 2, :], cg[j % 2][:], AH[:, 2 * j:2 * j + 2, :], ALU.subtract)\
                    .then_inc(S["act_low"], 1)
                ada_piece(l)
                if j == 10:
                    ada_piece(l)
                    ada_piece(l)

            def zero_pads(l):
                pool.wait_ge(S["products_done"], BY[f"cq{l}a"]["n"] + 1)
                pool.memset(up[:, :, 0:PAD], 0.0)
                pool.memset(p1[:, :, 0:PAD], 0.0)
                link(pool.memset(p2[:, :, 0:PAD], 0.0))

            def krot(l):
                pool.wait_ge(S["krope_done"], l + 1)
                zero_pads(l)
                src = kr[:].rearrange("p (a b) -> p a b", a=1).to_broadcast([32, 8, TOK])
                pool.tensor_copy(MK[64:96], src).then_inc(S["kfull"], 1)

            def pool_(l):
                pool.wait_ge(S["kfull"], l + 1)
                pool.wait_ge(S["u_ready"], 2 * l + 2)
                for i, (a, b) in enumerate(((up, p1), (p1, p2), (p2, p1), (p1, p2))):
                    s_ = 1 << i
                    link(pool.tensor_tensor(b[:, i:, PAD:], a[:, i:, PAD:], a[:, i:, PAD - s_:PAD + TOK - s_], ALU.add))
                for j, buf in enumerate((p1, p2)):
                    for g in (j, j + 2):
                        w = 2 << g
                        link(pool.tensor_tensor(buf[:, g, PAD:PAD + 16], buf[:, g, PAD:PAD + 16],
                                                col("cnt", 16 * g, 16), ALU.mult))
                        link(pool.tensor_scalar(buf[:, g, PAD + 16:], buf[:, g, PAD + 16:], 1.0 / w, None, ALU.mult))
                    pool.tensor_tensor(buf[:, j::2, PAD:], buf[:, j::2, PAD:], up[:, j::2, PAD:], ALU.subtract)\
                        .then_inc(S["pooled"], 1)

            pool.wait_ge(S["consts_in"], 16)
            pool.memset(att[:], 0.0).then_inc(S["att_zero"], 1)
            stages = dict(ffn_in=ffn_in, silu=silu, act=act_, krot=krot, pool=pool_)
            for stage, i in order:
                if stage in stages:
                    stages[stage](i)


LAMBDA_INIT = 0.2


def shape_constants():
    q, k = np.arange(P)[:, None], np.arange(TOK)[None, :]
    one = np.float32(1.0)
    c = {"ident": np.eye(P), "ones": np.ones((P, P)), "ones64": np.kron(np.eye(2), np.ones((64, 64)))}
    c["causal"] = np.where(k <= q + P, 0.0, NEG)
    for qt in range(2):
        nk = P * (qt + 1)
        t, j = q + P * qt, np.arange(nk)[None, :]
        m = [(t - j >= 0) & ((t - j) % d == 0) & (t - j <= w) for w, d in ((128, 1), (512, 4), (2048, 16))]
        c[f"dil{qt}"] = np.concatenate([np.where(v, 0.0, NEG) for v in m], 1)
    j, i = np.arange(P)[:, None], np.arange(P)[None, :]
    c["gla_mask"] = np.where((j // 64 == i // 64) & (j <= i), 1.0, 0.0)
    rot = np.zeros((P, P))
    for m in range(P):
        rot[m + 16 if m % 32 < 16 else m - 16, m] = -1.0 if m % 32 < 16 else 1.0
    c["rot"] = rot
    f = np.float32(10000.0) ** (-np.arange(0, 32, 2, dtype=np.float32) / np.float32(32))
    c["inv_freq"] = np.tile(f, 8)[:, None]
    c["cnt"] = np.tile(np.concatenate([1.0 / np.minimum(np.arange(16) + 1, 2 << g) for g in range(4)])[None], (P, 1))
    c["eps"] = np.full((P, 1), EPS)
    where, sizes = columns()
    a = np.zeros((P, sizes["consts"]), np.float32)
    for name, v in c.items():
        _, at, n = where[name]
        a[:, at:at + n] = v
    return a


def by_feature(v):
    v = np.asarray(v)
    return v.reshape(-1, P).T


def lay_params(i):
    where, sizes = columns()
    a = np.zeros((P, sizes["params"]), np.float32)

    def put(name, v, at=0):
        _, c0, n = where[name]
        a[:v.shape[0], c0 + at:c0 + at + v.shape[1]] = v

    for name, src in (("norm_mix", "norm_mix"), ("norm_ffn", "norm_ffn"), ("b_a", "ev_b_a"),
                      ("gla_gain", "ev_gla_gain"), ("diff_gain", "ev_diff_gain"), ("od_q_gain", "od_q_gain"),
                      ("od_k_gain", "od_k_gain"), ("ln1", "ln1_g_2"), ("ln2", "ln2_g_2"), ("b_ada", "b_ada_2"),
                      ("q_norm", "q_norm_g_2"), ("kv_norm", "kv_norm_g_2"), ("pool_scale", "pool_scale_2"),
                      ("final_g", "final_g_2"), ("c", "c_2")):
        put(name, by_feature(i[src]))
    for name, src in (("dq_gain", "ev_dq_gain"), ("dk_gain", "ev_dk_gain")):
        g = np.asarray(i[src]).reshape(64, 1)
        put(name, np.concatenate([g, g], 0))
    cw, cb = np.asarray(i["ffn_conv_w"]), np.asarray(i["ffn_conv_b"])
    taps = np.stack([cw[:, 0, 0], cw[:, 1, 0], cw[:, 2, 0], cb], 1)
    put("conv", taps.reshape(2, 4, 44, P).transpose(3, 0, 2, 1).reshape(P, -1))
    lam = np.concatenate([np.asarray(i[k]).reshape(-1) for k in ("ev_lq1", "ev_lk1", "ev_lq2", "ev_lk2")])
    put("lam", np.repeat(lam[None], P, 0))
    put("w_a2", np.asarray(i["ev_w_a2"])[0])
    put("w_ar", np.asarray(i["ev_w_in"])[0, :, 1536:1552].reshape(KB, P, 16).transpose(1, 0, 2).reshape(P, -1))
    for l in range(2):
        put("w_kr", np.asarray(i["w_in_2"])[l, :, 1152:1184].reshape(KB, P, 32).transpose(1, 0, 2).reshape(P, -1),
            256 * l)
    return a


def lay_stream(i):
    chunks, total = linear_chunks()
    out = np.zeros(P * total, np.float32)
    for ch in chunks:
        name, l = ch["src"]
        w = np.asarray(i[name])[l]
        if ch["diag"]:
            part = w.transpose(1, 0, 2).reshape(P, -1)
        else:
            w = w.reshape(w.shape[0], -1)[ch["rows"][0] * P:(ch["rows"][-1] + 1) * P][:, ch["cols"]]
            part = w.reshape(len(ch["rows"]), P, -1).transpose(1, 0, 2).reshape(P, -1)
        out[P * ch["at"]:P * (ch["at"] + ch["width"])] = part.reshape(-1)
    return out


def kernel(**inputs):
    import concourse.bacc as bacc
    from concourse.bass_utils import run_bass_kernel_spmd

    i = inputs
    _, total = linear_chunks()
    xT = np.ascontiguousarray(np.asarray(i["x"])[0].T.reshape(KB, P, TOK).transpose(1, 0, 2))
    wa = np.asarray(i["w_ada_2"]).reshape(2, 4, 2, P, 6, D)
    arrays = {
        "xT": xT, "stream": lay_stream(i), "ada": np.ascontiguousarray(wa.transpose(0, 4, 1, 3, 2, 5)).reshape(-1),
        "consts_d": shape_constants(), "params_d": lay_params(i),
        "positions": np.ascontiguousarray(np.asarray(i["positions_2"]).astype(np.int32)),
    }
    nc = bacc.Bacc("TRN2", target_bir_lowering=False, num_devices=1)
    args = {n: nc.dram_tensor(n, a.shape, mybir.dt.from_np(a.dtype), kind="ExternalInput").ap()
            for n, a in arrays.items()}
    out = nc.dram_tensor("out", (P, KB, TOK), F32, kind="ExternalOutput").ap()
    build(nc, out=out, **args)
    r = run_bass_kernel_spmd(nc, [arrays], core_ids=[0])
    y = r.results[0]["out"]
    return np.ascontiguousarray(y.transpose(1, 0, 2).reshape(D, TOK).T)[None]
```

```python
from contextlib import ExitStack

import numpy as np
import concourse.bass as bass
from concourse import mybir

P = 128
TOK = 256
D = 1024
KB = D // P
FF1, FF2 = 2816, 4096
EPS = 1e-6
F32 = mybir.dt.float32
F32R = mybir.dt.float32r
I32 = mybir.dt.int32
U32 = mybir.dt.uint32
ALU = mybir.AluOpType
ACT = mybir.ActivationFunctionType
AX = mybir.AxisListType
RAW, SPLIT, LIN, RELU = 3, 3, 3, 3
CHUNK = 2048
NEG = -1e30
EXP_LN = "natural_log_exp_and_others"
TWO_PI_PARTS = (6.28125, 0.0019302368164062500, 0.0000050703630862)


def linear_chunks():
    c = []

    def add(name, src, rows, cols, first=True, last=True, tm=False, diag=False, op="O", banks=None):
        ncols = len(cols)
        nb = max(1, ncols // 256) if not diag else 2
        c.append(dict(name=name, src=src, rows=list(rows), cols=cols, first=first, last=last, tm=tm,
                      diag=diag, op=op, banks=banks or nb, width=ncols * (1 if diag else len(rows))))

    def cols(a, n):
        return list(range(a, a + n))

    k8 = range(8)
    o = {"aq": 0, "ak": 256, "av": 512, "ag": 1024, "ar": 1536, "bq": 1552, "bk": 2064, "bv": 2576}
    w = ("ev_w_in", 0)
    for name, base, tm in (("av0", o["av"], 1), ("bq0", o["bq"], 0), ("bk0", o["bk"], 0), ("bv0", o["bv"], 1),
                           ("aq", o["aq"], 0), ("ak", o["ak"], 0), ("bq1", o["bq"] + 256, 0),
                           ("bk1", o["bk"] + 256, 0), ("av1", o["av"] + 256, 1), ("bv1", o["bv"] + 256, 1),
                           ("ag0", o["ag"], 0), ("ag1", o["ag"] + 256, 0)):
        add(name, w, k8, cols(base, 256), tm=bool(tm))

    def out_proj(tag, src):
        for p in range(4):
            add(f"{tag}{p}", src, k8, cols(256 * p, 256))

    def conv_ffn(l):
        for j in range(11):
            add(f"up{l}g{j}", ("ffn_w_up", l), k8, cols(256 * j, 256))
            add(f"up{l}v{j}", ("ffn_w_up", l), k8, cols(FF1 + 256 * j, 256))
        for p in range(4):
            for i, r in enumerate((range(0, 8), range(8, 16), range(16, 22))):
                add(f"down{l}_{p}_{i}", ("ffn_w_down", l), r, cols(256 * p, 256), i == 0, i == 2, op="A")

    out_proj("evo", ("ev_w_out", 0))
    conv_ffn(0)
    for hp in range(2):
        for g in range(3):
            for s in range(3):
                add(f"od{hp}{g}{s}", ("od_w_in", 0), k8, cols(g * 1536 + s * 512 + hp * 256, 256), tm=s == 2)
    for p in range(4):
        add(f"odo{p}", ("od_w_out", 0), range(4), cols(256 * p, 256))
    conv_ffn(1)
    nope = [h * 96 + i for h in range(8) for i in range(64)]
    rope = [h * 96 + 64 + i for h in range(8) for i in range(32)]
    for l in range(2):
        w = ("w_in_2", l)
        add(f"cq{l}a", w, k8, cols(512, 256))
        add(f"cq{l}b", w, k8, cols(768, 128))
        add(f"ckv{l}", w, k8, cols(896, 256))
        add(f"u{l}0", w, k8, cols(0, 256))
        add(f"u{l}1", w, k8, cols(256, 256))
        add(f"uqn{l}", ("w_uq_2", l), range(3), nope, op="Q")
        add(f"uqr{l}", ("w_uq_2", l), range(3), rope, op="Q")
        add(f"uk{l}", ("w_uk_2", l), range(2), cols(0, 512), op="C")
        add(f"uv{l}", ("w_uv_2", l), range(2), cols(0, 512), tm=True, op="C")
        for p in range(4):
            add(f"gz{l}a{p}", w, k8, cols(1184 + 256 * p, 256))
        add(f"wp{l}", ("w_pool_2", l), range(4), cols(0, 512), diag=True, op="Q")
        for p in range(4):
            add(f"gz{l}b{p}", w, k8, cols(2208 + 256 * p, 256))
        for i in range(2):
            add(f"pp{l}_{i}", ("p_pool_2", l), range(4), cols(512 * i, 512), op="Q")
        for i in range(2):
            add(f"pa{l}_{i}", ("p_attn_2", l), range(4), cols(512 * i, 512), op="C")
        out_proj(f"wo{l}_", ("w_out_2", l))
        for p in range(16):
            add(f"fa{l}_{p}", ("w_ff1_2", l), k8, cols(256 * p, 256))
        for p in range(4):
            for i in range(4):
                add(f"fb{l}_{p}_{i}", ("w_ff2_2", l), range(8 * i, 8 * i + 8), cols(256 * p, 256),
                    i == 0, i == 3, op="A")
    at, bank = 0, 0
    for n, x in enumerate(c):
        x["n"], x["at"] = n, at
        at += x["width"]
        if x["first"]:
            x["bank"] = bank
            bank += x["banks"]
        else:
            x["bank"] = c[n - 1]["bank"]
    return c, at


LATE = {"consts": "dil0", "params": "od_q_gain"}


def columns():
    where = {}
    sizes = {"consts": 0, "params": 0}

    def put(kind, name, n):
        where[name] = (kind, sizes[kind], n)
        sizes[kind] += n

    for name, n in (("ones", 128), ("eps", 1), ("ident", 128), ("ones64", 128), ("gla_mask", 128), ("causal", 256),
                    ("inv_freq", 1), ("dil0", 384), ("dil1", 768), ("rot", 128), ("cnt", 64)):
        put("consts", name, n)
    for name, n in (("norm_mix", 16), ("norm_ffn", 16), ("b_a", 2), ("gla_gain", 1), ("dq_gain", 1),
                    ("dk_gain", 1), ("diff_gain", 1), ("lam", 256), ("w_ar", 128), ("w_a2", 256),
                    ("od_q_gain", 1), ("od_k_gain", 1), ("conv", 2 * 44 * 4), ("ln1", 16), ("ln2", 16),
                    ("b_ada", 96), ("q_norm", 6), ("kv_norm", 4), ("pool_scale", 8), ("final_g", 8), ("c", 8),
                    ("w_kr", 512)):
        put("params", name, n)
    return where, sizes


def build(nc, xT, stream, ada, consts_d, params_d, positions, out):
    CH, _ = linear_chunks()
    BY = {x["name"]: x for x in CH}
    NCH = len(CH)
    where, sizes = columns()
    ctx = ExitStack()
    with ctx:
        def sb(name, shape, dt=F32, stack=ctx):
            return stack.enter_context(nc.sbuf_tensor(name, shape, dt))

        def sem(name):
            return ctx.enter_context(nc.semaphore(name))

        consts = sb("consts", [P, sizes["consts"]])
        params = sb("params", [P, sizes["params"]])

        def col(name, a=0, n=None):
            kind, at, size = where[name]
            t = consts if kind == "consts" else params
            return t[:, at + a:at + a + (size - a if n is None else n)]

        raw = [sb(f"raw{i}", [P, CHUNK]) for i in range(RAW)]
        high = [sb(f"high{i}", [P, CHUNK], F32R) for i in range(SPLIT)]
        low = [sb(f"low{i}", [P, CHUNK], F32R) for i in range(SPLIT)]
        x = sb("x", [P, KB, TOK])
        h = sb("h", [P, KB, TOK])
        OH = sb("op_high", [P, KB, TOK], F32R)
        OL = sb("op_low", [P, KB, TOK], F32R)
        rn = sb("rn", [P, TOK])
        sq = [sb(f"sq{i}", [P, 2, TOK]) for i in range(2)]
        rb = [sb(f"rb{i}", [P, 2, TOK]) for i in range(2)]
        cosT = sb("cosT", [P, TOK])
        sinT = sb("sinT", [P, TOK])
        mod = sb("mod", [P, 2, 48])
        gmod = sb("gmod", [P, 2, 2, KB])
        cact = sb("cact", [P, KB])
        small = sb("small", [P, 64])
        neglam = small[:, 0:1]
        gain8 = small[:, 1:2]

        first = ExitStack()
        f = lambda n, s, d=F32: sb(n, s, d, first)
        posi = f("posi", [P, TOK], I32)
        ang = f("ang", [P, TOK])
        turn = f("turn", [P, TOK])
        ar = f("ar", [16, TOK])
        la = f("la", [P, 2, TOK])
        bc = f("bc", [P, 2, TOK])
        eb = f("eb", [P, 2, TOK])
        enb = f("enb", [P, 2, TOK])
        ebl = f("ebl", [P, 2, TOK])
        dec = f("dec", [64, 4, 4])
        qd = f("qd", [64, 4, TOK])
        kd = f("kd", [64, 4, TOK])
        keT = f("keT", [64, 3, 256])
        va = f("va", [P, 2, 512])
        va1 = f("va1", [64, 512])
        att = f("att", [P, 4, 2, 128])
        st = [f(f"st{i}", [64, 4, 128]) for i in range(3)]
        sg = f("sg", [P, 4, TOK])
        Qd = f("Qd", [64, 2, 4, TOK])
        Kd = f("Kd", [64, 2, 4, TOK])
        vb = f("vb", [P, 2, 512])
        Sb = [f(f"Sb{i}", [P, 2, TOK]) for i in range(2)]
        W = [f(f"W{i}", [P, TOK]) for i in range(2)]
        WT = [f(f"WT{i}", [P, TOK]) for i in range(2)]
        stat = f("stat", [P, 2, 12])
        lamt = f("lamt", [P, 136])
        first.close()

        adaln = ExitStack()
        adaw = [sb(f"adaw{i}", [P, 2, D], F32, adaln) for i in range(2)]
        adas = [sb(f"adas{i}", [P, D], F32, adaln) for i in range(2)]

        ffn = ExitStack()
        f = lambda n, s, d=F32: sb(n, s, d, ffn)
        AH = f("act_high", [P, 22, TOK], F32R)
        AL = f("act_low", [P, 22, TOK], F32R)
        cg = [f(f"gate{i}", [P, 2, TOK]) for i in range(2)]
        cv = [f(f"val{i}", [P, 2, TOK]) for i in range(2)]
        ffn.close()

        odd = ExitStack()
        f = lambda n, s, d=F32: sb(n, s, d, odd)
        dq = [[f(f"dq{b}{g}", [P, 2, TOK]) for g in range(3)] for b in range(2)]
        dk = [[f(f"dk{b}{g}", [P, 2, TOK]) for g in range(3)] for b in range(2)]
        dv = [[f(f"dv{b}{g}", [P, 2, TOK]) for g in range(3)] for b in range(2)]
        DS = [f(f"DS{i}", [P, 3 * TOK]) for i in range(2)]
        DT = [f(f"DT{i}", [P, 6, P]) for i in range(2)]
        dstat = f("dstat", [P, 2, 4])
        odd.close()
        adaln.close()

        mla = ExitStack()
        f = lambda n, s, d=F32: sb(n, s, d, mla)
        MQ = f("MQ", [96, 8, TOK])
        MK = f("MK", [96, 8, TOK])
        mv = f("mv", [P, 2, 512])
        qr = f("qr", [P, 2, TOK])
        qs = f("qs", [P, 2, TOK])
        kr = f("kr", [32, TOK])
        krs = f("krs", [32, TOK])
        SQH = f("smallq_high", [P, 4, TOK], F32R)
        SQL = f("smallq_low", [P, 4, TOK], F32R)
        SCH = f("smallc_high", [P, 4, TOK], F32R)
        SCL = f("smallc_low", [P, 4, TOK], F32R)
        PAD = 16
        up = f("up", [P, 4, PAD + TOK])
        p1 = f("p1", [P, 4, PAD + TOK])
        p2 = f("p2", [P, 4, PAD + TOK])
        za = f("za", [P, KB, TOK])
        zb = f("zb", [P, KB, TOK])
        MS = [f(f"MS{i}", [P, TOK]) for i in range(2)]
        MT = [f(f"MT{i}", [P, TOK]) for i in range(2)]
        mstat = f("mstat", [P, 2, 4])
        mla.close()

        ffn2 = ExitStack()
        f = lambda n, s, d=F32: sb(n, s, d, ffn2)
        BH = f("act2_high", [P, 32, TOK], F32R)
        BL = f("act2_low", [P, 32, TOK], F32R)
        rl = [f(f"relu{i}", [P, 2, TOK]) for i in range(RELU)]
        ffn2.close()

        ps = [ctx.enter_context(nc.psum_tensor(f"bank{i}", [P, 2, TOK], F32)) for i in range(8)]
        NB, SB0, SB1, TB, OB = 3, 4, 5, 6, 7

        raw_in = [sem(f"raw_in{i}") for i in range(RAW)]
        names = """consts_in params_in late_in x_in pos_in high_ready low_ready products_done
            trig_angle trig_done lam_sums lam_exp lam_done dve_chain act_chain pool_chain
            x_updated squares_ready sumsq_ready rstd_ready normed operand_high operand_low
            unit_squares unit_sums unit_rstd unit_normed
            ar_done ar_copied la_done la_biased la_log la_diff gate_exps va_ready gla_q gla_k ket_done
            ket_copied att_done att_zero att_masked kv_done state_ready gla_o_done vb_ready silu_ag
            diff_scores diff_max diff_exp diff_w diff_turned diff_copied diff_pv mix_ready
            conv_init conv_done silu_done act_mul act_high act_low c_silu ada_in0 ada_in1 ada_scaled ada_added ada_sum mod_ready
            dil_scores dil_max dil_exp dil_w dil_turned dil_copied dil_pv dv_ready dil_out
            pool_zero kr_done kr_copied krot_done krope_done kfull q_nope k_nope qr_copied qrot_done q_rope mv_ready
            wide_squares wide_sums wide_rstd wide_normed cq_high cq_low ckv_high ckv_low
            u_ready pooled pooled_high pooled_low y_ready y_high y_low gates_raw gates gated_a
            mla_scores mla_max mla_exp mla_w mla_turned mla_copied mla_pv att_high att_low merged
            relu_done sq_done act2_high act2_low stored""".split()
        S = {n: sem(n) for n in names}

        block = ctx.enter_context(nc.Block())

        FILLS = {}
        total = 0
        for name, pairs in (("n0", 4), ("mix0", 4), ("n1", 4), ("n2", 4), ("mix1", 2), ("n3", 4), ("n4", 4),
                            ("merged0", 4), ("n5", 4), ("n6", 4), ("merged1", 4), ("n7", 4)):
            FILLS[name] = total
            total += pairs

        order = []
        units = {"bq0": 0, "bk0": 1, "bq1": 2, "bk1": 3}
        DIFF_U, GLA_U, DIFF_QK = (4, 7), (5, 6), (1, 3)

        def c(name):
            order.append(("chunk", name))

        def st_(name, i=0):
            order.append((name, i))

        def sw(kind, *units_):
            for u in units_:
                st_(kind + "_s", u)
            for u in units_:
                st_(kind + "_w", u)

        def each(kind, *units_):
            for u in units_:
                st_(kind, u)

        def projection(names, i, between=()):
            pair = behind = 0
            for n, name in enumerate(names):
                c(name)
                if pair > behind:
                    st_("sumsq", (i, behind))
                    behind += 1
                if BY[name]["last"]:
                    st_("square", (i, pair))
                    pair += 1
                if n < len(between):
                    st_(*between[n])
            st_("sumsq", (i, 3))

        for p in range(4):
            each("square", (0, p)), each("sumsq", (0, p))
        st_("norm", 0), st_("ar"), c("av0"), st_("la")
        c("bq0"), st_("la_exps"), c("bk0"), st_("unit", 0), c("bv0"), st_("unit", 1), c("aq"), st_("lam")
        sw("diff", 0, 1), c("ak"), each("diff_t", 0, 1), sw("diff", 2, 3), each("diff_p", 0, 1), st_("ket")
        c("bq1"), st_("gla_att"), each("diff_t", 2, 3), c("bk1"), st_("unit", 2), each("diff_p", 2, 3)
        st_("diff_n", 0), c("av1"), st_("unit", 3), st_("gla_kv"), st_("diff_r", 0), sw("diff", 4, 5)
        c("bv1"), st_("gla_o", 0), each("diff_t", 4, 5), sw("diff", 6, 7), c("ag0"), st_("gla_r", 0)
        st_("gla_o", 1), c("ag1"), st_("gla_r", 1), each("diff_p", 4, 5), each("diff_t", 6, 7), st_("ag_silu")
        each("diff_p", 6, 7), st_("diff_n", 1), st_("diff_r", 1), st_("trig")
        projection([f"evo{p}" for p in range(4)], 1)
        st_("late")

        def conv_stages(l):
            st_("norm", 2 * l + 1), st_("ffn_in", l)
            pieces = segs = 0
            for j in range(11):
                for half in "gv":
                    c(f"up{l}{half}{j}")
                    if half == "g" and j:
                        st_("act", (l, j - 1))
                    if half == "v":
                        st_("silu", (l, j))
                    if pieces >= 4 * segs + 6:
                        st_("ada_sum", (l, segs))
                        segs += 1
                    if j or half == "v":
                        for _ in range(2 if half == "v" and j in (2, 5, 8) else 1):
                            st_("ada", 24 * l + pieces)
                            pieces += 1
            st_("act", (l, 10))
            assert pieces == 24 and segs == 5
            projection([f"down{l}_{p}_{i}" for p in range(4) for i in range(3)], 2 * l + 2,
                       [("ada_sum", (l, 5)), ("mod", l)])

        conv_stages(0)
        st_("norm", 2)
        for hp in range(2):
            for g in range(3):
                for q in range(3):
                    c(f"od{hp}{g}{q}")
                    u = 8 + 6 * hp + 2 * g + q
                    if q >= 1:
                        st_("unit", u - 1)
                    if hp == 1:
                        k = 3 * g + q
                        if 1 <= k < 5:
                            st_("dil_t", k - 1)
                        if 2 <= k < 6:
                            st_("dil_p", k - 2)
                        if k == 6:
                            st_("dil_o", 0)
                        if k < 4:
                            st_("dil_s", k), st_("dil_w", k)
        for u in range(4, 8):
            st_("dil_s", u), st_("dil_w", u)
            if u > 4:
                st_("dil_t", u - 1)
            if u > 5:
                st_("dil_p", u - 2)
            if u == 4:
                st_("mix1", 0)
        st_("dil_t", 7), st_("dil_p", 6), st_("dil_p", 7), st_("dil_o", 1), st_("mix1", 1)
        projection([f"odo{p}" for p in range(4)], 3)
        conv_stages(1)
        for l in range(2):
            st_("norm", 4 + 2 * l), st_("kr", l), c(f"cq{l}a"), c(f"cq{l}b"), st_("krot", l), c(f"ckv{l}"), st_("wide", (l, 0))
            c(f"u{l}0"), st_("wide", (l, 1)), c(f"u{l}1"), c(f"uqn{l}"), c(f"uqr{l}"), c(f"uk{l}"), st_("qrot", l), c(f"uv{l}")
            st_("pool", l)
            for n in range(8):
                c(f"gz{l}{'ab'[n // 4]}{n % 4}")
                now = (l, 2 * n), (l, 2 * n + 1)
                before = (l, 2 * n - 2), (l, 2 * n - 1)
                if n:
                    each("mla_t", *before)
                sw("mla", *now)
                if n:
                    each("mla_p", *before)
                if n == 3:
                    st_("pool_split", l), c(f"wp{l}"), st_("y", l)
            st_("gates", l), c(f"pp{l}_0"), each("mla_t", *now), c(f"pp{l}_1"), each("mla_p", *now)
            c(f"pa{l}_0"), c(f"pa{l}_1")
            projection([f"wo{l}_{p}" for p in range(4)], 5 + 2 * l)
            st_("norm", 5 + 2 * l)
            for p in range(16):
                c(f"fa{l}_{p}")
                if p:
                    st_("act2", (l, p - 1))
            st_("act2", (l, 15))
            projection([f"fb{l}_{p}_{i}" for p in range(4) for i in range(4)], 6 + 2 * l)
        st_("norm", 8)
        for n, name in enumerate(v for k, v in order if k == "chunk"):
            assert CH[n]["name"] == name, (n, name, CH[n]["name"])

        LAG, used_at, done = RAW + SPLIT, [], 0
        for stage, i in order:
            if stage == "chunk":
                done = BY[i]["n"]
            elif stage == "ada":
                used_at.append(done)
        ADA_LOAD = [n + LAG for n in [BY["evo3"]["n"]] * 2 + used_at[:-2]]

        BEFORE_NORM, done = {}, None
        for stage, i in order:
            if stage == "chunk":
                done = BY[i]["n"]
            elif stage == "norm" and i:
                BEFORE_NORM[i] = done

        def bank_of(ch, i=0):
            return (ch["bank"] + i) % LIN

        def freed_by(ch, i):
            name = ch["name"]
            if name in ("av0", "av1"):
                return S["va_ready"], int(name[2]) + 1
            if name in units:
                return S["unit_normed"], units[name] + 1
            if name == "aq":
                return S["gla_q"], 1
            if name == "ak":
                return S["gla_k"], 1
            if name in ("bv0", "bv1"):
                return S["vb_ready"], int(name[2]) + 1
            if name in ("ag0", "ag1"):
                return S["silu_ag"], int(name[2]) + 1
            if name.startswith("evo"):
                return S["x_updated"], int(name[3]) + 1
            if name.startswith("up"):
                l, j = int(name[2]), int(name[4:])
                return S["conv_done"], 22 * l + 2 * j + (name[3] == "v") + 1
            if name.startswith("down"):
                l, p, _ = (int(v) for v in name[4:].split("_"))
                return S["x_updated"], 4 * (2 * l + 1) + p + 1
            if name.startswith("odo"):
                return S["x_updated"], 8 + int(name[3]) + 1
            if name.startswith("od"):
                hp, g, q = (int(v) for v in name[2:])
                if q == 2:
                    return S["dv_ready"], 3 * hp + g + 1
                return S["unit_normed"], 8 + 6 * hp + 2 * g + q + 1
            l = int([v for v in name if v.isdigit()][0])
            if name.startswith("cq"):
                return S["wide_normed"], 2 * l + 1
            if name.startswith("ckv"):
                return S["wide_normed"], 2 * l + 2
            if name[0] == "u" and name[1].isdigit():
                return S["u_ready"], 2 * l + int(name[2]) + 1
            if name.startswith("uqn"):
                return S["q_nope"], 2 * l + i + 1
            if name.startswith("uqr"):
                return S["qr_copied"], l + 1
            if name.startswith("uk"):
                return S["k_nope"], 2 * l + i + 1
            if name.startswith("uv"):
                return S["mv_ready"], 2 * l + i + 1
            if name.startswith("gz"):
                return S["gates_raw"], 8 * l + 4 * (name[3] == "b") + int(name[4]) + 1
            if name.startswith("wp"):
                return S["y_ready"], 2 * l + i + 1
            if name.startswith("pp"):
                return S["gated_a"], 4 * l + 2 * int(name[-1]) + i + 1
            if name.startswith("pa"):
                return S["merged"], 4 * l + 2 * int(name[-1]) + i + 1
            if name.startswith("wo"):
                return S["x_updated"], 16 + 8 * l + int(name[-1]) + 1
            if name.startswith("fa"):
                return S["relu_done"], 16 * l + int(name.split("_")[1]) + 1
            if name.startswith("fb"):
                return S["x_updated"], 20 + 8 * l + int(name.split("_")[1]) + 1
            raise ValueError(name)

        @block.sync
        def _(sp):
            sp.dma_start(x[:], xT).then_inc(S["x_in"], 16)
            early = {k: where[LATE[k]][1] for k in LATE}
            sp.dma_start(consts[:, 0:early["consts"]], consts_d[:, 0:early["consts"]]).then_inc(S["consts_in"], 16)
            sp.dma_start(params[:, 0:early["params"]], params_d[:, 0:early["params"]]).then_inc(S["params_in"], 16)
            ada_at = 0
            for ch in CH:
                n, w = ch["n"], ch["width"]
                if n == RAW:
                    sp.dma_start(posi[:], positions.to_broadcast([P, TOK])).then_inc(S["pos_in"], 16)
                    sp.dma_start(consts[:, early["consts"]:], consts_d[:, early["consts"]:]).then_inc(S["late_in"], 16)
                    sp.dma_start(params[:, early["params"]:], params_d[:, early["params"]:]).then_inc(S["late_in"], 16)
                if n >= RAW:
                    sp.wait_ge(S["low_ready"], n - RAW + 1)
                sp.dma_start(raw[n % RAW][:, 0:w], stream[ch["at"] * P:(ch["at"] + w) * P]
                             .rearrange("(p w) -> p w", p=P)).then_inc(raw_in[n % RAW], 16)
                while ada_at < 48 and ADA_LOAD[ada_at] <= n:
                    a = ada_at
                    if a < 2:
                        sp.wait_ge(S["products_done"], BY["evo3"]["n"] + 1)
                    else:
                        sp.wait_ge(S["ada_added"], a - 1)
                    sp.dma_start(adaw[a % 2][:].rearrange("p a b -> p (a b)"),
                                 ada[a * P * CHUNK:(a + 1) * P * CHUNK].rearrange("(p w) -> p w", p=P))\
                        .then_inc((S["ada_in0"], S["ada_in1"])[a % 2], 16)
                    ada_at += 1
            sp.wait_ge(S["normed"], 36)
            sp.dma_start(out, h[:]).then_inc(S["stored"], 16)
            sp.wait_ge(S["stored"], 16)

        @block.tensor
        def _(pe):
            free_after, taken = {}, set()

            def claim(b):
                assert b in free_after or b not in taken, b
                taken.add(b)
                if b in free_after:
                    pe.wait_ge(*free_after.pop(b))

            def operand_wait(name):
                if name in ("av0",):
                    return S["operand_low"], lambda k: FILLS["n0"] + k // 2 + 1
                if name == "evo0":
                    return S["operand_low"], lambda k: FILLS["mix0"] + k // 2 + 1
                if name in ("up0g0", "up1g0"):
                    return S["operand_low"], lambda k: FILLS["n1" if name[2] == "0" else "n3"] + k // 2 + 1
                if name == "od000":
                    return S["operand_low"], lambda k: FILLS["n2"] + k // 2 + 1
                if name == "odo0":
                    return S["operand_low"], lambda k: FILLS["mix1"] + k // 2 + 1
                if name.startswith("down") and name.split("_")[1] == "0":
                    l = int(name[4])
                    return S["act_low"], lambda k: 11 * l + k // 2 + 1
                if name.startswith("cq") and name.endswith("a"):
                    l = int(name[2])
                    return S["operand_low"], lambda k: FILLS[f"n{4 + 2 * l}"] + k // 2 + 1
                if name.startswith("uqn"):
                    return S["cq_low"], lambda k: int(name[3]) + 1
                if name.startswith("uk"):
                    return S["ckv_low"], lambda k: int(name[2]) + 1
                if name.startswith("wp"):
                    return S["pooled_low"], lambda k: 2 * int(name[2]) + 2
                if name.startswith("pp") and name.endswith("0"):
                    return S["y_low"], lambda k: 2 * int(name[2]) + k // 2 + 1
                if name.startswith("pa") and name.endswith("_0"):
                    return S["att_low"], lambda k: 2 * int(name[2]) + k // 2 + 1
                if name.startswith("wo") and name.endswith("_0"):
                    return S["operand_low"], lambda k: FILLS[f"merged{name[2]}"] + k // 2 + 1
                if name.startswith("fa") and name.endswith("_0"):
                    return S["operand_low"], lambda k: FILLS[f"n{5 + 2 * int(name[2])}"] + k // 2 + 1
                if name.startswith("fb") and name.split("_")[1] == "0":
                    return S["act2_low"], lambda k: 16 * int(name[2]) + k // 2 + 1
                return None

            def chunk(name):
                ch = BY[name]
                n, rows, width = ch["n"], ch["rows"], ch["width"]
                wh, wl = high[n % SPLIT], low[n % SPLIT]
                act = "A" if ch["op"] == "A" and name[0] == "d" else "B" if ch["op"] == "A" else ch["op"]
                oh, ol = {"O": (OH, OL), "A": (AH, AL), "B": (BH, BL), "Q": (SQH, SQL), "C": (SCH, SCL)}[act]
                waits, seen = operand_wait(name), 0
                ncols = len(ch["cols"])
                pe.wait_ge(S["low_ready"], n + 1)
                if ch["first"]:
                    for i in range(ch["banks"]):
                        claim(bank_of(ch, i))

                def need(k):
                    nonlocal seen
                    if waits is not None and waits[1](k) > seen:
                        seen = waits[1](k)
                        pe.wait_ge(waits[0], seen)

                if ch["tm"]:
                    for t in range(2):
                        for i, k in enumerate(rows):
                            need(k)
                            o = (ps[bank_of(ch)][:, t, :] if ncols == 256 else
                                 ps[bank_of(ch, t)][:].rearrange("p a b -> p (a b)"))
                            w = slice(i * ncols, (i + 1) * ncols)
                            tk = slice(t * P, (t + 1) * P)
                            pe.matmul(o, ol[:, k, tk], wh[:, w], start=i == 0, stop=False)
                            pe.matmul(o, oh[:, k, tk], wl[:, w], start=False, stop=False)
                            mm = pe.matmul(o, oh[:, k, tk], wh[:, w], start=False, stop=i == len(rows) - 1)
                else:
                    for b in range(ncols // P):
                        o = ps[bank_of(ch, b // 2)][:, b % 2, :]
                        mine = [b] if ch["diag"] else rows
                        for i, k in enumerate(mine):
                            need(k)
                            w = slice(b * P, (b + 1) * P) if ch["diag"] else slice(i * ncols + b * P,
                                                                                   i * ncols + (b + 1) * P)
                            one = ch["first"] and i == 0 and (b % 2 == 0 or (ch["last"]))
                            end = ch["last"] and i == len(mine) - 1
                            pe.matmul(o, wl[:, w], oh[:, k, :], start=one, stop=False, skip_group_check=True)
                            pe.matmul(o, wh[:, w], ol[:, k, :], start=False, stop=False, skip_group_check=True)
                            mm = pe.matmul(o, wh[:, w], oh[:, k, :], start=False, stop=end, skip_group_check=True)
                mm.then_inc(S["products_done"], 1)
                if ch["last"]:
                    for i in range(ch["banks"]):
                        free_after[bank_of(ch, i)] = freed_by(ch, i)

            def sumsq(a):
                i, p = a
                if p == 0:
                    claim(NB)
                pe.wait_ge(S["squares_ready"], 4 * i + p + 1)
                for k in (2 * p, 2 * p + 1):
                    mm = pe.matmul(ps[NB][:, 0, :], col("ones"), h[:, k, :], start=k == 0, stop=k == KB - 1)
                if p == 3:
                    mm.then_inc(S["sumsq_ready"], 1)
                    free_after[NB] = (S["rstd_ready"], i + 1)

            def late(_):
                pe.wait_ge(S["late_in"], 32)

            def unit(u):
                pe.wait_ge(S["unit_squares"], u + 1)
                claim(NB)
                pe.matmul(ps[NB][:].rearrange("p a b -> p (a b)"), col("ones64" if u < 4 else "ones"),
                          sq[u % 2][:].rearrange("p a b -> p (a b)"), start=True, stop=True).then_inc(S["unit_sums"], 1)
                free_after[NB] = (S["unit_rstd"], u + 1)

            def ar_(_):
                pe.wait_ge(S["params_in"], 16)
                claim(OB)
                for k in range(KB):
                    if k % 2 == 0:
                        pe.wait_ge(S["normed"], k // 2 + 1)
                    mm = pe.matmul(ps[OB][0:16, 0, :], col("w_ar", 16 * k, 16), h[:, k, :], start=k == 0,
                                   stop=k == KB - 1)
                mm.then_inc(S["ar_done"], 1)
                free_after[OB] = (S["ar_copied"], 1)

            def la_(_):
                pe.wait_ge(S["ar_copied"], 1)
                claim(TB)
                for b in range(2):
                    mm = pe.matmul(ps[TB][:, b, :], col("w_a2", b * P, P)[0:16], ar[:], start=True, stop=True)
                mm.then_inc(S["la_done"], 1)
                free_after[TB] = (S["la_biased"], 1)

            def ket(_):
                pe.wait_ge(S["gla_k"], 1)
                claim(TB)
                for t in range(2):
                    for b in range(2):
                        mm = pe.transpose(ps[TB][:, t, b * P:(b + 1) * P], la[:, b, t * P:(t + 1) * P], col("ident"))
                mm.then_inc(S["ket_done"], 1)
                free_after[TB] = (S["ket_copied"], 1)

            def gla_att(_):
                for hh in range(4):
                    if hh % 2 == 0:
                        claim((SB0, SB1)[hh // 2])
                    for t in range(2):
                        tk = slice(t * P, (t + 1) * P)
                        mm = pe.matmul(ps[(SB0, SB1)[hh // 2]][:, hh % 2, tk], kd[:, hh, tk], qd[:, hh, tk],
                                       start=True, stop=True)
                    if hh % 2:
                        mm.then_inc(S["att_done"], 1)
                        free_after[(SB0, SB1)[hh // 2]] = (S["att_masked"], hh // 2 + 1)

            def gla_kv(_):
                pe.wait_ge(S["ket_copied"], 1)
                pe.wait_ge(S["va_ready"], 2)
                for cc in range(3):
                    claim(TB)
                    v = (va[0:64, 0, :], va1[:], va[0:64, 1, :])[cc]
                    for hh in range(4):
                        o = ps[TB][0:64].rearrange("p a b -> p (a b)")
                        mm = pe.matmul(o[:, hh * P:(hh + 1) * P], keT[:, cc, hh * 64:(hh + 1) * 64],
                                       v[:, hh * P:(hh + 1) * P], start=True, stop=True)
                    mm.then_inc(S["kv_done"], 1)
                    free_after[TB] = (S["state_ready"], cc + 1)

            def gla_o(hp):
                if hp == 0:
                    pe.wait_ge(S["att_masked"], 2)
                    pe.wait_ge(S["state_ready"], 3)
                claim(OB)
                for hh in (2 * hp, 2 * hp + 1):
                    for t in range(2):
                        pe.matmul(ps[OB][:, hh % 2, t * P:(t + 1) * P], va[:, t, hh * P:(hh + 1) * P], att[:, hh, t, :],
                                  start=True, stop=False, skip_group_check=True)
                        for cc in (2 * t, 2 * t + 1):
                            if cc:
                                ck = slice(cc * 64, (cc + 1) * 64)
                                mm = pe.matmul(ps[OB][:, hh % 2, ck], st[cc - 1][:, hh, :], qd[:, hh, ck], start=False,
                                               stop=cc % 2 == 1, skip_group_check=True)
                mm.then_inc(S["gla_o_done"], 1)
                free_after[OB] = (S["unit_normed"], GLA_U[hp] + 1)

            def diff_s(u):
                hh, qt = u // 2, u % 2
                if u % 4 == 0:
                    pe.wait_ge(S["unit_normed"], DIFF_QK[u // 4] + 1)
                claim((SB0, SB1)[u % 2])
                nk = P * (qt + 1)
                for cc in range(2):
                    mm = pe.matmul(ps[(SB0, SB1)[u % 2]][:, cc, 0:nk], Qd[:, cc, hh, qt * P:(qt + 1) * P],
                                   Kd[:, cc, hh, 0:nk], start=True, stop=True)
                mm.then_inc(S["diff_scores"], 1)
                free_after[(SB0, SB1)[u % 2]] = (S["diff_max"], u + 1)

            def diff_t(u):
                pe.wait_ge(S["diff_w"], u + 1)
                if u % 2 == 0:
                    claim(TB)
                for kt in range(u % 2 + 1):
                    mm = pe.transpose(ps[TB][:, u % 2, kt * P:(kt + 1) * P], W[u % 2][:, kt * P:(kt + 1) * P],
                                      col("ident"))
                mm.then_inc(S["diff_turned"], 1)
                if u % 2:
                    free_after[TB] = (S["diff_copied"], u + 1)

            def diff_p(u):
                hh, qt = u // 2, u % 2
                pe.wait_ge(S["diff_copied"], u + 1)
                if u % 4 == 0:
                    pe.wait_ge(S["vb_ready"], u // 4 + 1)
                    claim(OB)
                for kt in range(qt + 1):
                    mm = pe.matmul(ps[OB][:, hh % 2, qt * P:(qt + 1) * P], vb[:, kt, hh * P:(hh + 1) * P],
                                   WT[u % 2][:, kt * P:(kt + 1) * P], start=kt == 0, stop=kt == qt)
                mm.then_inc(S["diff_pv"], 1)
                if u % 4 == 3:
                    free_after[OB] = (S["unit_normed"], DIFF_U[u // 4] + 1)

            def dil_s(u):
                hh, qt = u // 2, u % 2
                hp = hh // 2
                if u % 4 == 0:
                    pe.wait_ge(S["unit_normed"], 8 + 6 * hp + 6)
                nk = P * (qt + 1)
                for b in (SB0, SB1):
                    claim(b)
                for g in range(3):
                    o = ps[(SB0, SB1)[g // 2]][:, g % 2, 0:nk]
                    mm = pe.matmul(o, dq[hp][g][:, hh % 2, qt * P:(qt + 1) * P], dk[hp][g][:, hh % 2, 0:nk],
                                   start=True, stop=True)
                mm.then_inc(S["dil_scores"], 1)
                free_after[SB0] = free_after[SB1] = (S["dil_max"], u + 1)

            def dil_t(u):
                hh, qt = u // 2, u % 2
                hp, nk = hh // 2, P * (qt + 1)
                pe.wait_ge(S["dil_w"], u + 1)
                n = 3 * (qt + 1)
                for part in range(0, n, 3):
                    claim(TB)
                    for i in range(part, part + 3):
                        o = ps[TB][:].rearrange("p a b -> p (a b)")[:, (i - part) * P:(i - part + 1) * P]
                        mm = pe.transpose(o, DS[u % 2][:, i * P:(i + 1) * P], col("ident"))
                    mm.then_inc(S["dil_turned"], 1)
                    free_after[TB] = (S["dil_copied"], 3 * hh + qt + part // 3 + 1)

            def dil_p(u):
                hh, qt = u // 2, u % 2
                hp = hh // 2
                pe.wait_ge(S["dil_copied"], 3 * hh + 2 * qt + 1)
                if u % 4 == 0:
                    pe.wait_ge(S["dv_ready"], 3 * hp + 3)
                    claim(OB)
                for g in range(3):
                    for kt in range(qt + 1):
                        mm = pe.matmul(ps[OB][:, hh % 2, qt * P:(qt + 1) * P], dv[hp][g][:, kt, (hh % 2) * P:(hh % 2 + 1) * P],
                                       DT[u % 2][:, g * (qt + 1) + kt, :], start=g == 0 and kt == 0,
                                       stop=g == 2 and kt == qt)
                mm.then_inc(S["dil_pv"], 1)
                if u % 4 == 3:
                    free_after[OB] = (S["dil_out"], hp + 1)

            def ada_sum(a):
                l, seg = a
                pe.wait_ge(S["ada_added"], 4 * (6 * l + seg + 1))
                if seg == 0:
                    claim(OB)
                for b in range(8):
                    mm = pe.matmul(ps[OB][:, 0, 8 * seg + b:8 * seg + b + 1], adas[seg % 2][:, b * P:(b + 1) * P],
                                   col("ones", 0, 1), start=True, stop=True)
                mm.then_inc(S["ada_sum"], 1)
                if seg == 5:
                    free_after[OB] = (S["mod_ready"], l + 1)

            def kr_(l):
                claim(OB)
                for k in range(KB):
                    if k % 2 == 0:
                        pe.wait_ge(S["normed"], 4 * (4 + 2 * l) + k // 2 + 1)
                    mm = pe.matmul(ps[OB][0:32, 0, :], col("w_kr", (8 * l + k) * 32, 32), h[:, k, :], start=k == 0,
                                   stop=k == KB - 1)
                mm.then_inc(S["kr_done"], 1)
                free_after[OB] = (S["kr_copied"], l + 1)

            def krot(l):
                pe.wait_ge(S["kr_copied"], l + 1)
                claim(TB)
                pe.matmul(ps[TB][0:32, 0, :], col("rot", 0, 32)[0:32], kr[:], start=True, stop=True)\
                    .then_inc(S["krot_done"], 1)
                free_after[TB] = (S["krope_done"], l + 1)

            def wide(a):
                l, which = a
                i = 2 * l + which
                pe.wait_ge(S["wide_squares"], i + 1)
                claim(NB)
                blocks = range(3) if which == 0 else range(3, 5)
                for k in blocks:
                    mm = pe.matmul(ps[NB][:, 0, :], col("ones"), h[:, k, :], start=k == blocks[0], stop=k == blocks[-1])
                mm.then_inc(S["wide_sums"], 1)
                free_after[NB] = (S["wide_rstd"], i + 1)

            def qrot(l):
                pe.wait_ge(S["qr_copied"], l + 1)
                claim(TB)
                pe.matmul(ps[TB][:].rearrange("p a b -> p (a b)"), col("rot"), qr[:].rearrange("p a b -> p (a b)"),
                          start=True, stop=True).then_inc(S["qrot_done"], 1)
                free_after[TB] = (S["q_rope"], 2 * l + 1)

            def mla_s(a):
                l, u = a
                hh, qt = u // 2, u % 2
                U = 16 * l + u
                if u == 0:
                    pe.wait_ge(S["q_rope"], 2 * l + 2)
                    pe.wait_ge(S["q_nope"], 2 * l + 2)
                    pe.wait_ge(S["k_nope"], 2 * l + 2)
                    pe.wait_ge(S["kfull"], l + 1)
                claim((SB0, SB1)[u % 2])
                nk = P * (qt + 1)
                pe.matmul(ps[(SB0, SB1)[u % 2]][:, 0, 0:nk], MQ[:, hh, qt * P:(qt + 1) * P], MK[:, hh, 0:nk],
                          start=True, stop=True).then_inc(S["mla_scores"], 1)
                free_after[(SB0, SB1)[u % 2]] = (S["mla_max"], U + 1)

            def mla_t(a):
                l, u = a
                U = 16 * l + u
                pe.wait_ge(S["mla_w"], U + 1)
                if u % 2 == 0:
                    claim(TB)
                for kt in range(u % 2 + 1):
                    mm = pe.transpose(ps[TB][:, u % 2, kt * P:(kt + 1) * P], MS[u % 2][:, kt * P:(kt + 1) * P],
                                      col("ident"))
                mm.then_inc(S["mla_turned"], 1)
                if u % 2:
                    free_after[TB] = (S["mla_copied"], U + 1)

            def mla_p(a):
                l, u = a
                hh, qt = u // 2, u % 2
                U = 16 * l + u
                pe.wait_ge(S["mla_copied"], U + 1)
                if u == 0:
                    pe.wait_ge(S["mv_ready"], 2 * l + 2)
                if u % 8 == 0:
                    claim(OB)
                r = slice(64 * (hh % 2), 64 * (hh % 2) + 64)
                for kt in range(qt + 1):
                    mm = pe.matmul(ps[OB][r, (hh // 2) % 2, qt * P:(qt + 1) * P], mv[:, kt, hh * 64:(hh + 1) * 64],
                                   MT[u % 2][:, kt * P:(kt + 1) * P], start=kt == 0, stop=kt == qt)
                mm.then_inc(S["mla_pv"], 1)
                if u % 8 == 7:
                    free_after[OB] = (S["att_low"], 2 * l + u // 8 + 1)

            pe.wait_ge(S["consts_in"], 16)
            stages = dict(chunk=chunk, sumsq=sumsq, late=late, unit=unit, ar=ar_, la=la_, ket=ket, gla_att=gla_att,
                          gla_kv=gla_kv, diff_p=diff_p, dil_p=dil_p, mla_p=mla_p,
                          gla_o=gla_o, diff_s=diff_s, diff_t=diff_t, dil_s=dil_s, dil_t=dil_t, ada_sum=ada_sum, kr=kr_,
                          krot=krot, wide=wide, qrot=qrot, mla_s=mla_s, mla_t=mla_t, gla_r=lambda hp: unit(GLA_U[hp]),
                          diff_r=lambda hp: unit(DIFF_U[hp]))
            for stage, i in order:
                if stage in stages:
                    stages[stage](i)

        @block.scalar
        def _(act):
            chain, split_to = [0], [0]

            def link(ins):
                chain[0] += 1
                ins.then_inc(S["act_chain"], 1)
                act.wait_ge(S["act_chain"], chain[0])

            def high_upto(n):
                while split_to[0] <= min(n, NCH - 1):
                    m = split_to[0]
                    act.wait_ge(raw_in[m % RAW], 16 * (m // RAW + 1))
                    if m >= SPLIT:
                        act.wait_ge(S["products_done"], m - SPLIT + 1)
                        act.wait_ge(S["low_ready"], m - SPLIT + 1)
                    w = CH[m]["width"]
                    act.activation(high[m % SPLIT][:, 0:w], raw[m % RAW][:, 0:w], ACT.Copy)\
                        .then_inc(S["high_ready"], 1)
                    split_to[0] += 1

            def squares_of(u, bank):
                if u >= 2:
                    act.wait_ge(S["unit_sums"], u - 1)
                act.activation(sq[u % 2][:], ps[bank][:], ACT.Square).then_inc(S["unit_squares"], 1)

            def unit(u):
                act.wait_ge(S["unit_sums"], u + 1)
                if u >= 2:
                    act.wait_ge(S["unit_normed"], u - 1)
                link(act.activation(rb[u % 2][:], ps[NB][:], ACT.Ln, scale=1.0 / (64 if u < 4 else 128),
                                    bias=col("eps")))
                act.activation(rb[u % 2][:], rb[u % 2][:], ACT.Exp, scale=-0.5).then_inc(S["unit_rstd"], 1)

            def chunk(name):
                ch = BY[name]
                n = ch["n"]
                act.wait_ge(S["products_done"], n + 1)
                b = bank_of(ch)
                if name in ("av0", "av1"):
                    j = int(name[2]) * 256
                    act.activation(va[:, :, j:j + 256], ps[b][:], ACT.Copy)
                    act.activation(va1[:, j:j + 256], ps[b][64:128, 0, :], ACT.Copy).then_inc(S["va_ready"], 1)
                elif name in units:
                    squares_of(units[name], b)
                elif name in ("bv0", "bv1"):
                    j = int(name[2]) * 256
                    act.activation(vb[:, :, j:j + 256], ps[b][:], ACT.Copy).then_inc(S["vb_ready"], 1)
                elif name in ("ag0", "ag1"):
                    j = int(name[2]) * 2
                    act.activation(sg[:, j:j + 2, :], ps[b][:], ACT.Copy).then_inc(S["silu_ag"], 1)
                elif name.startswith("up"):
                    l, j, v = int(name[2]), int(name[4:]), int(name[3] == "v")
                    if j >= 2:
                        act.wait_ge(S["act_low"], 11 * l + j - 1)
                    dst = (cg, cv)[v][j % 2]
                    for i in range(2):
                        t = (44 * l + 22 * v + 2 * j + i) * 4
                        ins = act.activation(dst[:, i, :], ps[b][:, i, :], ACT.Identity, scale=col("conv", t + 2, 1),
                                             bias=col("conv", t + 3, 1))
                    ins.then_inc(S["conv_init"], 1)
                elif name.startswith("od") and name[2] != "o":
                    hp, g, q = (int(v) for v in name[2:])
                    if q == 2:
                        act.activation(dv[hp][g][:], ps[b][:], ACT.Copy).then_inc(S["dv_ready"], 1)
                    else:
                        squares_of(8 + 6 * hp + 2 * g + q, b)
                elif name.startswith("cq"):
                    if name[3] == "a":
                        act.activation(h[:, 0:2, :], ps[b][:], ACT.Square)
                    else:
                        act.activation(h[:, 2, :], ps[b][:, 0, :], ACT.Square).then_inc(S["wide_squares"], 1)
                elif name.startswith("ckv"):
                    act.activation(h[:, 3:5, :], ps[b][:], ACT.Square).then_inc(S["wide_squares"], 1)
                elif name[0] == "u" and name[1].isdigit():
                    j = int(name[2])
                    act.activation(up[:, 2 * j:2 * j + 2, PAD:], ps[b][:], ACT.Copy).then_inc(S["u_ready"], 1)
                elif name.startswith("uqn"):
                    for i in range(2):
                        for half in range(2):
                            ins = act.activation(MQ[0:64, 4 * i + half:4 * i + 4:2, :],
                                                 ps[bank_of(ch, i)][64 * half:64 * half + 64], ACT.Copy)
                        ins.then_inc(S["q_nope"], 1)
                elif name.startswith("uqr"):
                    act.activation(qr[:], ps[b][:], ACT.Copy).then_inc(S["qr_copied"], 1)
                elif name.startswith("uv"):
                    for t in range(2):
                        act.activation(mv[:, t, :], ps[bank_of(ch, t)][:].rearrange("p a b -> p (a b)"), ACT.Copy)\
                            .then_inc(S["mv_ready"], 1)
                elif name.startswith("gz"):
                    p = int(name[4])
                    act.activation((za, zb)[name[3] == "b"][:, 2 * p:2 * p + 2, :], ps[b][:], ACT.Copy)\
                        .then_inc(S["gates_raw"], 1)
                elif name.startswith("wp"):
                    l = int(name[2])
                    for g in range(4):
                        ins = act.activation(p1[:, g, PAD:], ps[bank_of(ch, g // 2)][:, g % 2, :], ACT.Copy,
                                             scale=col("pool_scale", 4 * l + g, 1))
                        if g % 2:
                            ins.then_inc(S["y_ready"], 1)
                elif name.startswith("fa"):
                    l, p = int(name[2]), int(name.split("_")[1])
                    if p >= RELU:
                        act.wait_ge(S["act2_low"], 16 * l + p - RELU + 1)
                    act.activation(rl[p % RELU][:], ps[b][:], ACT.Relu).then_inc(S["relu_done"], 1)
                elif name.startswith("pa"):
                    l, i2 = int(name[2]), int(name[-1])
                    for p in (2 * i2, 2 * i2 + 1):
                        act.wait_ge(S["merged"], 4 * l + p + 1)
                        act.activation(OH[:, 2 * p:2 * p + 2, :], h[:, 2 * p:2 * p + 2, :], ACT.Copy)\
                            .then_inc(S["operand_high"], 1)
                if n not in BEFORE_NORM.values():
                    high_upto(n + SPLIT)

            def square(a):
                i, p = a
                if i:
                    act.wait_ge(S["x_updated"], 4 * (i - 1) + p + 1)
                elif p == 0:
                    act.wait_ge(S["x_in"], 16)
                act.activation(h[:, 2 * p:2 * p + 2, :], x[:, 2 * p:2 * p + 2, :], ACT.Square)\
                    .then_inc(S["squares_ready"], 1)

            def norm(i):
                if i == 0:
                    act.wait_ge(S["consts_in"], 16)
                act.wait_ge(S["sumsq_ready"], i + 1)
                link(act.activation(rn[:], ps[NB][:, 0, :], ACT.Ln, scale=1.0 / D, bias=col("eps")))
                act.activation(rn[:], rn[:], ACT.Exp, scale=-0.5).then_inc(S["rstd_ready"], 1)
                if i < 8:
                    for p in range(4):
                        act.wait_ge(S["normed"], 4 * i + p + 1)
                        act.activation(OH[:, 2 * p:2 * p + 2, :], h[:, 2 * p:2 * p + 2, :], ACT.Copy)\
                            .then_inc(S["operand_high"], 1)
                high_upto(SPLIT - 1 if i == 0 else BEFORE_NORM[i] + SPLIT)

            def late(_):
                act.wait_ge(S["late_in"], 32)

            def trig(_):
                act.wait_ge(S["trig_angle"], 1)
                act.activation(sinT[:], ang[:], ACT.Sin)
                act.activation(cosT[:], turn[:], ACT.Sin).then_inc(S["trig_done"], 1)
                act.preload_act_table_set(EXP_LN)

            def lam(_):
                act.wait_ge(S["lam_sums"], 1)
                act.activation(small[:, 4:6], small[:, 2:4], ACT.Exp).then_inc(S["lam_exp"], 1)

            def ar_(_):
                act.wait_ge(S["ar_done"], 1)
                act.activation(ar[:], ps[OB][0:16, 0, :], ACT.Copy).then_inc(S["ar_copied"], 1)

            def la_(_):
                act.wait_ge(S["la_done"], 1)
                for b in range(2):
                    ins = act.activation(la[:, b, :], ps[TB][:, b, :], ACT.Identity, bias=col("b_a", b, 1))
                ins.then_inc(S["la_biased"], 1)
                act.wait_ge(S["la_biased"], 1)
                link(act.activation(ebl[:], la[:], ACT.Abs))
                link(act.activation(ebl[:], ebl[:], ACT.Exp, scale=-1.0))
                act.activation(ebl[:], ebl[:], ACT.Ln, bias=col("ones", 0, 1)).then_inc(S["la_log"], 1)

            def la_exps(_):
                act.wait_ge(S["la_diff"], 1)
                act.activation(eb[:], bc[:], ACT.Exp, scale=1 / 16).then_inc(S["gate_exps"], 1)
                act.activation(enb[:], bc[:], ACT.Exp, scale=-1 / 16).then_inc(S["gate_exps"], 1)
                act.activation(ebl[:], ebl[:], ACT.Exp, scale=1 / 16).then_inc(S["gate_exps"], 1)

            def ket(_):
                act.wait_ge(S["ket_done"], 1)
                for cc in range(3):
                    r = slice(64 * (cc % 2), 64 * (cc % 2) + 64)
                    ins = act.activation(keT[:, cc, :], ps[TB][r, cc // 2, :], ACT.Copy)
                ins.then_inc(S["ket_copied"], 1)

            def ag_silu(_):
                act.wait_ge(S["silu_ag"], 2)
                act.activation(sg[:], sg[:], ACT.Silu).then_inc(S["silu_ag"], 1)
                act.preload_act_table_set(EXP_LN)
                mix_high((0, 1))

            def mix_high(pairs):
                for p in pairs:
                    if p < 2:
                        act.wait_ge(S["mix_ready"], p + 1)
                    else:
                        act.wait_ge(S["unit_normed"], DIFF_U[p - 2] + 1)
                    act.activation(OH[:, 2 * p:2 * p + 2, :], h[:, 2 * p:2 * p + 2, :], ACT.Copy)\
                        .then_inc(S["operand_high"], 1)

            def softmax_exp(scores, sums, src, neg_max, total, scale, inc):
                act.wait_ge(*scores)
                act.activation(src, src, ACT.Exp, bias=neg_max, scale=scale, accum_out=total).then_inc(inc, 1)

            def diff_s(u):
                act.wait_ge(S["diff_max"], u + 1)
                nk = P * (u % 2 + 1)
                for cc in range(2):
                    ins = act.activation(Sb[u % 2][:, cc, 0:nk], Sb[u % 2][:, cc, 0:nk], ACT.Exp, scale=0.125,
                                         bias=stat[:, u % 2, 2 + cc:3 + cc], accum_out=stat[:, u % 2, 4 + cc:5 + cc])
                ins.then_inc(S["diff_exp"], 1)

            def diff_t(u):
                nk = P * (u % 2 + 1)
                act.wait_ge(S["diff_turned"], u - u % 2 + 2)
                if u >= 2:
                    act.wait_ge(S["diff_pv"], u - 1)
                act.activation(WT[u % 2][:, 0:nk], ps[TB][:, u % 2, 0:nk], ACT.Copy).then_inc(S["diff_copied"], 1)

            def dil_s(u):
                act.wait_ge(S["dil_max"], u + 1)
                nk = P * (u % 2 + 1)
                act.activation(DS[u % 2][:, 0:3 * nk], DS[u % 2][:, 0:3 * nk], ACT.Exp, scale=128 ** -0.5,
                               bias=dstat[:, u % 2, 1:2], accum_out=dstat[:, u % 2, 2:3]).then_inc(S["dil_exp"], 1)

            def dil_t(u):
                hh, qt = u // 2, u % 2
                for part in range(qt + 1):
                    turned = 3 * hh + qt + part + 1
                    act.wait_ge(S["dil_turned"], turned)
                    if u >= 2 and part == 0:
                        act.wait_ge(S["dil_pv"], u - 1)
                    act.activation(DT[u % 2][:, 3 * part:3 * part + 3, :], ps[TB][:].rearrange("p a b -> p (a b)")[:, 0:384]
                                   .rearrange("p (a b) -> p a b", a=3), ACT.Copy).then_inc(S["dil_copied"], 1)

            def dil_o(hp):
                act.wait_ge(S["dil_pv"], 4 * hp + 4)
                act.activation(h[:, 2 * hp:2 * hp + 2, :], ps[OB][:], ACT.Copy).then_inc(S["dil_out"], 1)

            def mix1(hp):
                act.wait_ge(S["dil_out"], hp + 1)
                act.wait_ge(S["products_done"], BY["od122"]["n"] + 1)
                act.activation(OH[:, 2 * hp:2 * hp + 2, :], h[:, 2 * hp:2 * hp + 2, :], ACT.Copy)\
                    .then_inc(S["operand_high"], 1)

            def ffn_in(l):
                if l == 0:
                    act.activation(cact[:], col("c"), ACT.Silu).then_inc(S["c_silu"], 1)

            def ada_(a):
                act.wait_ge((S["ada_in0"], S["ada_in1"])[a % 2], 16 * (a // 2 + 1))
                if a == 0:
                    act.wait_ge(S["c_silu"], 1)
                for i in range(2):
                    k = 2 * (a % 4) + i
                    ins = act.activation(adaw[a % 2][:, i, :], adaw[a % 2][:, i, :], ACT.Copy, scale=cact[:, k:k + 1])
                ins.then_inc(S["ada_scaled"], 1)

            def silu(a):
                l, j = a
                act.wait_ge(S["conv_done"], 22 * l + 2 * j + 1)
                act.activation(cg[j % 2][:], cg[j % 2][:], ACT.Silu).then_inc(S["silu_done"], 1)

            def act_(a):
                l, j = a
                act.wait_ge(S["act_mul"], 11 * l + j + 1)
                act.activation(AH[:, 2 * j:2 * j + 2, :], cg[j % 2][:], ACT.Copy).then_inc(S["act_high"], 1)
                if j == 10:
                    act.preload_act_table_set(EXP_LN)

            def act2(a):
                l, p = a
                act.wait_ge(S["sq_done"], 16 * l + p + 1)
                act.activation(BH[:, 2 * p:2 * p + 2, :], rl[p % RELU][:], ACT.Copy).then_inc(S["act2_high"], 1)

            def kr_(l):
                act.wait_ge(S["kr_done"], l + 1)
                act.activation(kr[:], ps[OB][0:32, 0, :], ACT.Copy).then_inc(S["kr_copied"], 1)

            def wide(a):
                l, which = a
                i = 2 * l + which
                act.wait_ge(S["wide_sums"], i + 1)
                if i:
                    act.wait_ge(S["wide_normed"], i)
                link(act.activation(rn[:], ps[NB][:, 0, :], ACT.Ln, scale=1.0 / (384, 256)[which], bias=col("eps")))
                act.activation(rn[:], rn[:], ACT.Exp, scale=-0.5).then_inc(S["wide_rstd"], 1)
                act.wait_ge(S["wide_normed"], i + 1)
                if which == 0:
                    act.activation(SQH[:, 0:3, :], h[:, 0:3, :], ACT.Copy).then_inc(S["cq_high"], 1)
                else:
                    act.activation(SCH[:, 0:2, :], h[:, 3:5, :], ACT.Copy).then_inc(S["ckv_high"], 1)

            def pool_split(l):
                act.wait_ge(S["pooled"], 2 * l + 1)
                act.activation(SQH[:, 0::2, :], p1[:, 0::2, PAD:], ACT.Copy).then_inc(S["pooled_high"], 1)
                act.wait_ge(S["pooled"], 2 * l + 2)
                act.activation(SQH[:, 1::2, :], p2[:, 1::2, PAD:], ACT.Copy).then_inc(S["pooled_high"], 1)

            def y_(l):
                for i in range(2):
                    act.wait_ge(S["y_ready"], 2 * l + i + 1)
                    act.activation(SQH[:, 2 * i:2 * i + 2, :], p1[:, 2 * i:2 * i + 2, PAD:], ACT.Copy)\
                        .then_inc(S["y_high"], 1)

            def gates(l):
                act.wait_ge(S["gates_raw"], 8 * l + 8)
                act.activation(za[:], za[:], ACT.Sigmoid).then_inc(S["gates"], 1)
                act.activation(zb[:], zb[:], ACT.Sigmoid).then_inc(S["gates"], 1)
                act.preload_act_table_set(EXP_LN)

            def mla_s(a):
                l, u = a
                U, nk = 16 * l + u, P * (u % 2 + 1)
                act.wait_ge(S["mla_max"], U + 1)
                act.activation(MS[u % 2][:, 0:nk], MS[u % 2][:, 0:nk], ACT.Exp, scale=96 ** -0.5,
                               bias=mstat[:, u % 2, 1:2], accum_out=mstat[:, u % 2, 2:3]).then_inc(S["mla_exp"], 1)

            def mla_t(a):
                l, u = a
                U, nk = 16 * l + u, P * (u % 2 + 1)
                act.wait_ge(S["mla_turned"], U - U % 2 + 2)
                if U >= 2:
                    act.wait_ge(S["mla_pv"], U - 1)
                act.activation(MT[u % 2][:, 0:nk], ps[TB][:, u % 2, 0:nk], ACT.Copy).then_inc(S["mla_copied"], 1)

            def mla_p(a):
                l, u = a
                U = 16 * l + u
                if u % 8 == 7:
                    i = u // 8
                    act.wait_ge(S["mla_pv"], U + 1)
                    act.activation(SCH[:, 2 * i:2 * i + 2, :], ps[OB][:], ACT.Copy).then_inc(S["att_high"], 1)

            act.preload_act_table_set(EXP_LN)

            def gla_o(hp):
                act.wait_ge(S["gla_o_done"], hp + 1)
                squares_of(GLA_U[hp], OB)

            def diff_n(i):
                act.wait_ge(S["diff_pv"], 4 * i + 4)
                squares_of(DIFF_U[i], OB)

            def diff_r(i):
                unit(DIFF_U[i])
                if i == 1:
                    mix_high((2, 3))

            stages = dict(chunk=chunk, square=square, norm=norm, late=late, dil_o=dil_o, mla_p=mla_p, unit=unit,
                          trig=trig, lam=lam, ar=ar_, la=la_, la_exps=la_exps, ket=ket,
                          ag_silu=ag_silu, diff_s=diff_s, diff_t=diff_t, dil_s=dil_s, dil_t=dil_t, mix1=mix1, ffn_in=ffn_in,
                          silu=silu, ada=ada_, act=act_, act2=act2, kr=kr_, wide=wide, pool_split=pool_split, y=y_, gates=gates,
                          mla_s=mla_s, mla_t=mla_t, gla_o=gla_o, gla_r=lambda hp: unit(GLA_U[hp]), diff_n=diff_n,
                          diff_r=diff_r)
            for stage, i in order:
                if stage in stages:
                    stages[stage](i)

        @block.vector
        def _(dve):
            chain, split_to = [0], [0]

            def link(ins):
                chain[0] += 1
                ins.then_inc(S["dve_chain"], 1)
                dve.wait_ge(S["dve_chain"], chain[0])

            def low_upto(n):
                while split_to[0] <= min(n, NCH - 1):
                    m = split_to[0]
                    if m >= SPLIT:
                        dve.wait_ge(S["products_done"], m - SPLIT + 1)
                    dve.wait_ge(S["high_ready"], m + 1)
                    w = CH[m]["width"]
                    dve.tensor_tensor(low[m % SPLIT][:, 0:w], raw[m % RAW][:, 0:w], high[m % SPLIT][:, 0:w],
                                      ALU.subtract).then_inc(S["low_ready"], 1)
                    split_to[0] += 1

            def operand_low(f, p):
                dve.wait_ge(S["operand_high"], FILLS[f] + p + 1)
                dve.tensor_tensor(OL[:, 2 * p:2 * p + 2, :], h[:, 2 * p:2 * p + 2, :], OH[:, 2 * p:2 * p + 2, :],
                                  ALU.subtract).then_inc(S["operand_low"], 1)

            def add_to_x(b, p, gain=None):
                xp = x[:, 2 * p:2 * p + 2, :]
                if gain is None:
                    dve.tensor_tensor(xp, ps[b][:], xp, ALU.add).then_inc(S["x_updated"], 1)
                else:
                    for i in range(2):
                        ins = dve.scalar_tensor_tensor(out=x[:, 2 * p + i, :], in0=ps[b][:, i, :],
                                                       scalar=gain[:, 2 * p + i:2 * p + i + 1], in1=x[:, 2 * p + i, :],
                                                       op0=ALU.mult, op1=ALU.add)
                    ins.then_inc(S["x_updated"], 1)

            def chunk(name):
                ch = BY[name]
                n, b = ch["n"], bank_of(ch)
                if ch["last"] and name.startswith(("aq", "ak", "evo", "odo", "down", "up", "uk", "pp", "pa", "wo", "fb")):
                    dve.wait_ge(S["products_done"], n + 1)
                if name == "aq":
                    dve.wait_ge(S["gate_exps"], 3)
                    for half in range(2):
                        r = slice(64 * half, 64 * half + 64)
                        ins = dve.scalar_tensor_tensor(out=qd[:, half::2, :], in0=ps[b][r], scalar=0.125, in1=eb[r],
                                                       op0=ALU.mult, op1=ALU.mult)
                    ins.then_inc(S["gla_q"], 1)
                elif name == "ak":
                    for half in range(2):
                        r = slice(64 * half, 64 * half + 64)
                        dve.tensor_tensor(kd[:, half::2, :], ps[b][r], enb[r], ALU.mult)
                    dve.tensor_tensor(la[:], ps[b][:], ebl[:], ALU.mult).then_inc(S["gla_k"], 1)
                elif name.startswith("evo"):
                    add_to_x(b, int(name[3]))
                elif name.startswith("odo"):
                    add_to_x(b, int(name[3]))
                elif name.startswith("down") and ch["last"]:
                    add_to_x(b, int(name.split("_")[1]))
                elif name.startswith("up"):
                    l, j, v = int(name[2]), int(name[4:]), int(name[3] == "v")
                    dst = (cg, cv)[v][j % 2]
                    dve.wait_ge(S["conv_init"], 22 * l + 2 * j + v + 1)
                    for tap in (1, 0):
                        d = 2 - tap
                        for i in range(2):
                            t = (44 * l + 22 * v + 2 * j + i) * 4
                            ins = dve.scalar_tensor_tensor(out=dst[:, i, d:], in0=ps[b][:, i, 0:TOK - d],
                                                           scalar=col("conv", t + tap, 1), in1=dst[:, i, d:],
                                                           op0=ALU.mult, op1=ALU.add)
                        if tap:
                            link(ins)
                    ins.then_inc(S["conv_done"], 1)
                elif name.startswith("uk"):
                    for i in range(2):
                        for half in range(2):
                            ins = dve.tensor_copy(MK[0:64, 4 * i + half:4 * i + 4:2, :],
                                                  ps[bank_of(ch, i)][64 * half:64 * half + 64])
                        ins.then_inc(S["k_nope"], 1)
                elif name.startswith("pp"):
                    l, i2 = int(name[2]), int(name[-1])
                    dve.wait_ge(S["gates"], 2 * l + 1)
                    for i in range(2):
                        p = 2 * i2 + i
                        dve.tensor_tensor(h[:, 2 * p:2 * p + 2, :], ps[bank_of(ch, i)][:], za[:, 2 * p:2 * p + 2, :],
                                          ALU.mult).then_inc(S["gated_a"], 1)
                elif name.startswith("pa"):
                    l, i2 = int(name[2]), int(name[-1])
                    dve.wait_ge(S["gates"], 2 * l + 2)
                    dve.wait_ge(S["gated_a"], 4 * l + 4)
                    for i in range(2):
                        p = 2 * i2 + i
                        hp_ = h[:, 2 * p:2 * p + 2, :]
                        zp = zb[:, 2 * p:2 * p + 2, :]
                        link(dve.tensor_tensor(zp, ps[bank_of(ch, i)][:], zp, ALU.mult))
                        dve.tensor_tensor(hp_, hp_, zp, ALU.add).then_inc(S["merged"], 1)
                    for i in range(2):
                        operand_low(f"merged{l}", 2 * i2 + i)
                elif name.startswith("wo"):
                    l = int(name[2])
                    add_to_x(b, int(name[-1]), mod[:, l, 16:24])
                elif name.startswith("fb") and ch["last"]:
                    l = int(name[2])
                    add_to_x(b, int(name.split("_")[1]), mod[:, l, 40:48])
                if n not in BEFORE_NORM.values():
                    low_upto(n + SPLIT)

            def norm(i):
                if i < 4:
                    g = col("norm_mix" if i % 2 == 0 else "norm_ffn", 8 * (i // 2), 8)
                    shift = None
                elif i < 8:
                    l, which = (i - 4) // 2, i % 2
                    g = gmod[:, l, which, :]
                    shift = mod[:, l, 24 * which:24 * which + 8]
                else:
                    g, shift = col("final_g"), None
                fill = {0: "n0", 1: "n1", 2: "n2", 3: "n3", 4: "n4", 5: "n5", 6: "n6", 7: "n7"}.get(i)
                if i == 0:
                    dve.wait_ge(S["params_in"], 16)
                dve.wait_ge(S["rstd_ready"], i + 1)
                for p in range(4):
                    for k in (2 * p, 2 * p + 1):
                        ins = dve.scalar_tensor_tensor(out=h[:, k, :], in0=x[:, k, :], scalar=g[:, k:k + 1], in1=rn[:],
                                                       op0=ALU.mult, op1=ALU.mult)
                    if shift is not None:
                        link(ins)
                        for k in (2 * p, 2 * p + 1):
                            ins = dve.tensor_scalar(h[:, k, :], h[:, k, :], shift[:, k:k + 1], None, ALU.add)
                    ins.then_inc(S["normed"], 1)
                    if p and fill:
                        operand_low(fill, p - 1)
                if fill:
                    operand_low(fill, 3)
                low_upto(SPLIT - 1 if i == 0 else BEFORE_NORM[i] + SPLIT)

            def late(_):
                dve.wait_ge(S["late_in"], 32)

            def trig(_):
                magic = 12582912.0
                dve.wait_ge(S["pos_in"], 16)
                dve.wait_ge(S["consts_in"], 16)
                link(dve.tensor_copy(ang[:], posi[:]))
                link(dve.tensor_scalar(ang[:], ang[:], col("inv_freq"), None, ALU.mult))
                link(dve.tensor_scalar(turn[:], ang[:], 1.0 / (2 * np.pi), None, ALU.mult))
                link(dve.tensor_scalar(turn[:], turn[:], magic, None, ALU.add))
                link(dve.tensor_scalar(turn[:], turn[:], -magic, None, ALU.add))
                for part in TWO_PI_PARTS:
                    link(dve.scalar_tensor_tensor(out=ang[:], in0=turn[:], scalar=-part, in1=ang[:], op0=ALU.mult,
                                                  op1=ALU.add))
                lim = 3.1415925
                link(dve.tensor_scalar(turn[:], ang[:], float(np.pi / 2), None, ALU.add))
                link(dve.tensor_scalar(rn[:], turn[:], float(np.pi), -2 * float(np.pi), ALU.is_gt, ALU.mult))
                link(dve.tensor_tensor(turn[:], turn[:], rn[:], ALU.add))
                link(dve.tensor_scalar(turn[:], turn[:], lim, -lim, ALU.min, ALU.max))
                dve.tensor_scalar(ang[:], ang[:], lim, -lim, ALU.min, ALU.max).then_inc(S["trig_angle"], 1)

            def lam(_):
                dve.wait_ge(S["params_in"], 16)
                v = col("lam").rearrange("p (a b) -> p a b", a=4)
                lt = lamt[:, 0:128].rearrange("p (a b) -> p a b", a=2)
                link(dve.tensor_tensor(lt, v[:, 0::2, :], v[:, 1::2, :], ALU.mult))
                dve.reduce_sum(small[:, 2:4], lt, AX.X).then_inc(S["lam_sums"], 1)
                dve.wait_ge(S["lam_exp"], 1)
                link(dve.tensor_tensor(small[:, 6:7], small[:, 5:6], small[:, 4:5], ALU.subtract))
                link(dve.tensor_scalar(gain8, col("diff_gain"), 1.0 - LAMBDA_INIT, None, ALU.mult))
                link(dve.tensor_scalar(neglam, small[:, 6:7], -LAMBDA_INIT, None, ALU.add))

            def la_(_):
                dve.wait_ge(S["la_log"], 1)
                link(dve.scalar_tensor_tensor(out=la[:], in0=la[:], scalar=0.0, in1=ebl[:], op0=ALU.min,
                                              op1=ALU.subtract))
                for b in range(2):
                    for cc in range(4):
                        ck = slice(64 * cc, 64 * cc + 64)
                        ins = dve.tensor_tensor_scan(out=bc[:, b, ck], data0=col("ones", 0, 64), data1=la[:, b, ck],
                                                     initial=0.0, op0=ALU.mult, op1=ALU.add)
                link(ins)
                b4 = bc[:].rearrange("p b (c t) -> p (b c) t", c=4)
                dve.tensor_tensor(ebl[:].rearrange("p b (c t) -> p (b c) t", c=4), b4[:, :, 63:64].to_broadcast([P, 8, 64]),
                                  b4, ALU.subtract).then_inc(S["la_diff"], 1)

            def la_exps(_):
                dve.wait_ge(S["gate_exps"], 3)
                for half in range(2):
                    e4 = eb[64 * half:64 * half + 64].rearrange("p b (c t) -> p b c t", c=4)
                    ins = dve.tensor_copy(dec[:, half::2, :], e4[:, :, :, 63])
                link(ins)

            def unit(u):
                dve.wait_ge(S["unit_rstd"], u + 1)
                if u < 4:
                    hp, k = u // 2, u % 2
                    for half in range(2):
                        r = slice(64 * half, 64 * half + 64)
                        ins = dve.scalar_tensor_tensor(out=(Qd, Kd)[k][:, half, 2 * hp:2 * hp + 2, :],
                                                       in0=ps[bank_of(BY[("bq0", "bk0", "bq1", "bk1")[u]])][r],
                                                       scalar=col(("dq_gain", "dk_gain")[k])[r], in1=rb[u % 2][r],
                                                       op0=ALU.mult, op1=ALU.mult)
                    ins.then_inc(S["unit_normed"], 1)
                elif u < 8:
                    p = {5: 0, 6: 1, 4: 2, 7: 3}[u]
                    dve.scalar_tensor_tensor(out=h[:, 2 * p:2 * p + 2, :], in0=ps[OB][:],
                                             scalar=col("gla_gain") if p < 2 else gain8, in1=rb[u % 2][:],
                                             op0=ALU.mult, op1=ALU.mult).then_inc(S["unit_normed"], 1)
                else:
                    hp, g, k = (u - 8) // 6, (u - 8) % 6 // 2, u % 2
                    dve.scalar_tensor_tensor(out=(dq, dk)[k][hp][g][:], in0=ps[bank_of(BY[f"od{hp}{g}{k}"])][:],
                                             scalar=col(("od_q_gain", "od_k_gain")[k]), in1=rb[u % 2][:],
                                             op0=ALU.mult, op1=ALU.mult).then_inc(S["unit_normed"], 1)

            def gla_att(_):
                dve.wait_ge(S["att_zero"], 1)
                for i in range(2):
                    dve.wait_ge(S["att_done"], i + 1)
                    mask = col("gla_mask").bitcast(U32).rearrange("p (a b) -> p a b", a=1).to_broadcast([P, 4, P])
                    dve.copy_predicated(out=att[:, 2 * i:2 * i + 2].rearrange("p a t b -> p (a t) b"), mask=mask,
                                        data=ps[(SB0, SB1)[i]][:].rearrange("p a (t b) -> p (a t) b", t=2))\
                        .then_inc(S["att_masked"], 1)

            def gla_kv(_):
                for cc in range(3):
                    dve.wait_ge(S["kv_done"], cc + 1)
                    kv = ps[TB][0:64].rearrange("p a (t b) -> p (a t) b", t=2)
                    if cc == 0:
                        dve.tensor_copy(st[0][:], kv).then_inc(S["state_ready"], 1)
                    else:
                        dve.wait_ge(S["state_ready"], cc)
                        link(dve.tensor_tensor(st[cc][:], st[cc - 1][:], dec[:, :, cc:cc + 1].to_broadcast([64, 4, P]),
                                               ALU.mult))
                        dve.tensor_tensor(st[cc][:], kv, st[cc][:], ALU.add).then_inc(S["state_ready"], 1)

            def ag_silu(_):
                dve.wait_ge(S["unit_normed"], GLA_U[1] + 1)
                dve.wait_ge(S["silu_ag"], 3)
                for p in range(2):
                    hp_ = h[:, 2 * p:2 * p + 2, :]
                    dve.tensor_tensor(hp_, hp_, sg[:, 2 * p:2 * p + 2, :], ALU.mult).then_inc(S["mix_ready"], 1)
                for p in range(2):
                    operand_low("mix0", p)

            def diff_r(i):
                unit(DIFF_U[i])
                if i == 1:
                    for p in (2, 3):
                        operand_low("mix0", p)

            def diff_s(u):
                qt = u % 2
                nk = P * (qt + 1)
                S_ = Sb[u % 2][:, :, 0:nk]
                m = col("causal")[:, TOK - nk:TOK].rearrange("p (a b) -> p a b", a=1).to_broadcast([P, 2, nk])
                dve.wait_ge(S["diff_scores"], u + 1)
                link(dve.tensor_tensor(S_, ps[(SB0, SB1)[u % 2]][:, :, 0:nk], m, ALU.add))
                link(dve.reduce_max(stat[:, u % 2, 0:2], S_, AX.X))
                dve.tensor_scalar(stat[:, u % 2, 2:4], stat[:, u % 2, 0:2], -0.125, None, ALU.mult)\
                    .then_inc(S["diff_max"], 1)

            def diff_w(u):
                nk = P * (u % 2 + 1)
                s_ = stat[:, u % 2]
                dve.wait_ge(S["diff_exp"], u + 1)
                link(dve.reciprocal(s_[:, 6:8], s_[:, 4:6]))
                link(dve.tensor_scalar(s_[:, 8:9], s_[:, 7:8], neglam, None, ALU.mult))
                if u >= 2:
                    dve.wait_ge(S["diff_turned"], u - 1)
                link(dve.tensor_scalar(W[u % 2][:, 0:nk], Sb[u % 2][:, 0, 0:nk], s_[:, 6:7], None, ALU.mult))
                dve.scalar_tensor_tensor(out=W[u % 2][:, 0:nk], in0=Sb[u % 2][:, 1, 0:nk], scalar=s_[:, 8:9],
                                         in1=W[u % 2][:, 0:nk], op0=ALU.mult, op1=ALU.add).then_inc(S["diff_w"], 1)

            def dil_s(u):
                qt = u % 2
                nk = P * (qt + 1)
                m = col(f"dil{qt}").rearrange("p (g k) -> p g k", g=3)
                S_ = DS[u % 2][:, 0:3 * nk].rearrange("p (g k) -> p g k", g=3)
                dve.wait_ge(S["dil_scores"], u + 1)
                if u >= 2:
                    dve.wait_ge(S["dil_turned"], 3 * (u // 2) - 2 if qt == 0 else 3 * (u // 2))
                dve.tensor_tensor(S_[:, 0:2, :], ps[SB0][:, :, 0:nk], m[:, 0:2, :], ALU.add)
                link(dve.tensor_tensor(S_[:, 2, :], ps[SB1][:, 0, 0:nk], m[:, 2, :], ALU.add))
                link(dve.reduce_max(dstat[:, u % 2, 0:1], DS[u % 2][:, 0:3 * nk], AX.X))
                dve.tensor_scalar(dstat[:, u % 2, 1:2], dstat[:, u % 2, 0:1], -(128 ** -0.5), None, ALU.mult)\
                    .then_inc(S["dil_max"], 1)

            def dil_w(u):
                nk = P * (u % 2 + 1)
                dve.wait_ge(S["dil_exp"], u + 1)
                link(dve.reciprocal(dstat[:, u % 2, 3:4], dstat[:, u % 2, 2:3]))
                dve.tensor_scalar(DS[u % 2][:, 0:3 * nk], DS[u % 2][:, 0:3 * nk], dstat[:, u % 2, 3:4], None, ALU.mult)\
                    .then_inc(S["dil_w"], 1)

            def mix1(hp):
                operand_low("mix1", hp)

            def mod_(l):
                dve.wait_ge(S["ada_sum"], 6 * (l + 1))
                dve.tensor_tensor(mod[:, l, :], ps[OB][:, 0, 0:48], col("b_ada", 48 * l, 48), ALU.add)\
                    .then_inc(S["mod_ready"], 1)
                dve.wait_ge(S["mod_ready"], l + 1)
                for which in range(2):
                    link(dve.scalar_tensor_tensor(out=gmod[:, l, which, :],
                                                  in0=mod[:, l, 24 * which + 8:24 * which + 16], scalar=1.0,
                                                  in1=col(("ln1", "ln2")[which], 8 * l, 8), op0=ALU.add,
                                                  op1=ALU.mult))

            def krot(l):
                dve.wait_ge(S["krot_done"], l + 1)
                dve.wait_ge(S["trig_done"], 1)
                link(dve.tensor_tensor(krs[:], ps[TB][0:32, 0, :], sinT[0:32], ALU.mult))
                link(dve.tensor_tensor(kr[:], kr[:], cosT[0:32], ALU.mult))
                dve.tensor_tensor(kr[:], kr[:], krs[:], ALU.add).then_inc(S["krope_done"], 1)

            def wide(a):
                l, which = a
                i = 2 * l + which
                dve.wait_ge(S["wide_rstd"], i + 1)
                if which == 0:
                    for k in range(3):
                        o = ps[bank_of(BY[f"cq{l}a"])][:, k, :] if k < 2 else ps[bank_of(BY[f"cq{l}b"])][:, 0, :]
                        ins = dve.scalar_tensor_tensor(out=h[:, k, :], in0=o, scalar=col("q_norm", 3 * l + k, 1),
                                                       in1=rn[:], op0=ALU.mult, op1=ALU.mult)
                    ins.then_inc(S["wide_normed"], 1)
                    dve.wait_ge(S["cq_high"], l + 1)
                    dve.tensor_tensor(SQL[:, 0:3, :], h[:, 0:3, :], SQH[:, 0:3, :], ALU.subtract)\
                        .then_inc(S["cq_low"], 1)
                else:
                    for k in range(2):
                        ins = dve.scalar_tensor_tensor(out=h[:, 3 + k, :], in0=ps[bank_of(BY[f"ckv{l}"])][:, k, :],
                                                       scalar=col("kv_norm", 2 * l + k, 1), in1=rn[:],
                                                       op0=ALU.mult, op1=ALU.mult)
                    ins.then_inc(S["wide_normed"], 1)
                    dve.wait_ge(S["ckv_high"], l + 1)
                    dve.tensor_tensor(SCL[:, 0:2, :], h[:, 3:5, :], SCH[:, 0:2, :], ALU.subtract)\
                        .then_inc(S["ckv_low"], 1)

            def qrot(l):
                dve.wait_ge(S["qrot_done"], l + 1)
                bc2 = lambda t: t[:].rearrange("p (a b) -> p a b", a=1).to_broadcast([P, 2, TOK])
                dve.tensor_tensor(qs[:], ps[TB][:], bc2(sinT), ALU.mult).then_inc(S["q_rope"], 1)
                link(dve.tensor_tensor(qr[:], qr[:], bc2(cosT), ALU.mult))
                dve.wait_ge(S["q_rope"], 2 * l + 1)
                for i in range(4):
                    r = slice(32 * i, 32 * i + 32)
                    ins = dve.tensor_tensor(MQ[64:96, i::4, :], qr[r], qs[r], ALU.add)
                ins.then_inc(S["q_rope"], 1)

            def pool_split(l):
                dve.wait_ge(S["pooled_high"], 2 * l + 1)
                dve.tensor_tensor(SQL[:, 0::2, :], p1[:, 0::2, PAD:], SQH[:, 0::2, :], ALU.subtract)\
                    .then_inc(S["pooled_low"], 1)
                dve.wait_ge(S["pooled_high"], 2 * l + 2)
                dve.tensor_tensor(SQL[:, 1::2, :], p2[:, 1::2, PAD:], SQH[:, 1::2, :], ALU.subtract)\
                    .then_inc(S["pooled_low"], 1)

            def y_(l):
                for i in range(2):
                    dve.wait_ge(S["y_high"], 2 * l + i + 1)
                    dve.tensor_tensor(SQL[:, 2 * i:2 * i + 2, :], p1[:, 2 * i:2 * i + 2, PAD:],
                                      SQH[:, 2 * i:2 * i + 2, :], ALU.subtract).then_inc(S["y_low"], 1)

            def mla_s(a):
                l, u = a
                U, nk = 16 * l + u, P * (u % 2 + 1)
                S_ = MS[u % 2][:, 0:nk]
                dve.wait_ge(S["mla_scores"], U + 1)
                if U >= 2:
                    dve.wait_ge(S["mla_turned"], U - 1)
                link(dve.tensor_tensor(S_, ps[(SB0, SB1)[u % 2]][:, 0, 0:nk], col("causal")[:, TOK - nk:TOK], ALU.add))
                link(dve.reduce_max(mstat[:, u % 2, 0:1], S_, AX.X))
                dve.tensor_scalar(mstat[:, u % 2, 1:2], mstat[:, u % 2, 0:1], -(96 ** -0.5), None, ALU.mult)\
                    .then_inc(S["mla_max"], 1)

            def mla_w(a):
                l, u = a
                U, nk = 16 * l + u, P * (u % 2 + 1)
                S_ = MS[u % 2][:, 0:nk]
                dve.wait_ge(S["mla_exp"], U + 1)
                link(dve.reciprocal(mstat[:, u % 2, 3:4], mstat[:, u % 2, 2:3]))
                dve.tensor_scalar(S_, S_, mstat[:, u % 2, 3:4], None, ALU.mult).then_inc(S["mla_w"], 1)

            def mla_p(a):
                l, u = a
                if u % 8 == 7:
                    i = u // 8
                    dve.wait_ge(S["att_high"], 2 * l + i + 1)
                    dve.tensor_tensor(SCL[:, 2 * i:2 * i + 2, :], ps[OB][:], SCH[:, 2 * i:2 * i + 2, :], ALU.subtract)\
                        .then_inc(S["att_low"], 1)

            stages = dict(chunk=chunk, norm=norm, late=late, unit=unit, trig=trig, lam=lam, la=la_, la_exps=la_exps, gla_att=gla_att,
                          gla_kv=gla_kv, ag_silu=ag_silu, diff_s=diff_s, diff_w=diff_w, diff_r=diff_r, dil_s=dil_s,
                          dil_w=dil_w, mix1=mix1, mod=mod_, krot=krot, wide=wide, qrot=qrot, pool_split=pool_split, y=y_,
                          mla_s=mla_s, mla_w=mla_w, mla_p=mla_p, gla_r=lambda hp: unit(GLA_U[hp]))
            for stage, i in order:
                if stage in stages:
                    stages[stage](i)

        @block.gpsimd
        def _(pool):
            chain = [0]

            def link(ins):
                chain[0] += 1
                ins.then_inc(S["pool_chain"], 1)
                pool.wait_ge(S["pool_chain"], chain[0])

            def ada_(a):
                seg, part = a // 4, a % 4
                acc, w = adas[seg % 2], adaw[a % 2]
                pool.wait_ge(S["ada_scaled"], a + 1)
                if part == 0:
                    if seg >= 2:
                        pool.wait_ge(S["ada_sum"], seg - 1)
                    pool.tensor_tensor(acc[:], w[:, 0, :], w[:, 1, :], ALU.add).then_inc(S["ada_added"], 1)
                    return
                pool.wait_ge(S["ada_added"], a)
                link(pool.tensor_tensor(acc[:], w[:, 0, :], acc[:], ALU.add))
                pool.tensor_tensor(acc[:], w[:, 1, :], acc[:], ALU.add).then_inc(S["ada_added"], 1)

            def silu(a):
                l, j = a
                pool.wait_ge(S["silu_done"], 11 * l + j + 1)
                pool.wait_ge(S["conv_done"], 22 * l + 2 * j + 2)
                pool.tensor_tensor(cg[j % 2][:], cg[j % 2][:], cv[j % 2][:], ALU.mult).then_inc(S["act_mul"], 1)

            def act_(a):
                l, j = a
                pool.wait_ge(S["act_high"], 11 * l + j + 1)
                pool.tensor_tensor(AL[:, 2 * j:2 * j + 2, :], cg[j % 2][:], AH[:, 2 * j:2 * j + 2, :], ALU.subtract)\
                    .then_inc(S["act_low"], 1)

            def act2(a):
                l, p = a
                r = rl[p % RELU][:]
                pool.wait_ge(S["relu_done"], 16 * l + p + 1)
                pool.tensor_tensor(r, r, r, ALU.mult).then_inc(S["sq_done"], 1)
                pool.wait_ge(S["act2_high"], 16 * l + p + 1)
                pool.tensor_tensor(BL[:, 2 * p:2 * p + 2, :], r, BH[:, 2 * p:2 * p + 2, :], ALU.subtract)\
                    .then_inc(S["act2_low"], 1)

            def zero_pads(l):
                pool.wait_ge(S["products_done"], BY[f"cq{l}a"]["n"] + 1)
                pool.memset(up[:, :, 0:PAD], 0.0)
                pool.memset(p1[:, :, 0:PAD], 0.0)
                link(pool.memset(p2[:, :, 0:PAD], 0.0))

            def krot(l):
                pool.wait_ge(S["krope_done"], l + 1)
                zero_pads(l)
                src = kr[:].rearrange("p (a b) -> p a b", a=1).to_broadcast([32, 8, TOK])
                pool.tensor_copy(MK[64:96], src).then_inc(S["kfull"], 1)

            def pool_(l):
                pool.wait_ge(S["late_in"], 32)
                pool.wait_ge(S["kfull"], l + 1)
                pool.wait_ge(S["u_ready"], 2 * l + 2)
                for i, (a, b) in enumerate(((up, p1), (p1, p2), (p2, p1), (p1, p2))):
                    s_ = 1 << i
                    link(pool.tensor_tensor(b[:, i:, PAD:], a[:, i:, PAD:], a[:, i:, PAD - s_:PAD + TOK - s_], ALU.add))
                for j, buf in enumerate((p1, p2)):
                    for g in (j, j + 2):
                        w = 2 << g
                        link(pool.tensor_tensor(buf[:, g, PAD:PAD + 16], buf[:, g, PAD:PAD + 16],
                                                col("cnt", 16 * g, 16), ALU.mult))
                        link(pool.tensor_scalar(buf[:, g, PAD + 16:], buf[:, g, PAD + 16:], 1.0 / w, None, ALU.mult))
                    pool.tensor_tensor(buf[:, j::2, PAD:], buf[:, j::2, PAD:], up[:, j::2, PAD:], ALU.subtract)\
                        .then_inc(S["pooled"], 1)

            pool.memset(att[:], 0.0).then_inc(S["att_zero"], 1)
            stages = dict(ada=ada_, silu=silu, act=act_, krot=krot, pool=pool_, act2=act2)
            for stage, i in order:
                if stage in stages:
                    stages[stage](i)


LAMBDA_INIT = 0.2


def shape_constants():
    q, k = np.arange(P)[:, None], np.arange(TOK)[None, :]
    one = np.float32(1.0)
    c = {"ident": np.eye(P), "ones": np.ones((P, P)), "ones64": np.kron(np.eye(2), np.ones((64, 64)))}
    c["causal"] = np.where(k <= q + P, 0.0, NEG)
    for qt in range(2):
        nk = P * (qt + 1)
        t, j = q + P * qt, np.arange(nk)[None, :]
        m = [(t - j >= 0) & ((t - j) % d == 0) & (t - j <= w) for w, d in ((128, 1), (512, 4), (2048, 16))]
        c[f"dil{qt}"] = np.concatenate([np.where(v, 0.0, NEG) for v in m], 1)
    j, i = np.arange(P)[:, None], np.arange(P)[None, :]
    c["gla_mask"] = np.where((j // 64 == i // 64) & (j <= i), 1.0, 0.0)
    rot = np.zeros((P, P))
    for m in range(P):
        rot[m + 16 if m % 32 < 16 else m - 16, m] = -1.0 if m % 32 < 16 else 1.0
    c["rot"] = rot
    f = np.float32(10000.0) ** (-np.arange(0, 32, 2, dtype=np.float32) / np.float32(32))
    c["inv_freq"] = np.tile(f, 8)[:, None]
    c["cnt"] = np.tile(np.concatenate([1.0 / np.minimum(np.arange(16) + 1, 2 << g) for g in range(4)])[None], (P, 1))
    c["eps"] = np.full((P, 1), EPS)
    where, sizes = columns()
    a = np.zeros((P, sizes["consts"]), np.float32)
    for name, v in c.items():
        _, at, n = where[name]
        a[:, at:at + n] = v
    return a


def by_feature(v):
    v = np.asarray(v)
    return v.reshape(-1, P).T


def lay_params(i):
    where, sizes = columns()
    a = np.zeros((P, sizes["params"]), np.float32)

    def put(name, v, at=0):
        _, c0, n = where[name]
        a[:v.shape[0], c0 + at:c0 + at + v.shape[1]] = v

    for name, src in (("norm_mix", "norm_mix"), ("norm_ffn", "norm_ffn"), ("b_a", "ev_b_a"),
                      ("gla_gain", "ev_gla_gain"), ("diff_gain", "ev_diff_gain"), ("od_q_gain", "od_q_gain"),
                      ("od_k_gain", "od_k_gain"), ("ln1", "ln1_g_2"), ("ln2", "ln2_g_2"), ("b_ada", "b_ada_2"),
                      ("q_norm", "q_norm_g_2"), ("kv_norm", "kv_norm_g_2"), ("pool_scale", "pool_scale_2"),
                      ("final_g", "final_g_2"), ("c", "c_2")):
        put(name, by_feature(i[src]))
    for name, src in (("dq_gain", "ev_dq_gain"), ("dk_gain", "ev_dk_gain")):
        g = np.asarray(i[src]).reshape(64, 1)
        put(name, np.concatenate([g, g], 0))
    cw, cb = np.asarray(i["ffn_conv_w"]), np.asarray(i["ffn_conv_b"])
    taps = np.stack([cw[:, 0, 0], cw[:, 1, 0], cw[:, 2, 0], cb], 1)
    put("conv", taps.reshape(2, 4, 44, P).transpose(3, 0, 2, 1).reshape(P, -1))
    lam = np.concatenate([np.asarray(i[k]).reshape(-1) for k in ("ev_lq1", "ev_lk1", "ev_lq2", "ev_lk2")])
    put("lam", np.repeat(lam[None], P, 0))
    put("w_a2", np.asarray(i["ev_w_a2"])[0])
    put("w_ar", np.asarray(i["ev_w_in"])[0, :, 1536:1552].reshape(KB, P, 16).transpose(1, 0, 2).reshape(P, -1))
    for l in range(2):
        put("w_kr", np.asarray(i["w_in_2"])[l, :, 1152:1184].reshape(KB, P, 32).transpose(1, 0, 2).reshape(P, -1),
            256 * l)
    return a


def lay_stream(i):
    chunks, total = linear_chunks()
    out = np.zeros(P * total, np.float32)
    for ch in chunks:
        name, l = ch["src"]
        w = np.asarray(i[name])[l]
        if ch["diag"]:
            part = w.transpose(1, 0, 2).reshape(P, -1)
        else:
            w = w.reshape(w.shape[0], -1)[ch["rows"][0] * P:(ch["rows"][-1] + 1) * P][:, ch["cols"]]
            part = w.reshape(len(ch["rows"]), P, -1).transpose(1, 0, 2).reshape(P, -1)
        out[P * ch["at"]:P * (ch["at"] + ch["width"])] = part.reshape(-1)
    return out


def kernel(**inputs):
    import concourse.bacc as bacc
    from concourse.bass_utils import run_bass_kernel_spmd

    i = inputs
    _, total = linear_chunks()
    xT = np.ascontiguousarray(np.asarray(i["x"])[0].T.reshape(KB, P, TOK).transpose(1, 0, 2))
    wa = np.asarray(i["w_ada_2"]).reshape(2, 4, 2, P, 6, D)
    arrays = {
        "xT": xT, "stream": lay_stream(i), "ada": np.ascontiguousarray(wa.transpose(0, 4, 1, 3, 2, 5)).reshape(-1),
        "consts_d": shape_constants(), "params_d": lay_params(i),
        "positions": np.ascontiguousarray(np.asarray(i["positions_2"]).astype(np.int32)),
    }
    nc = bacc.Bacc("TRN2", target_bir_lowering=False, num_devices=1)
    args = {n: nc.dram_tensor(n, a.shape, mybir.dt.from_np(a.dtype), kind="ExternalInput").ap()
            for n, a in arrays.items()}
    out = nc.dram_tensor("out", (P, KB, TOK), F32, kind="ExternalOutput").ap()
    build(nc, out=out, **args)
    r = run_bass_kernel_spmd(nc, [arrays], core_ids=[0])
    y = r.results[0]["out"]
    return np.ascontiguousarray(y.transpose(1, 0, 2).reshape(D, TOK).T)[None]
```
